# Optimizing a Trainium2 kernel written in Bass

```python
import math
import jax, jax.numpy as jnp
from jax import lax
import numpy as np

"""Hybrid bidirectional encoder trunk, two layers, applied to two request batches with shared weights.
Inputs: x_prompt (BATCH, SEQ, D_MODEL), x_sample (DEC_BATCH, DEC_SEQ, D_MODEL), then the weights.
Outputs: (y_prompt (BATCH, SEQ, D_MODEL), y_sample (DEC_BATCH, DEC_SEQ, D_MODEL)).
Even layers: parallel [bidirectional gated DeltaNet | bidirectional order-2 Hyena] behind one input and one output projection.
Odd layers: banded windowed grouped-query attention with per-head sink logits and ALiBi.
Every layer: RMSNorm -> hierarchical MoE (top-1 group, top-2 experts within group).
"""

D_MODEL = 1024
BATCH = 1
SEQ = 256
DEPTH = 2
DEC_BATCH = 1
DEC_SEQ = 256
PAST_LEN = 128

N_EVEN = (DEPTH + 1) // 2
N_ODD = DEPTH // 2
EPS = 1e-6

A_HEADS = 4
A_DK = 128
A_DV = 128
A_WIDTH = A_HEADS * A_DV
A_QKV = 2 * A_HEADS * A_DK + A_HEADS * A_DV
CHUNK = 64
SHORT_CONV = 3

B_WIDTH = D_MODEL - A_WIDTH
HY_ORDER = 2
HY_EMB = 33
HY_BANDS = (HY_EMB - 1) // 2
HY_FFN = 64
HY_TARGET = 1e-2
HY_FAST_PCT = 0.3
HY_SLOW_PCT = 1.5
HY_MIN_DECAY = math.log(HY_TARGET) / HY_SLOW_PCT
HY_MAX_DECAY = math.log(HY_TARGET) / HY_FAST_PCT

EVEN_IN = A_QKV + A_WIDTH + 4 * A_HEADS + 3 * B_WIDTH

C_HEADS = 16
C_KV_HEADS = 4
C_HEAD_DIM = 64
C_GROUP = C_HEADS // C_KV_HEADS
WINDOW = 128
C_BLOCK = 128
ODD_IN = (C_HEADS + 2 * C_KV_HEADS) * C_HEAD_DIM

N_GROUPS = 4
EXPERTS_PER_GROUP = 8
TOP_K_INNER = 2
D_EXPERT = 256

kernel_name = "hybrid_bidir_deltanet_hyena_swa_hmoe"

f32 = jnp.float32

def rmsnorm(x, g):
    xf = x.astype(f32)
    y = xf * lax.rsqrt(jnp.mean(xf * xf, axis=-1, keepdims=True) + EPS)
    return (y * g.astype(f32)).astype(x.dtype)

def l2norm(x):
    return x * lax.rsqrt(jnp.sum(x * x, axis=-1, keepdims=True) + EPS)

def centred_dwconv(x, w):
    L = x.shape[1]
    pad = (SHORT_CONV - 1) // 2
    xp = jnp.pad(x, ((0, 0), (pad, pad), (0, 0)))
    return sum(xp[:, j:j + L] * w[:, j] for j in range(SHORT_CONV))

def chunk_gated_delta(q, k, v, g, beta):
    B, H, L, DK = q.shape
    DV = v.shape[-1]
    N = L // CHUNK
    q = q * (DK ** -0.5)
    q = q.reshape(B, H, N, CHUNK, DK)
    k = k.reshape(B, H, N, CHUNK, DK)
    v = v.reshape(B, H, N, CHUNK, DV)
    beta = beta.reshape(B, H, N, CHUNK)
    gc = jnp.cumsum(g.reshape(B, H, N, CHUNK), axis=-1)
    tril = jnp.tril(jnp.ones((CHUNK, CHUNK), dtype=bool))
    strict = jnp.tril(jnp.ones((CHUNK, CHUNK), dtype=bool), -1)
    diff = gc[..., :, None] - gc[..., None, :]
    decay = jnp.where(tril, jnp.exp(jnp.where(tril, diff, 0.0)), 0.0)
    k_beta = k * beta[..., None]
    v_beta = v * beta[..., None]
    kk = jnp.einsum('bhncd,bhnsd->bhncs', k_beta, k) * decay
    a_mat = jnp.eye(CHUNK, dtype=f32) + jnp.where(strict, kk, 0.0)
    u = lax.linalg.triangular_solve(a_mat, v_beta, left_side=True, lower=True, unit_diagonal=True)
    w = lax.linalg.triangular_solve(a_mat, k_beta * jnp.exp(gc)[..., None], left_side=True, lower=True, unit_diagonal=True)
    qk = jnp.einsum('bhncd,bhnsd->bhncs', q, k) * decay
    q_dec = q * jnp.exp(gc)[..., None]
    k_dec = k * jnp.exp(gc[..., -1:] - gc)[..., None]
    g_last = jnp.exp(gc[..., -1])

    def step(S, xs):
        qk_i, qd_i, kd_i, u_i, w_i, gl_i = xs
        v_new = u_i - jnp.einsum('bhcd,bhde->bhce', w_i, S)
        o = jnp.einsum('bhcd,bhde->bhce', qd_i, S) + jnp.einsum('bhcs,bhse->bhce', qk_i, v_new)
        S = S * gl_i[..., None, None] + jnp.einsum('bhcd,bhce->bhde', kd_i, v_new)
        return S, o

    xs = tuple(jnp.moveaxis(t, 2, 0) for t in (qk, q_dec, k_dec, u, w, g_last))
    S0 = jnp.zeros((B, H, DK, DV), f32)
    _, o = lax.scan(step, S0, xs)
    return jnp.moveaxis(o, 0, 2).reshape(B, H, L, DV)

def gated_deltanet_bidir(qkv, z, ab, conv_a, alog_f, alog_b, dtb_f, dtb_b, onorm):
    B, L, _ = qkv.shape
    qkv = jax.nn.silu(centred_dwconv(qkv, conv_a))
    q, k, v = jnp.split(qkv, [A_HEADS * A_DK, 2 * A_HEADS * A_DK], axis=-1)

    def heads(t, d):
        return t.reshape(B, L, A_HEADS, d).transpose(0, 2, 1, 3).astype(f32)

    q = l2norm(heads(q, A_DK))
    k = l2norm(heads(k, A_DK))
    v = heads(v, A_DV)
    b_f, b_b, a_f, a_b = jnp.split(ab.astype(f32), 4, axis=-1)

    def gates(b_raw, a_raw, alog, dtb):
        beta = jax.nn.sigmoid(b_raw)
        g = -jnp.exp(alog.astype(f32)) * jax.nn.softplus(a_raw + dtb.astype(f32))
        return beta.transpose(0, 2, 1), g.transpose(0, 2, 1)

    beta_f, g_f = gates(b_f, a_f, alog_f, dtb_f)
    beta_b, g_b = gates(b_b, a_b, alog_b, dtb_b)
    flip = lambda t: jnp.flip(t, axis=2)
    o = chunk_gated_delta(q, k, v, g_f, beta_f) + flip(
        chunk_gated_delta(flip(q), flip(k), flip(v), flip(g_b), flip(beta_b)))
    o = o.transpose(0, 2, 1, 3)
    o = rmsnorm(o, onorm) * jax.nn.silu(z.reshape(B, L, A_HEADS, A_DV).astype(f32))
    return o.reshape(B, L, A_WIDTH).astype(qkv.dtype)

def hyena_filters(L, w1, b1, w2, b2, w3, b3, w4, freq):
    t = jnp.linspace(0.0, 1.0, L, dtype=f32)[:, None]
    wpos = (2.0 * math.pi / L) * jnp.arange(L, dtype=f32)[:, None]
    bands = jnp.linspace(1e-4, HY_BANDS - 1, HY_BANDS, dtype=f32)[None, :]
    feats = jnp.concatenate([t, jnp.cos(bands * wpos), -jnp.sin(bands * wpos)], axis=-1)
    fr = freq.astype(f32)
    h = jnp.sin(fr[0] * (feats @ w1.astype(f32) + b1.astype(f32)))
    h = jnp.sin(fr[1] * (h @ w2.astype(f32) + b2.astype(f32)))
    h = jnp.sin(fr[2] * (h @ w3.astype(f32) + b3.astype(f32)))
    h = (h @ w4.astype(f32)).reshape(L, HY_ORDER, 2, B_WIDTH)
    deltas = jnp.abs(jnp.linspace(HY_MIN_DECAY, HY_MAX_DECAY, B_WIDTH, dtype=f32))
    window = jnp.exp(-t * deltas[None, :])
    return h * window[:, None, None, :]

def bidir_fftconv(u, h_fwd, h_bwd, d_bias):
    L, C = h_fwd.shape
    kfull = jnp.concatenate([(h_fwd[0] + h_bwd[0])[None], h_fwd[1:], jnp.zeros((1, C), f32), h_bwd[1:][::-1]], axis=0)
    kf = jnp.fft.rfft(kfull, n=2 * L, axis=0)
    uf = jnp.fft.rfft(u, n=2 * L, axis=1)
    y = jnp.fft.irfft(uf * kf[None], n=2 * L, axis=1)[:, :L]
    return y + u * d_bias.astype(f32)

def hyena_bidir(hx, conv_b, w1, b1, w2, b2, w3, b3, w4, freq, dbias):
    L = hx.shape[1]
    hx = centred_dwconv(hx, conv_b).astype(f32)
    x1, x2, v = jnp.split(hx, 3, axis=-1)
    filt = hyena_filters(L, w1, b1, w2, b2, w3, b3, w4, freq)
    zz = v
    for o, gate in enumerate((x1, x2)):
        zz = gate * bidir_fftconv(zz, filt[:, o, 0], filt[:, o, 1], dbias[o])
    return zz

def even_mixer(h, w_in, conv_a, alog_f, alog_b, dtb_f, dtb_b, onorm, conv_b,
               w1, b1, w2, b2, w3, b3, w4, freq, dbias, w_out):
    p = h @ w_in
    qkv, z, ab, hx = jnp.split(p, [A_QKV, A_QKV + A_WIDTH, A_QKV + A_WIDTH + 4 * A_HEADS], axis=-1)
    o_a = gated_deltanet_bidir(qkv, z, ab, conv_a, alog_f, alog_b, dtb_f, dtb_b, onorm)
    o_b = hyena_bidir(hx, conv_b, w1, b1, w2, b2, w3, b3, w4, freq, dbias).astype(h.dtype)
    return jnp.concatenate([o_a, o_b], axis=-1) @ w_out

def windowed_gqa(h, w_qkv, sinks, w_out):
    B, L, _ = h.shape
    nb = L // C_BLOCK
    qkv = h @ w_qkv
    q, k, v = jnp.split(qkv, [C_HEADS * C_HEAD_DIM, (C_HEADS + C_KV_HEADS) * C_HEAD_DIM], axis=-1)
    q = q.reshape(B, nb, C_BLOCK, C_KV_HEADS, C_GROUP, C_HEAD_DIM)

    def band(t):
        t = t.reshape(B, L, C_KV_HEADS, C_HEAD_DIM)
        tp = jnp.pad(t, ((0, 0), (C_BLOCK, C_BLOCK), (0, 0), (0, 0))).reshape(B, nb + 2, C_BLOCK, C_KV_HEADS, C_HEAD_DIM)
        return jnp.concatenate([tp[:, :-2], tp[:, 1:-1], tp[:, 2:]], axis=2)

    kb, vb = band(k), band(v)
    qi = jnp.arange(C_BLOCK)[:, None]
    kj = jnp.arange(3 * C_BLOCK)[None, :]
    rel = C_BLOCK + qi - kj
    in_win = jnp.abs(rel) <= WINDOW
    slopes = (2.0 ** (-8.0 * jnp.arange(1, C_HEADS + 1, dtype=f32) / C_HEADS)).reshape(C_KV_HEADS, C_GROUP)
    alibi = -slopes[:, :, None, None] * jnp.abs(rel).astype(f32)
    sink = jnp.broadcast_to(sinks.astype(f32).reshape(C_KV_HEADS, C_GROUP)[None, :, :, None, None],
                            (B, C_KV_HEADS, C_GROUP, C_BLOCK, 1))
    scale = C_HEAD_DIM ** -0.5

    def block(args):
        qn, kn, vn, n = args
        s = jnp.einsum('bqhgd,bkhd->bhgqk', qn, kn).astype(f32) * scale + alibi
        key_pos = (n - 1) * C_BLOCK + kj
        valid = in_win & (key_pos >= 0) & (key_pos < L)
        s = jnp.where(valid, s, -jnp.inf)
        p = jax.nn.softmax(jnp.concatenate([s, sink], axis=-1), axis=-1)[..., :-1]
        return jnp.einsum('bhgqk,bkhd->bqhgd', p.astype(vn.dtype), vn)

    o = lax.map(block, (jnp.moveaxis(q, 1, 0), jnp.moveaxis(kb, 1, 0), jnp.moveaxis(vb, 1, 0), jnp.arange(nb)))
    o = jnp.moveaxis(o, 0, 1).reshape(B, L, C_HEADS * C_HEAD_DIM)
    return o @ w_out

def hier_moe(h, w_group, w_expert, w_gate, w_up, w_down):
    B, L, Dm = h.shape
    t = h.reshape(B * L, Dm)
    T = t.shape[0]
    g_logit = (t @ w_group).astype(f32)
    g_prob = jax.nn.softmax(g_logit, axis=-1)
    _, g_sel = lax.top_k(g_logit, 1)
    g_sel = g_sel[:, 0]
    p_sel = jnp.take_along_axis(g_prob, g_sel[:, None], axis=-1)[:, 0]
    e_logit = (t @ w_expert).astype(f32).reshape(T, N_GROUPS, EXPERTS_PER_GROUP)
    e_sel = jnp.take_along_axis(e_logit, g_sel[:, None, None], axis=1)[:, 0]
    top_v, top_i = lax.top_k(e_sel, TOP_K_INNER)
    top_w = jax.nn.softmax(top_v, axis=-1)
    inner = jnp.sum(top_w[..., None] * jax.nn.one_hot(top_i, EXPERTS_PER_GROUP, dtype=f32), axis=1)
    comb = (p_sel[:, None, None] * jax.nn.one_hot(g_sel, N_GROUPS, dtype=f32)[:, :, None] * inner[:, None, :]).astype(t.dtype)
    out = jnp.zeros_like(t)
    for g in range(N_GROUPS):
        hg = jax.nn.silu(jnp.einsum('td,edf->tef', t, w_gate[g])) * jnp.einsum('td,edf->tef', t, w_up[g])
        out = out + jnp.einsum('tef,efd->td', hg * comb[:, g, :, None], w_down[g])
    return out.reshape(B, L, Dm)

def trunk(x, norm_mix, norm_ffn, norm_final,
          ev_w_in, ev_conv_a, ev_alog_f, ev_alog_b, ev_dtb_f, ev_dtb_b, ev_onorm, ev_conv_b,
          hy_w1, hy_b1, hy_w2, hy_b2, hy_w3, hy_b3, hy_w4, hy_freq, hy_dbias, ev_w_out,
          od_w_qkv, od_sinks, od_w_out,
          moe_w_group, moe_w_expert, moe_w_gate, moe_w_up, moe_w_down):
    for layer in range(DEPTH):
        i = layer // 2
        h = rmsnorm(x, norm_mix[layer])
        if layer % 2 == 0:
            x = x + even_mixer(h, ev_w_in[i], ev_conv_a[i], ev_alog_f[i], ev_alog_b[i], ev_dtb_f[i], ev_dtb_b[i],
                               ev_onorm[i], ev_conv_b[i], hy_w1[i], hy_b1[i], hy_w2[i], hy_b2[i], hy_w3[i], hy_b3[i],
                               hy_w4[i], hy_freq[i], hy_dbias[i], ev_w_out[i])
        else:
            x = x + windowed_gqa(h, od_w_qkv[i], od_sinks[i], od_w_out[i])
        h = rmsnorm(x, norm_ffn[layer])
        x = x + hier_moe(h, moe_w_group[layer], moe_w_expert[layer], moe_w_gate[layer], moe_w_up[layer], moe_w_down[layer])
    return rmsnorm(x, norm_final)

def setup_inputs(seed: int = 0) -> dict:
    key = jax.random.key(seed)
    ks = iter(jax.random.split(key, 40))

    def nrm(shape, scale):
        return jax.random.normal(next(ks), shape, f32) * scale

    def gain(shape):
        return 1.0 + 0.02 * jax.random.normal(next(ks), shape, f32)

    def alog(shape):
        return jnp.log(jax.random.uniform(next(ks), shape, f32, minval=1.0, maxval=16.0))

    def dtb(shape):
        u = jax.random.uniform(next(ks), shape, f32)
        dt = jnp.exp(u * (math.log(0.1) - math.log(1e-3)) + math.log(1e-3))
        return dt + jnp.log(-jnp.expm1(-dt))

    D = D_MODEL
    return {
        "x_prompt": nrm((BATCH, SEQ, D), 1.0),
        "x_sample": nrm((DEC_BATCH, DEC_SEQ, D), 1.0),
        "norm_mix": gain((DEPTH, D)),
        "norm_ffn": gain((DEPTH, D)),
        "norm_final": gain((D,)),
        "ev_w_in": nrm((N_EVEN, D, EVEN_IN), D ** -0.5),
        "ev_conv_a": nrm((N_EVEN, A_QKV, SHORT_CONV), SHORT_CONV ** -0.5),
        "ev_alog_f": alog((N_EVEN, A_HEADS)),
        "ev_alog_b": alog((N_EVEN, A_HEADS)),
        "ev_dtb_f": dtb((N_EVEN, A_HEADS)),
        "ev_dtb_b": dtb((N_EVEN, A_HEADS)),
        "ev_onorm": gain((N_EVEN, A_DV)),
        "ev_conv_b": nrm((N_EVEN, 3 * B_WIDTH, SHORT_CONV), SHORT_CONV ** -0.5),
        "hy_w1": nrm((N_EVEN, HY_EMB, HY_FFN), HY_EMB ** -0.5),
        "hy_b1": nrm((N_EVEN, HY_FFN), 0.02),
        "hy_w2": nrm((N_EVEN, HY_FFN, HY_FFN), HY_FFN ** -0.5),
        "hy_b2": nrm((N_EVEN, HY_FFN), 0.02),
        "hy_w3": nrm((N_EVEN, HY_FFN, HY_FFN), HY_FFN ** -0.5),
        "hy_b3": nrm((N_EVEN, HY_FFN), 0.02),
        "hy_w4": nrm((N_EVEN, HY_FFN, HY_ORDER * 2 * B_WIDTH), 0.05 * HY_FFN ** -0.5),
        "hy_freq": gain((N_EVEN, 3, HY_FFN)),
        "hy_dbias": nrm((N_EVEN, HY_ORDER, B_WIDTH), 1.0),
        "ev_w_out": nrm((N_EVEN, A_WIDTH + B_WIDTH, D), (A_WIDTH + B_WIDTH) ** -0.5),
        "od_w_qkv": nrm((N_ODD, D, ODD_IN), D ** -0.5),
        "od_sinks": nrm((N_ODD, C_HEADS), 0.5),
        "od_w_out": nrm((N_ODD, C_HEADS * C_HEAD_DIM, D), (C_HEADS * C_HEAD_DIM) ** -0.5),
        "moe_w_group": nrm((DEPTH, D, N_GROUPS), D ** -0.5),
        "moe_w_expert": nrm((DEPTH, D, N_GROUPS * EXPERTS_PER_GROUP), D ** -0.5),
        "moe_w_gate": nrm((DEPTH, N_GROUPS, EXPERTS_PER_GROUP, D, D_EXPERT), D ** -0.5),
        "moe_w_up": nrm((DEPTH, N_GROUPS, EXPERTS_PER_GROUP, D, D_EXPERT), D ** -0.5),
        "moe_w_down": nrm((DEPTH, N_GROUPS, EXPERTS_PER_GROUP, D_EXPERT, D), D_EXPERT ** -0.5),
    }

def reference(x_prompt, x_sample, norm_mix, norm_ffn, norm_final,
              ev_w_in, ev_conv_a, ev_alog_f, ev_alog_b, ev_dtb_f, ev_dtb_b, ev_onorm, ev_conv_b,
              hy_w1, hy_b1, hy_w2, hy_b2, hy_w3, hy_b3, hy_w4, hy_freq, hy_dbias, ev_w_out,
              od_w_qkv, od_sinks, od_w_out,
              moe_w_group, moe_w_expert, moe_w_gate, moe_w_up, moe_w_down):
    params = (norm_mix, norm_ffn, norm_final,
              ev_w_in, ev_conv_a, ev_alog_f, ev_alog_b, ev_dtb_f, ev_dtb_b, ev_onorm, ev_conv_b,
              hy_w1, hy_b1, hy_w2, hy_b2, hy_w3, hy_b3, hy_w4, hy_freq, hy_dbias, ev_w_out,
              od_w_qkv, od_sinks, od_w_out,
              moe_w_group, moe_w_expert, moe_w_gate, moe_w_up, moe_w_down)
    y_prompt = trunk(x_prompt, *params)
    y_sample = trunk(x_sample, *params)
    return (y_prompt, y_sample)


_drawn_inputs = setup_inputs


def setup_inputs(seed=0):
    import zlib

    import numpy as np

    out = dict(_drawn_inputs(seed))
    spreads = {}
    factors = {'norm_final': 8.238, 'od_sinks': 2.793, 'hy_b1': 2.669, 'hy_b3': 2.738}
    for name, (base, spread) in spreads.items():
        noise = np.random.default_rng([zlib.crc32(name.encode()), seed]).standard_normal(out[name].shape)
        drawn = base * np.exp(spread * noise) if base else spread * noise
        out[name] = __import__('jax').numpy.asarray(drawn.astype(out[name].dtype))
    for name, factor in factors.items():
        out[name] = (out[name] * factor).astype(out[name].dtype)
    return out
```

```python
import math
from contextlib import ExitStack

import numpy as np

import concourse.bass as bass
from concourse import mybir

D, SEQ, NSEQ = 1024, 256, 2
TOK = NSEQ * SEQ
P = 128
NT = TOK // P
KT = D // P
EPS = 1e-6
HEADS, CHUNK = 4, 64
B_WIDTH = 512
HQ, HD, WINDOW = 16, 64, 128
NEXP, NGRP, EPG, FE = 32, 4, 8, 256
CAP = P // 2
NPAIR = NEXP // 2
ROUNDS = TOK // CAP
NOROW = 4096.0
U = 512
NEG = -1e30
LEVELS = (1, 2, 4, 8, 16, 32)
GUW = KT * 2 * FE
DNW = (FE // P) * D


def persistent_constants():
    c = np.zeros((P, 1024), np.float32)
    r = np.arange(P)
    c[:, 0:128] = np.eye(P)
    c[:, 128:256] = r[:, None] < r[None, :]
    c[:, 256:384] = 1.0
    c[:, 384:416] = np.arange(NEXP)[None, :]
    for k in range(2):
        for t in range(NT):
            c[:, 416 + k * NT + t] = k * TOK + t * P + r
    c[:, 424] = EPS
    c[:, 428:460] = np.arange(NEXP)[None, :] * CAP
    c[:, 460:492] = np.arange(NEXP)[None, :] // EPG
    return c


def mixer_constants():
    c = np.zeros((P, 12 * U), np.float32)
    r = np.arange(P)
    row, col = r[:, None], r[None, :]
    same = row // CHUNK == col // CHUNK
    for n, s in enumerate(LEVELS):
        low = (row // (2 * s) == col // (2 * s)) & ((row // s) % 2 == 1) & ((col // s) % 2 == 0)
        c[:, n * P:(n + 1) * P] = low
        c[:, (6 + n) * P:(7 + n) * P] = low.T
    c[:, 12 * P:13 * P] = same & (row <= col)
    c[:, 13 * P:14 * P] = same & (row >= col)
    c[:, 14 * P:15 * P] = same
    t = np.arange(SEQ)
    f = np.arange(SEQ)
    w = 2.0 * np.pi * np.outer(t, f) / (2 * SEQ)
    alt = (-1.0) ** t
    cos, msin = np.cos(w), -np.sin(w)
    fu = np.concatenate([cos, msin], 1)
    fu[:, SEQ] = alt
    fs = msin.copy()
    fs[:, 0] = 0.0
    fc = cos[:, :P].copy()
    fc[:, 0] = alt
    g = np.concatenate([2 * cos.T, 2 * msin.T], 0) / (2 * SEQ)
    g[0] *= 0.5
    g[SEQ] = alt / (2 * SEQ)
    for k in range(4):
        c[:, 4 * U + k * SEQ:4 * U + (k + 1) * SEQ] = g[k * P:(k + 1) * P]
    for k in range(2):
        c[:, 6 * U + k * U:6 * U + (k + 1) * U] = fu[k * P:(k + 1) * P]
        c[:, 8 * U + k * SEQ:8 * U + (k + 1) * SEQ] = fs[k * P:(k + 1) * P]
        c[:, 9 * U + k * P:9 * U + (k + 1) * P] = fc[k * P:(k + 1) * P]
    tt = np.linspace(0.0, 1.0, SEQ)[:, None]
    wpos = (2.0 * np.pi / SEQ) * t[:, None]
    bands = np.linspace(1e-4, 15, 16)[None, :]
    feats = np.concatenate([tt, np.cos(bands * wpos), -np.sin(bands * wpos)], 1)
    c[0:33, 9 * U + 256:10 * U] = feats.T
    deltas = np.abs(np.linspace(math.log(1e-2) / 1.5, math.log(1e-2) / 0.3, B_WIDTH))
    win = np.exp(-tt * deltas[None, :])
    for k in range(2):
        c[:, (10 + k) * U:(11 + k) * U] = win[k * P:(k + 1) * P]
    return c


def distance_constants():
    i = np.arange(SEQ)[:, None]
    j = np.arange(SEQ)[None, :]
    d = np.where(np.abs(i - j) <= WINDOW, -np.abs(i - j).astype(np.float64), NEG)
    return d.reshape(2, P, SEQ).transpose(1, 0, 2).reshape(P, 2 * SEQ).astype(np.float32).copy()


PA_CONVA, PA_CONVB, PA_DB, PA_ON = 0, 36, 72, 80
PA_FREQ, PA_B = 81, 84
PA_ALOG, PA_DTB, PA_SINK = 87, 95, 103
PA_W1, PA_W2, PA_W3 = 119, 183, 247
PA_W4 = 311
NPAR = PA_W4 + 2048


def trunk_program(nc, x_in, gains, pconst, mconst, dconst, params, w_in, w_ab, w_out0, w_qkv, w_out1,
                  w_router, w_gu, w_dn, y_out):
    f32, u32 = mybir.dt.float32, mybir.dt.uint32
    ALU, ACT = mybir.AluOpType, mybir.ActivationFunctionType
    AXX = mybir.AxisListType.X
    ctx = ExitStack()
    with ctx:
        def sb(name, shape, dt=f32):
            return ctx.enter_context(nc.sbuf_tensor(name, shape, dt))

        def sem(name):
            return ctx.enter_context(nc.semaphore(name))

        def sems(name, n):
            return [sem(f"{name}{i}") for i in range(n)]

        h_dram = [nc.dram_tensor(f"h_dram{L}", (TOK, D), f32, kind="Internal").ap() for L in range(2)]
        yk_dram = [nc.dram_tensor(f"yk_dram{L}", (2 * TOK, D), f32, kind="Internal").ap() for L in range(2)]
        tab_dram = [nc.dram_tensor(f"tab_dram{L}", (P, P), f32, kind="Internal").ap() for L in range(2)]

        arena = sb("arena", [P, 100 * U])
        parm = sb("parm", [P, PA_W4])

        def units(a, n=1):
            return arena[:, a * U:(a + n) * U]

        X = units(0, 8).rearrange("p (t d) -> p t d", t=NT)
        HT = units(8, 8).rearrange("p (k t) -> p k t", k=KT)
        pc = units(16, 2)
        ident, strictU, ones = pc[:, 0:128], pc[:, 128:256], pc[:, 256:384]
        iota_e, tokid, eps_c = pc[:, 384:416], pc[:, 416:424], pc[:, 424:425]
        e_row, e_grp = pc[:, 428:460], pc[:, 460:492]
        gu = [units(18 + 16 * s, 16).rearrange("p (h k n) -> p h k n", h=2, k=KT) for s in range(2)]
        dn = [units(50 + 8 * s, 8).rearrange("p (h f n) -> p h f n", h=2, f=FE // P) for s in range(2)]
        mc = units(18, 12)

        def mask(n):
            return mc[:, n * P:(n + 1) * P]
        incl = [mask(12), mask(13)]
        chunk_ones = mask(14)
        G = mc[:, 4 * U:6 * U].rearrange("p (k t) -> p k t", k=4)
        F = mc[:, 6 * U:8 * U].rearrange("p (k f) -> p k f", k=2)
        Fs0 = mc[:, 8 * U:9 * U].rearrange("p (k f) -> p k f", k=2)
        Fc0 = mc[:, 9 * U:9 * U + 256].rearrange("p (k f) -> p k f", k=2)
        featsT = mc[0:33, 9 * U + 256:10 * U]
        window = mc[:, 10 * U:12 * U].rearrange("p (k f) -> p k f", k=2)
        wchunk = [units(30 + 8 * s, 8).rearrange("p (k n) -> p k n", k=KT) for s in range(3)]
        NCH = 7
        hx = units(54, 12).rearrange("p (m t) -> p m t", m=12)
        qT, kT, vT, zT = (units(66 + 4 * s, 4).rearrange("p (h t) -> p h t", h=HEADS) for s in range(4))
        qkvz = units(66, 16).rearrange("p (m t) -> p m t", m=16)
        Kf = units(82, 10).rearrange("p (o j c) -> p o j c", o=2, j=5)
        HP = units(92, 8).rearrange("p (o i s c) -> p o i s c", o=2, i=2, s=2)
        w4 = units(50, 4)[0:64, :]
        UT = units(30, 4).rearrange("p (b i c) -> p b i c", b=2, i=2)
        RF = units(66, 4).rearrange("p (j s c) -> p j s c", j=2, s=2)
        fz = units(70, 2)[0:64, 0:3 * SEQ].rearrange("p (j t) -> p j t", j=3)
        norow = units(72)[:, 0:P]
        YF = units(34, 8).rearrange("p (b f c) -> p b f c", b=2, f=4)
        TP = units(42, 8).rearrange("p (s j c) -> p s j c", s=2, j=4)
        Z1 = units(50, 4).rearrange("p (m t) -> p m t", m=4)
        OB = units(92, 4).rearrange("p (m t) -> p m t", m=4)
        ZT = units(96, 2).rearrange("p (s t) -> p s t", s=2)
        ktok = units(8, 4).rearrange("p (t h d) -> p t h d", t=NT, h=HEADS)
        vtok = units(12, 4).rearrange("p (t h d) -> p t h d", t=NT, h=HEADS)
        sqn = units(42, 4).rearrange("p (s t) -> p s t", s=4)
        rsn = units(46, 4).rearrange("p (s t) -> p s t", s=4)

        def h4(ap):
            return ap.rearrange("p (h c) -> p h c", h=HEADS)
        QK, QD, KD, UU, WT = ([h4(units(22 + 4 * n + q)) for q in range(4)] for n in range(5))
        XX, XT, AA, AL, YY = ([h4(units(42 + 4 * n + q)) for q in range(4)] for n in range(5))
        KBG = [h4(units(82 + q)) for q in range(4)]
        VB = [h4(units(86 + q)) for q in range(4)]
        DA, DT = h4(units(90)), h4(units(91))
        RG = [h4(units(96 + s)) for s in range(2)]
        VN = [h4(units(98 + s)) for s in range(2)]
        ST = [[h4(units(62 + 2 * d + s)) for s in range(2)] for d in range(2)]
        OA = units(74, 4).rearrange("p (h t) -> p h t", h=HEADS)
        osq = units(22, 4).rearrange("p (h t) -> p h t", h=HEADS)
        ors = units(26, 4).rearrange("p (h t) -> p h t", h=HEADS)
        wo = [units(a, 16).rearrange("p (k n) -> p k n", k=KT) for a in (42, 34)]
        aw = [units(a, 8).rearrange("p (k n) -> p k n", k=KT) for a in (18, 26, 50)]
        QT = units(66, 8).rearrange("p (m t) -> p m t", m=8)
        KTT = units(74, 2).rearrange("p (m t) -> p m t", m=2)
        V = units(76, 2).rearrange("p (t n) -> p t n", t=NT)
        SC = [units(78 + s).rearrange("p (h k) -> p h k", h=2) for s in range(4)]
        PT = [units(82 + 2 * s, 2).rearrange("p (j h q) -> p j h q", j=2, h=4) for s in range(2)]
        negd = units(90).rearrange("p (b k) -> p b k", b=2)
        OT = units(91, 8).rearrange("p (m t) -> p m t", m=8)
        HTOK = [units(54, 8).rearrange("p (t d) -> p t d", t=NT)] + \
               [units(66, 8).rearrange("p (t d) -> p t d", t=NT) for _ in range(4)]
        GAIN = [units(62, 2)] + [units(86, 2)] * 4
        JUNK = [units(64, 2)] + [units(88, 2)] * 4
        xg = [units(66 + 2 * s, 2) for s in range(4)]
        xgT = [units(78 + 2 * s, 2).rearrange("p (k t) -> p k t", k=KT) for s in range(2)]
        yt = [units(74 + 2 * s, 2) for s in range(2)]
        sil = [units(88)[:, 256 * s:256 * s + 256] for s in range(2)]
        act_h = [units(89)[:, 256 * s:256 * s + 256] for s in range(2)]
        actT = [units(90)[:, 256 * s:256 * s + 256].rearrange("p (j t) -> p j t", j=2) for s in range(2)]
        YK = units(66, 16).rearrange("p (n d) -> p n d", n=8)
        tab_sb = units(91)[:, 0:128]
        tab_val = units(91)[:, 128:256]
        tab_gat = units(91)[:, 256:384]
        router = units(92)[:, 0:KT * 36].rearrange("p (k n) -> p k n", k=KT)

        ss = sb("ss", [P, 5, NT])
        rstd = sb("rstd", [P, 5, NT])
        lnv = sb("lnv", [P, 5, NT])
        ab = sb("ab", [P, NT, 16])
        gt = sb("gt", [P, 6, NT, 8])
        wab = units(98)[:, 0:128].rearrange("p (k n) -> p k n", k=KT)
        GTEMP, BETA, GG, GC, KDS, KBS = range(6)
        rt = units(94, 4)
        lg = rt[:, 0:144].rearrange("p (t n) -> p t n", t=NT)
        gpad = rt[:, 144:176].rearrange("p (t n) -> p t n", t=NT)
        top_g = rt[:, 176:208].rearrange("p (t n) -> p t n", t=NT)
        idx_g = rt[:, 208:240].bitcast(u32).rearrange("p (t n) -> p t n", t=NT)
        top_e = rt[:, 240:272].rearrange("p (t n) -> p t n", t=NT)
        idx_e = rt[:, 272:304].bitcast(u32).rearrange("p (t n) -> p t n", t=NT)
        fi = rt[:, 304:320].rearrange("p (t n) -> p t n", t=NT)
        gexp = rt[:, 320:336].rearrange("p (t n) -> p t n", t=NT)
        emsk = rt[:, 336:464].rearrange("p (t n) -> p t n", t=NT)
        oh = rt[:, 512:1024].rearrange("p (k t n) -> p k t n", k=4, t=NT)
        gat_i = rt[:, 1024:1152].bitcast(u32)
        sca_i = rt[:, 1152:1280].bitcast(u32)
        rtmp = rt[:, 1280:1312].rearrange("p (k t) -> p k t", k=8)
        coef = sb("coef", [P, 8, NT])
        rowf = sb("rowf", [P, 2, NT])
        rowi = sb("rowi", [P, 2, NT], u32)
        gcur = sb("gcur", [P, 4], u32)
        scur = sb("scur", [P, 4], u32)
        cmax = sb("cmax", [P, 1])
        flag = sb("flag", [P, 1], u32)
        mx = sb("mx", [P, 8, 2])
        den = sb("den", [P, 8, 2])
        es = sb("es", [P, 8, 2])
        nb = sb("nb", [P, 8, 2])
        sink8 = sb("sink8", [P, HQ])
        gls = sb("gls", [P, 8, HEADS, 2])

        pb = [ctx.enter_context(nc.psum_tensor(f"bank{i}", [P, U], f32)) for i in range(8)]

        ld_x, ld_p, ld_ab, ld_w4, ld_dist = (sem(n) for n in
            ("x_loaded", "params_loaded", "wab_loaded", "w4_loaded", "dist_loaded"))
        ld_gain = sem("gain_loaded")
        ld_wc = sems("w_in_loaded", 3)
        ld_wo = sem("w_out_loaded")
        ld_aw = sem("w_qkv_loaded")
        ld_rt = sem("router_loaded")
        tab_init = sem("table_initialised")
        s_ss, s_rstd = sem("sumsq_done"), sem("rstd_done")
        s_h = sem("h_done")
        s_tr = sem("h_transposed")
        s_hTa, s_hTd = sem("hT_even_copied"), sem("hT_odd_copied")
        s_x = sem("x_updated")
        dch, ach, pch = sem("vector_chain"), sem("scalar_chain"), sem("pool_chain")
        f_ps, f_sin, f_ht, f_h4 = (sem(n) for n in ("filter_psum", "filter_sin", "filter_taps", "filter_rows"))
        f_red = sem("filter_reduced")
        m_qm, m_gl = sem("qkmat_masked"), sem("chunk_gates_kept")
        r_gs = sem("group_shifted")
        e_cg, e_cs = sem("gather_ids_copied"), sem("scatter_ids_copied")
        f_k, f_kc = sem("filter_dft"), sem("filter_dft_copied")
        s_pm, s_cva, s_cvd, s_sil = (sem(n) for n in ("proj_done", "conv_centre", "conv_sides", "silu_done"))
        s_ab, s_abc = sem("ab_done"), sem("ab_copied")
        y_tr, y_ut, y_u, y_p, y_y, y_i, y_z, y_o = (sem(n) for n in (
            "hy_transposed", "hy_time_copied", "hy_spectrum", "hy_products", "hy_product_sums",
            "hy_inverse", "hy_biased", "hy_gated"))
        g_gate, g_cum, g_gc, g_gx = (sem(n) for n in ("gates_done", "cumsum_done", "cumsum_copied", "cumsum_exp"))
        n_sq, n_ss, n_rs, n_n = (sem(n) for n in ("squared", "sumsq_bcast", "rstd_bcast", "qk_normed"))
        t_kv, t_kvc = sem("kv_transposed"), sem("kv_copied")
        m_r, m_gb, m_kk, m_qk = (sem(n) for n in ("decay_rows", "decay_bcast", "kk_done", "qk_done"))
        m_d, m_c, m_e, m_a, m_q, m_s = (sem(n) for n in (
            "decay_diff", "decay_clamped", "decay_exp", "amat_done", "qkmat_done", "scaled_done"))
        m_m, m_mt, m_x0, m_al = (sem(n) for n in ("mask1_done", "mask1_transposed", "inverse_started", "level_masked"))
        m_y, m_yc, m_xp, m_xc = (sem(n) for n in ("zT_done", "zT_copied", "offdiag_done", "inverse_updated"))
        m_uw, m_uwc, m_qd = sem("uw_done"), sem("uw_copied"), sem("qdec_done")
        c_w, c_v, c_o, c_oc, c_s, c_sc = (sem(n) for n in (
            "scan_ws", "scan_vnew", "scan_o", "scan_o_copied", "scan_kv", "scan_state"))
        o_n = sem("o_gated")
        p_o = sem("out_proj_done")
        r_lg, r_lc, r_oh, r_rk, r_row, r_val, r_tt, r_fl = (sem(n) for n in (
            "logits_done", "group_exp_done", "onehot_done", "rank_done", "rows_done", "table_loaded",
            "table_transposed", "slots_ready"))
        r_sc, r_hd = sem("ids_scattered"), sem("h_stored")
        w_gs, w_ds = sems("gate_up_loaded", 2), sems("down_loaded", 2)
        e_xg = sems("expert_gathered", 4)
        e_T, e_xa, e_xd = sem("exp_transposed"), sem("exp_xT_a_copied"), sem("exp_xT_d_copied")
        e_GU, e_si, e_ac = sem("exp_gate_up"), sem("exp_silu"), sem("exp_act")
        e_HT, e_aT, e_D, e_ya, e_yd = (sem(n) for n in (
            "exp_act_transposed", "exp_actT_copied", "exp_down", "exp_y_a_copied", "exp_y_d_copied"))
        e_sc = sems("expert_scattered", 2)
        ld_yk = sems("yk_loaded", NT)
        ov = [{n: sem(f"more_{n}{L}") for n in ("pe", "act", "dve", "ids", "w", "g", "sc")} for L in range(2)]
        a_pm, a_pca, a_pcd = sem("qkv_done"), sem("qkv_even_copied"), sem("qkv_odd_copied")
        a_s, a_sc, a_mx, a_nb = (sem(n) for n in ("scores_done", "scores_biased", "score_max", "score_negmax"))
        a_e, a_rd, a_p, a_pt, a_pc, a_o, a_oc = (sem(n) for n in (
            "exp_done", "den_recip", "probs_done", "probs_transposed", "probsT_copied", "attn_out", "attn_copied"))
        st_y = sem("y_stored")

        X_DONE = [0, 8, 16, 24, 32]
        LOGD = 1.0 / D

        def slopes(head):
            return float(2.0 ** (-8.0 * (head + 1) / HQ))

        def head_of(t, s):
            return (4 * s + t) if t < 4 else (8 + 4 * s + t - 4)

        block = ctx.enter_context(nc.Block())

        @block.sync
        def _(sp):
            for t in range(NT):
                sp.dma_start(X[:, t, :], x_in[t * P:(t + 1) * P, :]).then_inc(ld_x, 16)
            sp.dma_start(pc, pconst[:, :]).then_inc(ld_p, 16)
            sp.dma_start(parm[:, :], params[:, 0:PA_W4]).then_inc(ld_p, 16)
            sp.dma_start(GAIN[0], gains[0, :, :]).then_inc(ld_gain, 16)
            sp.dma_start(mc, mconst[:, :]).then_inc(ld_p, 16)
            sp.wait_ge(pch, 1)
            for L in range(2):
                sp.dma_start(tab_dram[L][:, :], norow).then_inc(tab_init, 16)
            for c in range(NCH):
                if c >= 3:
                    sp.wait_ge(s_pm, 4 * (c - 2))
                if c == 2:
                    sp.dma_start(w4, params[0:64, PA_W4:NPAR]).then_inc(ld_w4, 16)
                    sp.wait_ge(f_h4, 8)
                sp.dma_start(wchunk[c % 3], w_in[c, :, :, :]).then_inc(ld_wc[c % 3], 16)
            sp.wait_ge(f_k, 10)
            sp.dma_start(wab, w_ab[:, :, :]).then_inc(ld_ab, 16)
            sp.wait_ge(m_uw, 2 * 8)
            sp.dma_start(wo[0], w_out0[:, :, :]).then_inc(ld_wo, 16)

            def moe_loads(L):
                sp.dma_start(GAIN[2 * L + 1], gains[2 * L + 1, :, :]).then_inc(ld_gain, 16)
                sp.dma_start(router, w_router[L, :, :, :]).then_inc(ld_rt, 16)
                for p in range(2):
                    if L == 0 or p == 1:
                        sp.dma_start(gu[p], w_gu[L, p, :, :]).then_inc(w_gs[p], 16)
                    if L == 0:
                        sp.dma_start(dn[p], w_dn[L, p, :, :]).then_inc(w_ds[p], 16)
                sp.wait_ge(s_h, NT * (2 * L + 2))
                for t in range(NT):
                    sp.dma_start(h_dram[L][t * P:(t + 1) * P, :], HTOK[1][:, t, :]).then_inc(r_hd, 16)
                sp.wait_ge(r_sc, 128 * (L + 1))
                sp.dma_start(tab_sb, tab_dram[L][:, :]).then_inc(r_val, 16)

                B = NPAIR * L
                with sp.Fori(0, NPAIR // 2 - 1) as i:
                    for j in range(2):
                        g_src = w_gu[L, bass.ds(sp.snap(i * 2 + (j + 2)), 1), :, :].rearrange("o p n -> (o p) n")
                        d_src = w_dn[L, bass.ds(sp.snap(i * 2 + (j + 2)), 1), :, :].rearrange("o p n -> (o p) n")
                        sp.wait_ge(e_GU, i * 2 + (j + 1 + B))
                        sp.dma_start(gu[j], g_src).then_inc(w_gs[j], 16)
                        sp.wait_ge(e_D, i * 2 + (j + 1 + B))
                        sp.dma_start(dn[j], d_src).then_inc(w_ds[j], 16)
                o = ov[L]
                sp.wait_ge(r_fl, L + 1)
                more = sp.value_load(flag[0:1, 0:1], min_val=0, max_val=TOK)
                with sp.If(more > CAP):
                    sp.wait_ge(e_D, NPAIR * (L + 1))
                    sp.dma_start(gu[0], w_gu[L, 0, :, :]).then_inc(o["w"], 16)
                    sp.dma_start(dn[0], w_dn[L, 0, :, :]).then_inc(o["w"], 16)
                    for r in range(1, ROUNDS):
                        lo = 1 if r == 1 else 0
                        with sp.Fori(lo, NPAIR) as e:
                            g_src = w_gu[L, bass.ds(e, 1), :, :].rearrange("o p n -> (o p) n")
                            d_src = w_dn[L, bass.ds(e, 1), :, :].rearrange("o p n -> (o p) n")
                            sp.wait_ge(o["pe"], e * 4 + 4 * (r - 1) * NPAIR)
                            sp.dma_start(gu[0], g_src).then_inc(o["w"], 16)
                            sp.dma_start(dn[0], d_src).then_inc(o["w"], 16)
                    sp.wait_ge(o["sc"], 16 * NPAIR * (ROUNDS - 1))
                for s in range(2):
                    sp.wait_ge(e_sc[s], 16 * (NPAIR // 2) * (L + 1))
                for n in range(8):
                    sp.dma_start(YK[:, n, :], yk_dram[L][n * P:(n + 1) * P, :]).then_inc(ld_yk[n % NT], 16)

            sp.wait_ge(p_o, 8)
            moe_loads(0)
            sp.wait_ge(e_D, NPAIR)
            for s in range(3):
                sp.dma_start(aw[s], w_qkv[s, :, :, :]).then_inc(ld_aw, 16)
            sp.dma_start(wo[1], w_out1[:, :, :]).then_inc(ld_wo, 16)
            sp.dma_start(GAIN[2], gains[2, :, :]).then_inc(ld_gain, 16)
            sp.dma_start(negd, dconst[:, :].rearrange("p (b k) -> p b k", b=2)).then_inc(ld_dist, 16)
            sp.wait_ge(a_pm, 14)
            sp.dma_start(gu[0], w_gu[1, 0, :, :]).then_inc(w_gs[0], 16)
            for s in range(2):
                sp.dma_start(dn[s], w_dn[1, s, :, :]).then_inc(w_ds[s], 16)
            sp.wait_ge(s_h, 3 * NT)
            sp.wait_ge(p_o, 16)
            moe_loads(1)
            sp.wait_ge(s_h, 4 * NT)
            sp.dma_start(GAIN[4], gains[4, :, :]).then_inc(ld_gain, 16)
            for t in range(NT):
                sp.wait_ge(s_h, 4 * NT + t + 1)
                sp.dma_start(y_out[t * P:(t + 1) * P, :], HTOK[4][:, t, :]).then_inc(st_y, 16)
            sp.wait_ge(st_y, 16 * NT)

        @block.tensor
        def _(pe):
            mm, tr = nc.tensor.matmul, nc.tensor.transpose

            def transpose_h(n):
                for k in range(KT):
                    if k == 0:
                        pe.wait_ge(s_h, NT * (n + 1))
                    if k >= 2:
                        pe.wait_ge((s_hTa, s_hTd)[k % 2], 4 * n + k // 2)
                    for t in range(NT):
                        i = tr(pb[k % 2][:, t * P:(t + 1) * P], HTOK[n][:, t, k * P:(k + 1) * P], ident)
                    i.then_inc(s_tr, 1)

            def hT_ready(n):
                pe.wait_ge(s_hTa, 4 * (n + 1))
                pe.wait_ge(s_hTd, 4 * (n + 1))

            pe.wait_ge(ld_p, 48)
            mm(pb[7][0:64, 0:SEQ], parm[0:33, PA_W1:PA_W1 + 64], featsT, start=True, stop=True).then_inc(f_ps, 1)
            for j in range(2):
                pe.wait_ge(f_sin, j + 1)
                w = (PA_W2, PA_W3)[j]
                mm(pb[7][0:64, 0:SEQ], parm[0:64, w:w + 64], fz[:, 0, :], start=True, stop=True).then_inc(f_ps, 1)
            pe.wait_ge(ld_p, 48)
            transpose_h(0)
            pe.wait_ge(f_sin, 3)
            pe.wait_ge(ld_w4, 16)
            for n in range(8):
                o, i, s = n // 4, (n // 2) % 2, n % 2
                if n >= 4:
                    pe.wait_ge(f_ht, n // 2 - 1)
                mm(pb[2 + n % 4][:, :], fz[:, 0, i * P:(i + 1) * P], w4[:, (2 * o + s) * U:(2 * o + s + 1) * U],
                   start=True, stop=True).then_inc(f_h4, 1)
            for o in range(2):
                pe.wait_ge(f_ht, 2 * (o + 1))
                for j in range(5):
                    n = 5 * o + j
                    if n >= 2:
                        pe.wait_ge(f_kc, n - 1)
                    for i in range(2):
                        lhs = F[:, i, j * P:(j + 1) * P] if j < 2 else (
                            Fs0[:, i, (j - 2) * P:(j - 1) * P] if j < 4 else Fc0[:, i, :])
                        q = mm(pb[6 + n % 2][:, :], lhs, HP[:, o, i, 1 if j in (2, 3) else 0, :],
                               start=(i == 0), stop=(i == 1))
                    q.then_inc(f_k, 1)
            hT_ready(0)
            for m in range(28):
                c = m // 4
                if m % 4 == 0:
                    pe.wait_ge(ld_wc[c % 3], 16 * (c // 3 + 1))
                if m >= 4:
                    if m - 4 < 24:
                        pe.wait_ge(s_cvd, 2 * (m - 3))
                for k in range(KT):
                    i = mm(pb[m % 4][:, :], wchunk[c % 3][:, k, (m % 4) * P:(m % 4 + 1) * P], HT[:, k, :],
                           start=(k == 0), stop=(k == KT - 1))
                i.then_inc(s_pm, 1)
            pe.wait_ge(ld_ab, 16)
            for t in range(NT):
                for k in range(KT):
                    i = mm(pb[4][:, t * 16:(t + 1) * 16], HT[:, k, t * P:(t + 1) * P], wab[:, k, :],
                           start=(k == 0), stop=(k == KT - 1))
            i.then_inc(s_ab, 1)

            pe.wait_ge(s_abc, 1)
            pe.wait_ge(f_kc, 10)
            for o in range(2):
                src = hx[:, 8:12, :] if o == 0 else Z1
                if o == 0:
                    pe.wait_ge(s_cvd, 24)
                    pe.wait_ge(s_sil, 16)
                else:
                    pe.wait_ge(y_o, 4)
                for n in range(4):
                    if o == 1:
                        pe.wait_ge(y_z, 4)
                    for c in range(4):
                        i = tr(pb[n][:, c * P:(c + 1) * P], src[:, c, n * P:(n + 1) * P], ident)
                    i.then_inc(y_tr, 1)
                for b in range(2):
                    pe.wait_ge(y_ut, 4 * o + 2 * b + 2)
                    for pair in range(2):
                        u = 2 * b + pair
                        if u >= 2:
                            pe.wait_ge(y_p, 16 * o + 4 * (u - 1))
                        for ri in range(2):
                            f = pair + 2 * ri
                            for i in range(2):
                                q = mm(pb[4 + 2 * (u % 2) + ri][:, :], F[:, i, f * P:(f + 1) * P], UT[:, b, i, :],
                                       start=(i == 0), stop=(i == 1))
                        q.then_inc(y_u, 1)
                pe.wait_ge(y_y, 8 * (o + 1))
                for c in range(4):
                    for b in range(2):
                        for f in range(4):
                            i = mm(pb[c][:, b * SEQ:(b + 1) * SEQ], YF[:, b, f, c * P:(c + 1) * P], G[:, f, :],
                                   start=(f == 0), stop=(f == 3))
                    i.then_inc(y_i, 1)

            pe.wait_ge(g_gate, 1)
            pe.wait_ge(y_p, 32)
            for d in range(2):
                mm(pb[4][:, 16 * d:16 * d + 16], incl[d], gt[:, GG, :, 4 * d:4 * d + 4], start=True, stop=True)
            mm(pb[4][:, 32:64], chunk_ones, gt[:, GG, :, :], start=True, stop=True).then_inc(g_cum, 1)
            pe.wait_ge(y_z, 8)
            for n in range(8):
                pe.wait_ge(n_sq, n + 1)
                if n >= 2:
                    pe.wait_ge(n_rs, n - 1)
                mm(pb[6 + n % 2][:, :], ones, sqn[:, n % 4, :], start=True, stop=True).then_inc(n_ss, 1)
            for n in range(8):
                src = vT if n < 4 else kT
                t = n % 4
                if n == 4:
                    pe.wait_ge(n_n, 8)
                if n >= 4:
                    pe.wait_ge(t_kvc, n - 3)
                for h in range(HEADS):
                    i = tr(pb[n % 4][:, h * P:(h + 1) * P], src[:, h, t * P:(t + 1) * P], ident)
                i.then_inc(t_kv, 1)
            pe.wait_ge(t_kvc, 8)

            for b in range(NSEQ):
                for q in range(4):
                    n = 4 * b + q
                    t, d = 2 * b + q // 2, q % 2
                    pe.wait_ge(m_r, n + 1)
                    if n >= 2:
                        pe.wait_ge(m_d, n - 1)
                        pe.wait_ge(m_e, 3 * (n - 1))
                    mm(pb[0 + n % 2][:, :], ones, RG[n % 2], start=True, stop=True).then_inc(m_gb, 1)
                    if d == 0:
                        if n >= 2:
                            pe.wait_ge(m_a, n)
                            pe.wait_ge(m_q, n)
                        for h in range(HEADS):
                            i = mm(pb[2][:, h * P:(h + 1) * P], kT[:, h, t * P:(t + 1) * P],
                                   kT[:, h, t * P:(t + 1) * P], start=True, stop=True)
                        i.then_inc(m_kk, 1)
                        for h in range(HEADS):
                            i = mm(pb[3][:, h * P:(h + 1) * P], kT[:, h, t * P:(t + 1) * P],
                                   qT[:, h, t * P:(t + 1) * P], start=True, stop=True)
                        i.then_inc(m_qk, 1)
                for q in range(4):
                    n = 4 * b + q
                    pe.wait_ge(m_m, n + 1)
                    if q >= 2:
                        pe.wait_ge(m_x0, 2 * (n - 1))
                    for h in range(HEADS):
                        i = tr(pb[4 + q % 2][:, h * P:(h + 1) * P], AL[q][:, h, :], ident)
                    i.then_inc(m_mt, 1)
                for lv in range(1, 6):
                    for q in range(4):
                        n = 4 * b + q
                        g = 20 * b + 4 * (lv - 1) + q
                        pe.wait_ge(m_al, g + 1)
                        if lv == 1:
                            pe.wait_ge(m_x0, 2 * (n + 1))
                            pe.wait_ge(m_q, n + 1)
                        else:
                            pe.wait_ge(m_xc, 36 * b + 8 * (lv - 2) + 2 * (q + 1))
                        if g >= 2:
                            pe.wait_ge(m_yc, g - 1)
                        for h in range(HEADS):
                            i = mm(pb[g % 2][:, h * P:(h + 1) * P], AL[q][:, h, :], XT[q][:, h, :],
                                   start=True, stop=True)
                        i.then_inc(m_y, 1)
                    for q in range(4):
                        g = 20 * b + 4 * (lv - 1) + q
                        pe.wait_ge(m_yc, g + 1)
                        n2 = 36 * b + 8 * (lv - 1) + (2 * q if lv < 5 else q)
                        if lv < 5:
                            if n2 >= 4:
                                pe.wait_ge(m_xc, n2 - 3)
                            for h in range(HEADS):
                                i = mm(pb[2 + n2 % 4][:, h * P:(h + 1) * P], YY[q][:, h, :], XX[q][:, h, :],
                                       start=True, stop=True)
                            i.then_inc(m_xp, 1)
                            n2 += 1
                        if n2 >= 4:
                            pe.wait_ge(m_xc, n2 - 3)
                        for h in range(HEADS):
                            i = mm(pb[2 + n2 % 4][:, h * P:(h + 1) * P], XX[q][:, h, :], YY[q][:, h, :],
                                   start=True, stop=True)
                        i.then_inc(m_xp, 1)
                for q in range(4):
                    n = 4 * b + q
                    pe.wait_ge(m_s, 3 * (n + 1))
                    pe.wait_ge(m_xc, 36 * (b + 1))
                    if q >= 2:
                        pe.wait_ge(m_uwc, 2 * (n - 1))
                    for h in range(HEADS):
                        i = mm(pb[2 * (q % 2)][:, h * P:(h + 1) * P], XT[q][:, h, :], VB[q][:, h, :],
                               start=True, stop=True)
                    i.then_inc(m_uw, 1)
                    for h in range(HEADS):
                        i = mm(pb[2 * (q % 2) + 1][:, h * P:(h + 1) * P], KBG[q][:, h, :], XT[q][:, h, :],
                               start=True, stop=True)
                    i.then_inc(m_uw, 1)
                pe.wait_ge(m_uwc, 8 * (b + 1))
                pe.wait_ge(m_qd, 4 * (b + 1))
                pe.wait_ge(m_qm, 4 * (b + 1))
                pe.wait_ge(n_n, 8)
                for s in range(4):
                    for d in range(2):
                        g = 8 * b + 2 * s + d
                        c = s if d == 0 else 3 - s
                        q, half = 2 * (c // 2) + d, c % 2
                        rows = slice(CHUNK * half, CHUNK * half + CHUNK)
                        S = ST[d][s % 2]
                        if s > 0:
                            pe.wait_ge(c_sc, 6 * b + 2 * s + d - 1)
                            pe.wait_ge(c_v, g - 1)
                            for h in range(HEADS):
                                i = mm(pb[4 + d][rows, h * P:(h + 1) * P], WT[q][:, h, rows], S[:, h, :],
                                       start=True, stop=True)
                            i.then_inc(c_w, 1)
                    for d in range(2):
                        g = 8 * b + 2 * s + d
                        c = s if d == 0 else 3 - s
                        q, half = 2 * (c // 2) + d, c % 2
                        rows = slice(CHUNK * half, CHUNK * half + CHUNK)
                        S = ST[d][s % 2]
                        pe.wait_ge(c_v, g + 1)
                        if g >= 2:
                            pe.wait_ge(c_oc, g - 1)
                        for h in range(HEADS):
                            out = pb[6 + d][:, h * CHUNK:(h + 1) * CHUNK]
                            if s > 0:
                                mm(out, S[:, h, :], QD[q][:, h, rows], start=True, stop=False)
                            i = mm(out, VN[d][rows, h, :], QK[q][rows, h, rows], start=(s == 0), stop=True)
                        i.then_inc(c_o, 1)
                        if s < 3:
                            for h in range(HEADS):
                                i = mm(pb[2 + d][:, h * P:(h + 1) * P], KD[q][rows, h, :], VN[d][rows, h, :],
                                       start=True, stop=True)
                            i.then_inc(c_s, 1)

            pe.wait_ge(c_oc, 16)
            for h in range(HEADS):
                pe.wait_ge(n_sq, 8 + h + 1)
                if h >= 2:
                    pe.wait_ge(n_rs, 8 + h - 1)
                mm(pb[h % 2][:, :], ones, osq[:, h, :], start=True, stop=True).then_inc(n_ss, 1)

            def out_proj(L, oT):
                pe.wait_ge(ld_wo, 16 * (L + 1))
                for n in range(8):
                    t, c = n // 2, n % 2
                    if n >= 2:
                        pe.wait_ge(s_x, X_DONE[2 * L] + n - 1)
                    for k in range(KT):
                        i = mm(pb[2 + n % 2][:, :], oT(k)[:, t * P:(t + 1) * P], wo[L][:, k, c * U:(c + 1) * U],
                               start=(k == 0), stop=(k == KT - 1))
                    i.then_inc(p_o, 1)

            pe.wait_ge(o_n, HEADS)
            pe.wait_ge(c_sc, 12)
            pe.wait_ge(y_o, 8)
            out_proj(0, lambda k: OA[:, k, :] if k < 4 else OB[:, k - 4, :])

            def gate_up_products(out, xT, w):
                for k in range(KT):
                    for h in range(2):
                        cols = slice(CAP * h, CAP * h + CAP)
                        i = mm(out[cols, :], xT[:, k, cols], w[:, h, k, :], start=(k == 0), stop=(k == KT - 1))
                return i

            def down_products(aT, w):
                for c in range(2):
                    for f in range(2):
                        for h in range(2):
                            cols = slice(CAP * h, CAP * h + CAP)
                            i = mm(pb[5 + c][cols, :], aT[:, f, cols], w[:, h, f, c * U:(c + 1) * U],
                                   start=(f == 0), stop=(f == 1))
                return i

            def moe(L):
                n = 2 * L + 1
                transpose_h(n)
                hT_ready(n)
                pe.wait_ge(ld_rt, 16 * (L + 1))
                for t in range(NT):
                    for k in range(KT):
                        i = mm(pb[2][:, t * 36:(t + 1) * 36], HT[:, k, t * P:(t + 1) * P], router[:, k, :],
                               start=(k == 0), stop=(k == KT - 1))
                i.then_inc(r_lg, 1)
                pe.wait_ge(r_oh, L + 1)
                for t in range(NT):
                    for u in range(t + 1):
                        mm(pb[3][:, t * NEXP:(t + 1) * NEXP], ones if u < t else strictU, oh[:, 2, u, :],
                           start=(u == 0), stop=(u == t))
                for u in range(NT):
                    i = mm(pb[3][:, NT * NEXP:(NT + 1) * NEXP], ones, oh[:, 2, u, :], start=(u == 0), stop=(u == NT - 1))
                i.then_inc(r_rk, 1)
                pe.wait_ge(r_val, 16 * (L + 1))
                tr(pb[4][:, 0:P], tab_sb, ident).then_inc(r_tt, 1)
                pe.wait_ge(r_fl, L + 1)
                B = NPAIR * L

                def transposes(e, j):
                    pe.wait_ge(e_xg[j], (e - j) * 4 + (16 + 4 * B))
                    if not (isinstance(e, int) and e + B == 0):
                        pe.wait_ge(e_xa, e + B)
                        pe.wait_ge(e_xd, e + B)
                    for half in range(2):
                        for k in range(4):
                            i = tr(pb[half][:, k * P:(k + 1) * P],
                                   xg[j][:, (4 * half + k) * P:(4 * half + k + 1) * P], ident)
                    i.then_inc(e_T, 1)

                def gate_up(e, j):
                    pe.wait_ge(w_gs[j % 2], (e - j % 2) * 8 + (16 + 8 * B))
                    pe.wait_ge(e_xa, e + (B + 1))
                    pe.wait_ge(e_xd, e + (B + 1))
                    if not (isinstance(e, int) and e + B < 2):
                        pe.wait_ge(e_ac, e + (B - 1))
                    gate_up_products(pb[2 + j % 2], xgT[j % 2], gu[j % 2]).then_inc(e_GU, 1)

                def act_transposes(e, j):
                    pe.wait_ge(e_ac, e + (B + 1))
                    if not (isinstance(e, int) and e + B == 0):
                        pe.wait_ge(e_aT, e + B)
                    for f in range(2):
                        i = tr(pb[4][:, f * P:(f + 1) * P], act_h[j % 2][:, f * P:(f + 1) * P], ident)
                    i.then_inc(e_HT, 1)

                def down(e, j):
                    pe.wait_ge(e_aT, e + (B + 1))
                    if not (isinstance(e, int) and e + B == 0):
                        pe.wait_ge(e_ya, e + B)
                        pe.wait_ge(e_yd, e + B)
                    pe.wait_ge(w_ds[j % 2], (e - j % 2) * 8 + (16 + 8 * B))
                    down_products(actT[j % 2], dn[j % 2]).then_inc(e_D, 1)

                def four(i, first=False, last=False):
                    for j in range(4):
                        e = i * 4 + j
                        gate_up(e, j)
                        if not (first and j == 0):
                            act_transposes(e - 1, (j - 1) % 4)
                        if not (last and j == 3):
                            transposes(e + 1, (j + 1) % 4)
                        if not (first and j == 0):
                            down(e - 1, (j - 1) % 4)

                transposes(0, 0)
                four(0, first=True)
                with pe.Fori(1, NPAIR // 4 - 1) as i:
                    four(i)
                four(NPAIR // 4 - 1, last=True)
                act_transposes(NPAIR - 1, 3)
                down(NPAIR - 1, 3)

                o = ov[L]
                more = nc.tensor.value_load(flag[0:1, 0:1], min_val=0, max_val=TOK)
                with pe.If(more > CAP):
                    pe.wait_ge(e_ya, B + NPAIR)
                    pe.wait_ge(e_yd, B + NPAIR)
                    pe.wait_ge(e_aT, B + NPAIR)
                    for r in range(1, ROUNDS):
                        R = (r - 1) * NPAIR
                        with pe.Fori(0, NPAIR) as e:
                            pe.wait_ge(o["g"], e * 16 + 16 * (R + 1))
                            for half in range(2):
                                for k in range(4):
                                    i = tr(pb[half][:, k * P:(k + 1) * P],
                                           xg[0][:, (4 * half + k) * P:(4 * half + k + 1) * P], ident)
                            i.then_inc(o["pe"], 1)
                            pe.wait_ge(o["act"], e * 4 + (4 * R + 1))
                            pe.wait_ge(o["dve"], e * 3 + (3 * R + 1))
                            pe.wait_ge(o["w"], e * 32 + 32 * (R + 1))
                            i = gate_up_products(pb[2], xgT[0], gu[0])
                            i.then_inc(o["pe"], 1)
                            pe.wait_ge(o["dve"], e * 3 + (3 * R + 2))
                            for f in range(2):
                                i = tr(pb[4][:, f * P:(f + 1) * P], act_h[0][:, f * P:(f + 1) * P], ident)
                            i.then_inc(o["pe"], 1)
                            pe.wait_ge(o["act"], e * 4 + (4 * R + 3))
                            i = down_products(actT[0], dn[0])
                            i.then_inc(o["pe"], 1)
                            pe.wait_ge(o["act"], e * 4 + (4 * R + 4))
                            pe.wait_ge(o["dve"], e * 3 + (3 * R + 3))

            moe(0)

            transpose_h(2)
            hT_ready(2)
            for m in range(14):
                if m == 0:
                    pe.wait_ge(ld_aw, 48)
                if m >= 4:
                    pe.wait_ge((a_pca, a_pcd)[m % 2], m // 2 - 1)
                for k in range(KT):
                    if m < 10:
                        i = mm(pb[m % 4][:, :], aw[m // 4][:, k, (m % 4) * P:(m % 4 + 1) * P], HT[:, k, :],
                               start=(k == 0), stop=(k == KT - 1))
                    else:
                        t = m - 10
                        i = mm(pb[m % 4][:, 0:256], HT[:, k, t * P:(t + 1) * P], aw[2][:, k, 256:512],
                               start=(k == 0), stop=(k == KT - 1))
                i.then_inc(a_pm, 1)
            pe.wait_ge(a_pca, 7)
            pe.wait_ge(a_pcd, 7)

            def unit(n):
                b, qb, g, pr = n // 16, (n // 8) % 2, (n // 2) % 4, n % 2
                return b, qb, g, pr

            def scores(n):
                b, qb, g, pr = unit(n)
                rows = slice(64 * (g % 2), 64 * (g % 2) + 64)
                if n >= 2:
                    pe.wait_ge(a_sc, 2 * (n - 1))
                for hh in range(2):
                    t = 4 * (g // 2) + 2 * pr + hh
                    tok0 = b * SEQ + qb * P
                    i = mm(pb[n % 2][:, hh * SEQ:(hh + 1) * SEQ], QT[rows, t, tok0:tok0 + P],
                           KTT[rows, g // 2, b * SEQ:(b + 1) * SEQ], start=True, stop=True)
                i.then_inc(a_s, 1)

            def probs_t(n):
                pe.wait_ge(a_p, n + 1)
                if n >= 2:
                    pe.wait_ge(a_pc, n - 1)
                for hh in range(2):
                    for kt in range(2):
                        i = tr(pb[2 + n % 2][:, (2 * kt + hh) * P:(2 * kt + hh + 1) * P],
                               SC[n % 4][:, hh, kt * P:(kt + 1) * P], ident)
                i.then_inc(a_pt, 1)

            def pv(u):
                b, qb, g, _ = unit(2 * u)
                rows = slice(64 * (g % 2), 64 * (g % 2) + 64)
                pe.wait_ge(a_pc, 2 * u + 2)
                if u >= 2:
                    pe.wait_ge(a_oc, u - 1)
                for kt in range(2):
                    i = mm(pb[4 + u % 2][rows, :], V[:, 2 * b + kt, g * HD:(g + 1) * HD], PT[u % 2][:, kt, :, :],
                           start=(kt == 0), stop=(kt == 1))
                i.then_inc(a_o, 1)

            NU = 32
            for n in range(NU + 4):
                if n < NU:
                    scores(n)
                if 2 <= n < NU + 2:
                    probs_t(n - 2)
                if n >= 4 and n % 2 == 1:
                    pv((n - 5) // 2)
            pe.wait_ge(a_oc, 16)
            out_proj(1, lambda k: OT[:, k, :])
            moe(1)


        @block.scalar
        def _(act):
            af = nc.scalar.activation
            ac = [0]

            def link(i):
                ac[0] += 1
                i.then_inc(ach, 1)
                act.wait_ge(ach, ac[0])

            def norm_stats(n):
                for t in range(NT):
                    if n:
                        act.wait_ge(s_x, X_DONE[n] - 8 + 2 * (t + 1))
                    link(af(JUNK[n], X[:, t, :], ACT.Square, accum_out=ss[:, n, t:t + 1]))
                link(af(lnv[:, n, :], ss[:, n, :], ACT.Ln, bias=eps_c, scale=LOGD))
                af(rstd[:, n, :], lnv[:, n, :], ACT.Exp, scale=-0.5).then_inc(s_rstd, 1)

            def hT_copies(n):
                for k in range(0, KT, 2):
                    act.wait_ge(s_tr, KT * n + k + 1)
                    af(HT[:, k, :], pb[0][:, :], ACT.Copy).then_inc(s_hTa, 1)

            act.wait_ge(ld_x, 16 * NT)
            act.wait_ge(ld_p, 48)
            norm_stats(0)
            for j in range(3):
                act.wait_ge(f_red, j + 1)
                af(fz[:, 0, :], fz[:, 1, :], ACT.Sin).then_inc(f_sin, 1)
            hT_copies(0)
            for n in range(10):
                act.wait_ge(f_k, n + 1)
                af(Kf[:, n // 5, n % 5, :], pb[6 + n % 2][:, :], ACT.Copy).then_inc(f_kc, 1)

            def silu_tile(m):
                act.wait_ge(s_cvd, 2 * (m + 1))
                af(qkvz[:, m - 12, :], qkvz[:, m - 12, :], ACT.Silu).then_inc(s_sil, 1)
            for m in range(28):
                if m == 12:
                    act.wait_ge(tab_init, 32)
                act.wait_ge(s_pm, m + 1)
                if m < 24:
                    dst = hx[:, m, :] if m < 12 else qkvz[:, m - 12, :]
                    w = PA_CONVB + 3 * m + 1 if m < 12 else PA_CONVA + 3 * (m - 12) + 1
                    af(dst, pb[m % 4][:, :], ACT.Copy, scale=parm[:, w:w + 1]).then_inc(s_cva, 1)
                else:
                    if m == 24:
                        silu_tile(23)
                    af(qkvz[:, m - 12, :], pb[m % 4][:, :], ACT.Silu).then_inc(s_sil, 1)
                if 13 <= m < 24:
                    silu_tile(m - 1)

            act.wait_ge(s_abc, 1)
            af(gt[:, GTEMP, :, :], ab[:, :, 0:8], ACT.Exp, scale=-1.0)
            act.wait_ge(s_abc, 2)
            link(af(gt[:, KDS, :, :], gt[:, KDS, :, :], ACT.Exp))
            link(af(gt[:, KDS, :, :], gt[:, KDS, :, :], ACT.Ln, bias=ones[:, 0:1]))
            af(gt[:, KBS, 0, :], parm[:, PA_ALOG:PA_ALOG + 8], ACT.Exp).then_inc(g_gx, 1)

            for o in range(2):
                for n in range(4):
                    act.wait_ge(y_tr, 4 * o + n + 1)
                    af(UT[:, n // 2, n % 2, :], pb[n][:, :], ACT.Copy).then_inc(y_ut, 1)

            act.wait_ge(g_gc, 1)
            af(gt[:, KDS, :, :], gt[:, KDS, :, :], ACT.Exp)
            af(gt[:, KBS, :, :], gt[:, GC, :, :], ACT.Exp).then_inc(g_gx, 1)

            def qk_rstd(n):
                act.wait_ge(n_ss, n + 1)
                if n >= 4:
                    act.wait_ge(n_n, n - 3)
                link(af(rsn[:, n % 4, :], pb[6 + n % 2][:, :], ACT.Ln, bias=eps_c))
                af(rsn[:, n % 4, :], rsn[:, n % 4, :], ACT.Exp, scale=-0.5).then_inc(n_rs, 1)

            act.wait_ge(y_y, 16)
            for n in range(8):
                if n >= 4:
                    act.wait_ge(n_ss, n - 3)
                af(sqn[:, n % 4, :], qkvz[:, n, :], ACT.Square).then_inc(n_sq, 1)
                if n >= 1:
                    qk_rstd(n - 1)
            qk_rstd(7)
            for n in range(8):
                act.wait_ge(t_kv, n + 1)
                dst = vtok[:, n, :, :] if n < 4 else ktok[:, n - 4, :, :]
                af(dst, h4(pb[n % 4][:, :]), ACT.Copy).then_inc(t_kvc, 1)

            for b in range(NSEQ):
                if b == 1:
                    act.wait_ge(c_o, 8)
                    act.wait_ge(c_s, 6)
                for q in range(4):
                    n = 4 * b + q
                    act.wait_ge(m_d, n + 1)
                    af(QD[q], h4(pb[n % 2][:, :]), ACT.Exp).then_inc(m_e, 1)
                    act.wait_ge(m_e, 3 * n + 1)
                    last = QD[q][:, :, 63:128:64] if q % 2 == 0 else QD[q][:, :, 0:128:64]
                    af(gls[:, n, :, :], last, ACT.Copy).then_inc(m_gl, 1)
                    af(DA, DA, ACT.Exp, scale=-1.0).then_inc(m_e, 1)
                    af(DT, DT, ACT.Exp).then_inc(m_e, 1)
                for g in range(20 * b, 20 * b + 20):
                    act.wait_ge(m_y, g + 1)
                    af(YY[g % 4], h4(pb[g % 2][:, :]), ACT.Copy).then_inc(m_yc, 1)
                for q in range(4):
                    for j in range(2):
                        act.wait_ge(m_uw, 8 * b + 2 * q + j + 1)
                        af((UU, WT)[j][q], h4(pb[2 * (q % 2) + j][:, :]), ACT.Copy).then_inc(m_uwc, 1)

            act.wait_ge(c_oc, 16)
            for h in range(HEADS):
                af(osq[:, h, :], OA[:, h, :], ACT.Square).then_inc(n_sq, 1)
            for h in range(HEADS):
                act.wait_ge(n_ss, 8 + h + 1)
                link(af(ors[:, h, :], pb[h % 2][:, :], ACT.Ln, bias=eps_c, scale=1.0 / P))
                af(ors[:, h, :], ors[:, h, :], ACT.Exp, scale=-0.5).then_inc(n_rs, 1)

            def moe(L):
                n = 2 * L + 1
                norm_stats(n)
                hT_copies(n)
                act.wait_ge(r_gs, L + 1)
                af(gexp, gexp, ACT.Exp)
                af(coef[:, 0, :], coef[:, 0, :], ACT.Exp).then_inc(r_lc, 1)
                B = NPAIR * L
                act.wait_ge(r_fl, L + 1)

                def xT_copy(e, j):
                    act.wait_ge(e_T, e + (B + 1))
                    af(xgT[j % 2][:, 0:4, :], pb[0][:, :].rearrange("p (k t) -> p k t", k=4), ACT.Copy).then_inc(e_xa, 1)

                def silu(e, j):
                    act.wait_ge(e_GU, e + (B + 1))
                    if not (isinstance(e, int) and e + B < 2):
                        act.wait_ge(e_ac, e + (B - 1))
                    af(sil[j % 2], pb[2 + j % 2][:, 0:FE], ACT.Silu).then_inc(e_si, 1)

                def actT_copy(e, j):
                    act.wait_ge(e_HT, e + (B + 1))
                    af(actT[j % 2], pb[4][:, 0:FE].rearrange("p (j t) -> p j t", j=2), ACT.Copy).then_inc(e_aT, 1)

                def y_copy(e, j):
                    act.wait_ge(e_D, e + (B + 1))
                    if not (isinstance(e, int) and e + B < 2):
                        act.wait_ge(e_sc[j % 2], e * 8 + (8 * B - 8 * (j % 2)))
                    af(yt[j % 2][:, 0:U], pb[5][:, :], ACT.Copy).then_inc(e_ya, 1)

                def four(i, first=False, last=False):
                    for j in range(4):
                        e = i * 4 + j
                        silu(e, j)
                        if not (first and j == 0):
                            actT_copy(e - 1, (j - 1) % 4)
                        if not (last and j == 3):
                            xT_copy(e + 1, (j + 1) % 4)
                        if not (first and j == 0):
                            y_copy(e - 1, (j - 1) % 4)

                xT_copy(0, 0)
                four(0, first=True)
                with act.Fori(1, NPAIR // 4 - 1) as i:
                    four(i)
                four(NPAIR // 4 - 1, last=True)
                actT_copy(NPAIR - 1, 3)
                y_copy(NPAIR - 1, 3)

                o = ov[L]
                more = nc.scalar.value_load(flag[0:1, 0:1], min_val=0, max_val=TOK)
                with act.If(more > CAP):
                    for s in range(2):
                        act.wait_ge(e_sc[s], 16 * (NPAIR // 2) * (L + 1))
                    for r in range(1, ROUNDS):
                        R = (r - 1) * NPAIR
                        with act.Fori(0, NPAIR) as e:
                            act.wait_ge(o["pe"], e * 4 + (4 * R + 1))
                            af(xgT[0][:, 0:4, :], pb[0][:, :].rearrange("p (k t) -> p k t", k=4), ACT.Copy)\
                                .then_inc(o["act"], 1)
                            act.wait_ge(o["pe"], e * 4 + (4 * R + 2))
                            af(sil[0], pb[2][:, 0:FE], ACT.Silu).then_inc(o["act"], 1)
                            act.wait_ge(o["pe"], e * 4 + (4 * R + 3))
                            af(actT[0], pb[4][:, 0:FE].rearrange("p (j t) -> p j t", j=2), ACT.Copy)\
                                .then_inc(o["act"], 1)
                            act.wait_ge(o["pe"], e * 4 + (4 * R + 4))
                            af(yt[0][:, 0:U], pb[5][:, :], ACT.Copy).then_inc(o["act"], 1)

            moe(0)
            norm_stats(2)
            hT_copies(2)
            for m in range(0, 14, 2):
                act.wait_ge(a_pm, m + 1)
                if m < 10:
                    af(QT[:, m, :] if m < 8 else KTT[:, m - 8, :], pb[m % 4][:, :], ACT.Copy).then_inc(a_pca, 1)
                else:
                    af(V[:, m - 10, :], pb[m % 4][:, 0:256], ACT.Copy).then_inc(a_pca, 1)

            def exps(n):
                act.wait_ge(a_nb, n + 1)
                for hh in range(2):
                    af(SC[n % 4][:, hh, :], SC[n % 4][:, hh, :], ACT.Exp, bias=nb[:, n % 8, hh:hh + 1],
                       scale=HD ** -0.5, accum_out=den[:, n % 8, hh:hh + 1])
                af(es[:, n % 8, :], es[:, n % 8, :], ACT.Exp).then_inc(a_e, 1)

            def probsT_copy(n):
                u = n // 2
                act.wait_ge(a_pt, n + 1)
                if u >= 2:
                    act.wait_ge(a_o, u - 1)
                af(PT[u % 2][:, :, 2 * (n % 2):2 * (n % 2) + 2, :],
                   pb[2 + n % 2][:, :].rearrange("p (j h q) -> p j h q", j=2, h=2), ACT.Copy).then_inc(a_pc, 1)

            def o_copy(u):
                b, qb, g = u // 8, (u // 4) % 2, u % 4
                rows = slice(64 * (g % 2), 64 * (g % 2) + 64)
                tok0 = b * SEQ + qb * P
                act.wait_ge(a_o, u + 1)
                af(OT[rows, 4 * (g // 2):4 * (g // 2) + 4, tok0:tok0 + P],
                   pb[4 + u % 2][rows, :].rearrange("p (h q) -> p h q", h=4), ACT.Copy).then_inc(a_oc, 1)

            NU = 32
            for n in range(NU + 4):
                if n < NU:
                    exps(n)
                if 2 <= n < NU + 2:
                    probsT_copy(n - 2)
                if n >= 4 and n % 2 == 1:
                    o_copy((n - 5) // 2) if n >= 5 else None
            moe(1)
            norm_stats(4)

        @block.vector
        def _(dve):
            v = nc.vector
            dc = [0]

            def link(i):
                dc[0] += 1
                i.then_inc(dch, 1)
                dve.wait_ge(dch, dc[0])

            def bc(ap, shape, axis):
                return ap.unsqueeze(axis).broadcast_to(shape)

            def norm_apply(n):
                dve.wait_ge(s_rstd, n + 1)
                dve.wait_ge(ld_gain, 16 * (n + 1))
                for t in range(NT):
                    v.scalar_tensor_tensor(HTOK[n][:, t, :], X[:, t, :], rstd[:, n, t:t + 1], GAIN[n],
                                           ALU.mult, ALU.mult).then_inc(s_h, 1)

            def hT_copies(n):
                for k in range(1, KT, 2):
                    dve.wait_ge(s_tr, KT * n + k + 1)
                    v.tensor_copy(HT[:, k, :], pb[1][:, :]).then_inc(s_hTd, 1)

            def reduce_angle(j):
                C = 2 * math.pi
                hi = float(np.float32(6.28125))
                lo = C - hi
                magic = 12582912.0
                z, m, x = fz[:, 1, :], fz[:, 2, :], pb[7][0:64, 0:SEQ]
                if j == 0:
                    dve.wait_ge(ld_p, 48)
                dve.wait_ge(f_ps, j + 1)
                link(v.tensor_scalar(z, x, parm[0:64, PA_B + j:PA_B + j + 1], parm[0:64, PA_FREQ + j:PA_FREQ + j + 1],
                                     ALU.add, ALU.mult))
                link(v.tensor_scalar(m, z, 1.0 / C, magic, ALU.mult, ALU.add))
                link(v.tensor_scalar(m, m, magic, None, ALU.subtract))
                link(v.scalar_tensor_tensor(z, m, -hi, z, ALU.mult, ALU.add))
                link(v.scalar_tensor_tensor(z, m, -lo, z, ALU.mult, ALU.add))
                lim = 3.1415925
                v.tensor_scalar(z, z, lim, -lim, ALU.min, ALU.max).then_inc(f_red, 1)

            reduce_angle(0)
            norm_apply(0)
            reduce_angle(1)
            reduce_angle(2)
            hT_copies(0)
            for n in range(8):
                o, i, s = n // 4, (n // 2) % 2, n % 2
                dve.wait_ge(f_h4, n + 1)
                k = v.tensor_tensor(RF[:, i, s, :], pb[2 + n % 4][:, :], window[:, i, :], ALU.mult)
                if s == 1:
                    link(k)
                    v.tensor_tensor(HP[:, o, i, 0, :], RF[:, i, 0, :], RF[:, i, 1, :], ALU.add)
                    v.tensor_tensor(HP[:, o, i, 1, :], RF[:, i, 0, :], RF[:, i, 1, :], ALU.subtract).then_inc(f_ht, 1)
            for m in range(24):
                base = hx[:, m, :] if m < 12 else qkvz[:, m - 12, :]
                w = PA_CONVB + 3 * m if m < 12 else PA_CONVA + 3 * (m - 12)
                dst = base.rearrange("p (b t) -> p b t", b=NSEQ)
                src = pb[m % 4][:, :].rearrange("p (b t) -> p b t", b=NSEQ)
                dve.wait_ge(s_cva, m + 1)
                v.scalar_tensor_tensor(dst[:, :, 1:SEQ], src[:, :, 0:SEQ - 1], parm[:, w:w + 1], dst[:, :, 1:SEQ],
                                       ALU.mult, ALU.add).then_inc(s_cvd, 1)
                dve.wait_ge(s_cvd, 2 * m + 1)
                v.scalar_tensor_tensor(dst[:, :, 0:SEQ - 1], src[:, :, 1:SEQ], parm[:, w + 2:w + 3],
                                       dst[:, :, 0:SEQ - 1], ALU.mult, ALU.add).then_inc(s_cvd, 1)
            dve.wait_ge(s_ab, 1)
            v.tensor_copy(ab[:, :, :], pb[4][:, 0:64].rearrange("p (t n) -> p t n", t=NT)).then_inc(s_abc, 1)
            dve.wait_ge(s_abc, 1)
            dtb = bc(parm[:, PA_DTB:PA_DTB + 8], [P, NT, 8], 1)
            link(v.tensor_tensor(gt[:, GG, :, :], ab[:, :, 8:16], dtb, ALU.add))
            v.scalar_tensor_tensor(gt[:, KDS, :, :], gt[:, GG, :, :], -1.0, gt[:, GG, :, :],
                                   ALU.mult, ALU.min).then_inc(s_abc, 1)
            dve.wait_ge(g_gx, 1)
            link(v.tensor_scalar(gt[:, GTEMP, :, :], gt[:, GTEMP, :, :], 1.0, None, ALU.add))
            link(v.reciprocal(gt[:, BETA, :, :], gt[:, GTEMP, :, :]))
            v.tensor_scalar(gt[:, GTEMP, :, :], gt[:, BETA, :, :], -1.0, None, ALU.mult)
            link(v.scalar_tensor_tensor(gt[:, GG, :, :], gt[:, GG, :, :], 0.0, gt[:, KDS, :, :], ALU.max, ALU.add))
            link(v.tensor_tensor(gt[:, GG, :, :], gt[:, GG, :, :], bc(gt[:, KBS, 0, :], [P, NT, 8], 1), ALU.mult))
            v.tensor_scalar(gt[:, GG, :, :], gt[:, GG, :, :], -1.0, None, ALU.mult).then_inc(g_gate, 1)

            for o in range(2):
                for u in range(4):
                    b, pair = u // 2, u % 2
                    re, im = pb[4 + 2 * (u % 2)][:, :], pb[5 + 2 * (u % 2)][:, :]
                    A, Bk, C = Kf[:, o, pair, :], Kf[:, o, 2 + pair, :], Kf[:, o, 4 if pair == 0 else 1, :]
                    dve.wait_ge(y_u, 4 * o + u + 1)
                    if 4 * o + u >= 2:
                        dve.wait_ge(y_y, 2 * (4 * o + u - 1))
                    T = TP[:, u % 2, :, :]
                    v.tensor_tensor(T[:, 0, :], re, A, ALU.mult).then_inc(y_p, 1)
                    v.tensor_tensor(T[:, 1, :], im, Bk, ALU.mult).then_inc(y_p, 1)
                    v.tensor_tensor(T[:, 2, :], re, Bk, ALU.mult).then_inc(y_p, 1)
                    v.tensor_tensor(T[:, 3, :], im, C, ALU.mult).then_inc(y_p, 1)
                for c in range(4):
                    src = hx[:, 8 + c, :] if o == 0 else Z1[:, c, :]
                    n = 4 * o + c
                    dve.wait_ge(y_i, n + 1)
                    if n >= 2:
                        dve.wait_ge(y_o, n - 1)
                    w = PA_DB + 4 * o + c
                    v.scalar_tensor_tensor(ZT[:, c % 2, :], src, parm[:, w:w + 1], pb[c][:, :],
                                           ALU.mult, ALU.add).then_inc(y_z, 1)

            dve.wait_ge(g_cum, 1)
            for d in range(2):
                i = v.tensor_copy(gt[:, GC, :, 4 * d:4 * d + 4], pb[4][:, 16 * d:16 * d + 16].rearrange("p (t h) -> p t h", t=NT))
            link(i)
            v.tensor_tensor(gt[:, KDS, :, :], pb[4][:, 32:64].rearrange("p (t n) -> p t n", t=NT), gt[:, GC, :, :],
                            ALU.subtract).then_inc(g_gc, 1)
            dve.wait_ge(g_gx, 2)
            v.tensor_tensor(gt[:, KBS, :, :], gt[:, KBS, :, :], gt[:, BETA, :, :], ALU.mult).then_inc(g_gate, 1)
            for n in range(8):
                dve.wait_ge(n_rs, n + 1)
                v.scalar_tensor_tensor(qkvz[:, n, :], qkvz[:, n, :], float(P) ** -0.5 if n < 4 else 1.0, rsn[:, n % 4, :],
                                       ALU.mult, ALU.mult).then_inc(n_n, 1)

            S4 = [P, HEADS, P]
            for b in range(NSEQ):
                if b == 1:
                    dve.wait_ge(c_o, 8)
                    dve.wait_ge(c_s, 6)
                for q in range(4):
                    n = 4 * b + q
                    t, d = 2 * b + q // 2, q % 2
                    gcol = gt[:, GC, t, 4 * d:4 * d + 4]
                    dve.wait_ge(m_gb, n + 1)
                    if n:
                        dve.wait_ge(m_q, n)
                    link(v.tensor_tensor(DT, h4(pb[n % 2][:, :]), bc(gcol, S4, 2), ALU.subtract))
                    v.tensor_scalar(DA, DT, 0.0, None, ALU.max)
                    v.tensor_scalar(DT, DT, 0.0, None, ALU.min).then_inc(m_d, 1)
                    dve.wait_ge(m_e, 3 * n + 3)
                    dve.wait_ge(m_kk, 2 * b + q // 2 + 1)
                    link(v.tensor_tensor(AA[q], h4(pb[2][:, :]), DA, ALU.mult))
                    v.tensor_tensor(AA[q], AA[q], bc(gt[:, GTEMP, t, 4 * d:4 * d + 4], S4, 2), ALU.mult).then_inc(m_a, 1)
                    dve.wait_ge(m_qk, 2 * b + q // 2 + 1)
                    v.tensor_tensor(QK[q], h4(pb[3][:, :]), DT, ALU.mult).then_inc(m_q, 1)
                eye = bc(ident, S4, 1)
                for q in range(4):
                    n = 4 * b + q
                    dve.wait_ge(m_m, n + 1)
                    v.tensor_tensor(XX[q], AL[q], eye, ALU.add).then_inc(m_x0, 1)
                    dve.wait_ge(m_mt, n + 1)
                    v.tensor_tensor(XT[q], h4(pb[4 + q % 2][:, :]), eye, ALU.add).then_inc(m_x0, 1)
                for lv in range(1, 6):
                    for q in range(4):
                        n2 = 36 * b + 8 * (lv - 1) + (2 * q if lv < 5 else q)
                        if lv < 5:
                            dve.wait_ge(m_xp, n2 + 2)
                            v.tensor_tensor(XX[q], XX[q], h4(pb[2 + n2 % 4][:, :]), ALU.add).then_inc(m_xc, 1)
                            n2 += 1
                        dve.wait_ge(m_xp, n2 + 1)
                        v.tensor_tensor(XT[q], XT[q], h4(pb[2 + n2 % 4][:, :]), ALU.add).then_inc(m_xc, 1)
                for s in range(4):
                    for d in range(2):
                        g = 8 * b + 2 * s + d
                        c = s if d == 0 else 3 - s
                        q, half = 2 * (c // 2) + d, c % 2
                        rows = slice(CHUNK * half, CHUNK * half + CHUNK)
                        if g >= 2:
                            dve.wait_ge(c_o, g - 1)
                            if s > 0:
                                dve.wait_ge(c_s, 6 * b + 2 * (s - 1) + d + 1)
                        if s == 0:
                            dve.wait_ge(m_uwc, 8 * b + 2 * q + 1)
                            v.tensor_copy(VN[d][rows, :, :], UU[q][rows, :, :]).then_inc(c_v, 1)
                        else:
                            dve.wait_ge(c_w, 6 * b + 2 * (s - 1) + d + 1)
                            v.tensor_tensor(VN[d][rows, :, :], UU[q][rows, :, :], h4(pb[4 + d][rows, :]),
                                            ALU.subtract).then_inc(c_v, 1)
                    for d in range(2):
                        g = 8 * b + 2 * s + d
                        c = s if d == 0 else 3 - s
                        q, half = 2 * (c // 2) + d, c % 2
                        if s < 3:
                            dve.wait_ge(c_s, 6 * b + 2 * s + d + 1)
                            new = ST[d][(s + 1) % 2]
                            if s == 0:
                                v.tensor_copy(new, h4(pb[2 + d][:, :])).then_inc(c_sc, 1)
                            else:
                                for h in range(HEADS):
                                    i = v.scalar_tensor_tensor(new[:, h, :], ST[d][s % 2][:, h, :],
                                                               gls[:, 4 * b + q, h, half:half + 1],
                                                               pb[2 + d][:, h * P:(h + 1) * P], ALU.mult, ALU.add)
                                i.then_inc(c_sc, 1)
                        dve.wait_ge(c_o, g + 1)
                        dst = OA[:, :, b * SEQ + c * CHUNK:b * SEQ + (c + 1) * CHUNK]
                        src = pb[6 + d][:, 0:HEADS * CHUNK].rearrange("p (h c) -> p h c", h=HEADS)
                        if s < 2:
                            v.tensor_copy(dst, src).then_inc(c_oc, 1)
                        else:
                            v.tensor_tensor(dst, dst, src, ALU.add).then_inc(c_oc, 1)
            for h in range(HEADS):
                dve.wait_ge(n_rs, 8 + h + 1)
                link(v.scalar_tensor_tensor(OA[:, h, :], OA[:, h, :], parm[:, PA_ON:PA_ON + 1], ors[:, h, :],
                                            ALU.mult, ALU.mult))
                v.tensor_tensor(OA[:, h, :], OA[:, h, :], zT[:, h, :], ALU.mult).then_inc(o_n, 1)

            def out_proj(L):
                for n in range(8):
                    t, c = n // 2, n % 2
                    dst = X[:, t, c * U:(c + 1) * U]
                    dve.wait_ge(p_o, 8 * L + n + 1)
                    v.tensor_tensor(dst, dst, pb[2 + n % 2][:, :], ALU.add).then_inc(s_x, 1)

            def moe(L):
                n = 2 * L + 1
                dve.wait_ge(s_x, X_DONE[n])
                norm_apply(n)
                hT_copies(n)
                S32 = [P, NT, NEXP]
                link(v.memset(gpad, -3.0e38))
                dve.wait_ge(r_lg, L + 1)
                lps = pb[2][:, 0:NT * 36].rearrange("p (t n) -> p t n", t=NT)
                v.tensor_copy(lg, lps)
                link(v.tensor_copy(gpad[:, :, 0:NGRP], lps[:, :, 0:NGRP]))
                for t in range(NT):
                    i = v.max(top_g[:, t, :], gpad[:, t, :])
                link(i)
                for t in range(NT):
                    i = v.max_index(idx_g[:, t, :], top_g[:, t, :], gpad[:, t, :])
                link(i)
                v.tensor_tensor(gexp, lg[:, :, 0:NGRP], top_g[:, :, 0:1].broadcast_to([P, NT, NGRP]), ALU.subtract)
                link(v.tensor_copy(fi[:, :, 0:1], idx_g[:, :, 0:1]))
                link(v.tensor_tensor(oh[:, 3, :, :], bc(e_grp, S32, 1), fi[:, :, 0:1].broadcast_to(S32), ALU.is_equal))
                v.tensor_scalar(emsk, oh[:, 3, :, :], -1.0, -NEG, ALU.add, ALU.mult)
                link(v.tensor_tensor(oh[:, 0, :, :], oh[:, 3, :, :], lg[:, :, NGRP:NGRP + NEXP], ALU.mult))
                link(v.tensor_tensor(emsk, emsk, oh[:, 0, :, :], ALU.add))
                for t in range(NT):
                    i = v.max(top_e[:, t, :], emsk[:, t, :])
                link(i)
                for t in range(NT):
                    i = v.max_index(idx_e[:, t, :], top_e[:, t, :], emsk[:, t, :])
                link(i)
                v.tensor_tensor(coef[:, 0, :].unsqueeze(2), top_e[:, :, 1:2], top_e[:, :, 0:1], ALU.subtract).then_inc(r_gs, 1)
                link(v.tensor_copy(fi[:, :, 1:3], idx_e[:, :, 0:2]))
                for k in range(2):
                    i = v.tensor_tensor(oh[:, k, :, :], bc(iota_e, S32, 1), fi[:, :, 1 + k:2 + k].broadcast_to(S32), ALU.is_equal)
                link(i)
                v.tensor_tensor(oh[:, 2, :, :], oh[:, 0, :, :], oh[:, 1, :, :], ALU.add).then_inc(r_oh, 1)
                dve.wait_ge(r_lc, L + 1)
                link(v.tensor_reduce(coef[:, 1, :], gexp, AXX, ALU.add))
                link(v.scalar_tensor_tensor(coef[:, 2, :], coef[:, 0, :], 1.0, coef[:, 1, :], ALU.add, ALU.mult))
                link(v.reciprocal(coef[:, 3, :], coef[:, 2, :]))
                v.tensor_tensor(coef[:, 4, :], coef[:, 3, :], coef[:, 0, :], ALU.mult)
                dve.wait_ge(r_rk, L + 1)
                rps = pb[3][:, 0:NT * NEXP].rearrange("p (t n) -> p t n", t=NT)
                link(v.tensor_reduce(cmax[:, :], pb[3][:, NT * NEXP:(NT + 1) * NEXP], AXX, ALU.max))
                v.tensor_copy(flag[:, :], cmax[:, :])
                for k in range(2):
                    link(v.tensor_tensor(emsk, oh[:, k, :, :], rps, ALU.mult))
                    link(v.tensor_reduce(rowf[:, k, :], emsk, AXX, ALU.add))
                link(v.tensor_scalar(rtmp[:, 0:2, :], fi[:, :, 1:3].rearrange("p t k -> p k t"), float(CAP), None, ALU.mult))
                link(v.tensor_tensor(rtmp[:, 0:2, :], rtmp[:, 0:2, :], rowf[:, :, :], ALU.add))
                for r in range(1, ROUNDS):
                    link(v.tensor_scalar(rtmp[:, 2:4, :], rowf[:, :, :], float(CAP * r), float((NEXP - 1) * CAP), ALU.is_ge, ALU.mult))
                    link(v.tensor_tensor(rtmp[:, 0:2, :], rtmp[:, 0:2, :], rtmp[:, 2:4, :], ALU.add))
                v.tensor_copy(rowi[:, :, :], rtmp[:, 0:2, :]).then_inc(r_row, 1)
                dve.wait_ge(r_tt, L + 1)
                link(v.tensor_copy(tab_val, pb[4][:, 0:P]))
                v.tensor_copy(sca_i, tab_val)
                link(v.tensor_scalar(tab_gat, tab_val, float(TOK), -float(TOK), ALU.is_ge, ALU.mult))
                link(v.tensor_tensor(tab_gat, tab_gat, tab_val, ALU.add))
                v.tensor_copy(gat_i, tab_gat).then_inc(r_fl, 1)
                B = NPAIR * L

                def xT_copy(e, j):
                    dve.wait_ge(e_T, e + (B + 1))
                    v.tensor_copy(xgT[j % 2][:, 4:8, :], pb[1][:, :].rearrange("p (k t) -> p k t", k=4)).then_inc(e_xd, 1)

                def product(e, j):
                    dve.wait_ge(e_si, e + (B + 1))
                    v.tensor_tensor(act_h[j % 2], sil[j % 2], pb[2 + j % 2][:, FE:2 * FE], ALU.mult).then_inc(e_ac, 1)

                def y_copy(e, j):
                    dve.wait_ge(e_D, e + (B + 1))
                    if not (isinstance(e, int) and e + B < 2):
                        dve.wait_ge(e_sc[j % 2], e * 8 + (8 * B - 8 * (j % 2)))
                    v.tensor_copy(yt[j % 2][:, U:2 * U], pb[6][:, :]).then_inc(e_yd, 1)

                def four(i, first=False, last=False):
                    for j in range(4):
                        e = i * 4 + j
                        product(e, j)
                        if not (last and j == 3):
                            xT_copy(e + 1, (j + 1) % 4)
                        if not (first and j == 0):
                            y_copy(e - 1, (j - 1) % 4)

                xT_copy(0, 0)
                four(0, first=True)
                with dve.Fori(1, NPAIR // 4 - 1) as i:
                    four(i)
                four(NPAIR // 4 - 1, last=True)
                y_copy(NPAIR - 1, 3)

                o = ov[L]
                more = nc.vector.value_load(flag[0:1, 0:1], min_val=0, max_val=TOK)
                with dve.If(more > CAP):
                    for s in range(2):
                        dve.wait_ge(e_sc[s], 16 * (NPAIR // 2) * (L + 1))
                    for r in range(1, ROUNDS):
                        R = (r - 1) * NPAIR
                        with dve.Fori(0, NPAIR) as e:
                            dve.wait_ge(o["pe"], e * 4 + (4 * R + 1))
                            v.tensor_copy(xgT[0][:, 4:8, :], pb[1][:, :].rearrange("p (k t) -> p k t", k=4))\
                                .then_inc(o["dve"], 1)
                            dve.wait_ge(o["act"], e * 4 + (4 * R + 2))
                            v.tensor_tensor(act_h[0], sil[0], pb[2][:, FE:2 * FE], ALU.mult).then_inc(o["dve"], 1)
                            dve.wait_ge(o["pe"], e * 4 + (4 * R + 4))
                            v.tensor_copy(yt[0][:, U:2 * U], pb[6][:, :]).then_inc(o["dve"], 1)

                for t in range(NT):
                    for k in range(2):
                        dve.wait_ge(ld_yk[t], 32 * (L + 1))
                        if k:
                            dve.wait_ge(s_x, X_DONE[n] + 2 * t + 1)
                        v.scalar_tensor_tensor(X[:, t, :], YK[:, k * NT + t, :], coef[:, 3 + k, t:t + 1], X[:, t, :],
                                               ALU.mult, ALU.add).then_inc(s_x, 1)

            out_proj(0)
            moe(0)
            norm_apply(2)
            hT_copies(2)
            link(v.tensor_scalar(sink8[:, :], parm[:, PA_SINK:PA_SINK + HQ], float(HD) ** 0.5, None, ALU.mult))
            for m in range(1, 14, 2):
                dve.wait_ge(a_pm, m + 1)
                if m < 10:
                    v.tensor_copy(QT[:, m, :] if m < 8 else KTT[:, m - 8, :], pb[m % 4][:, :]).then_inc(a_pcd, 1)
                else:
                    v.tensor_copy(V[:, m - 10, :], pb[m % 4][:, 0:256]).then_inc(a_pcd, 1)
            dve.wait_ge(ld_dist, 16)
            NU = 32

            def bias_and_max(n):
                qb, g, pr = (n // 8) % 2, (n // 2) % 4, n % 2
                head = 4 * g + 2 * pr
                sc, r = SC[n % 4], n % 8
                dve.wait_ge(a_s, n + 1)
                if n >= 4:
                    dve.wait_ge(a_pt, n - 3)
                for hh in range(2):
                    v.scalar_tensor_tensor(sc[:, hh, :], negd[:, qb, :], slopes(head + hh) * HD ** 0.5,
                                           pb[n % 2][:, hh * SEQ:(hh + 1) * SEQ], ALU.mult, ALU.add).then_inc(a_sc, 1)
                dve.wait_ge(a_sc, 2 * (n + 1))
                link(v.tensor_reduce(mx[:, r, :], sc, AXX, ALU.max))
                link(v.tensor_tensor(mx[:, r, :], mx[:, r, :], sink8[:, head:head + 2], ALU.max))
                link(v.tensor_scalar(nb[:, r, :], mx[:, r, :], -(HD ** -0.5), None, ALU.mult))
                v.scalar_tensor_tensor(es[:, r, :], sink8[:, head:head + 2], HD ** -0.5, nb[:, r, :],
                                       ALU.mult, ALU.add).then_inc(a_nb, 1)

            def denominators(n):
                r = n % 8
                dve.wait_ge(a_e, n + 1)
                link(v.tensor_tensor(den[:, r, :], den[:, r, :], es[:, r, :], ALU.add))
                v.reciprocal(den[:, r, :], den[:, r, :]).then_inc(a_rd, 1)
            for n in range(NU + 1):
                if n < NU:
                    bias_and_max(n)
                if n:
                    denominators(n - 1)
            out_proj(1)
            moe(1)
            norm_apply(4)

        @block.gpsimd
        def _(pool):
            g_ = nc.gpsimd
            S4 = [P, HEADS, P]

            def bc(ap, shape, axis):
                return ap.unsqueeze(axis).broadcast_to(shape)

            def count(value):
                return value if isinstance(value, int) else pool.to_reg(value)
            g_.memset(norow, NOROW).then_inc(pch, 1)
            last_token, last_row = pool.to_reg(TOK - 1), pool.to_reg(2 * TOK - 1)
            for o in range(2):
                for u in range(4):
                    b, pair = u // 2, u % 2
                    T = TP[:, u % 2, :, :]
                    pool.wait_ge(y_p, 16 * o + 4 * u + 2)
                    if o == 1 and u == 0:
                        pool.wait_ge(y_i, 4)
                    g_.tensor_tensor(YF[:, b, pair, :], T[:, 0, :], T[:, 1, :], ALU.subtract).then_inc(y_y, 1)
                    pool.wait_ge(y_p, 16 * o + 4 * u + 4)
                    g_.tensor_tensor(YF[:, b, pair + 2, :], T[:, 2, :], T[:, 3, :], ALU.add).then_inc(y_y, 1)
                for c in range(4):
                    pool.wait_ge(y_z, 4 * o + c + 1)
                    dst = Z1[:, c, :] if o == 0 else OB[:, c, :]
                    g_.tensor_tensor(dst, ZT[:, c % 2, :], hx[:, 4 * o + c, :], ALU.mult).then_inc(y_o, 1)
            pool.wait_ge(y_o, 8)
            pool.wait_ge(g_gate, 2)

            def decay_rows(n):
                t, d = n // 2, n % 2
                if n >= 2:
                    pool.wait_ge(m_gb, n - 1)
                g_.tensor_tensor(RG[n % 2], bc(incl[d], S4, 1), bc(gt[:, GG, t, 4 * d:4 * d + 4], S4, 2),
                                 ALU.mult).then_inc(m_r, 1)
            for b in range(NSEQ):
                for q in range(2):
                    decay_rows(4 * b + q)
                if b == 1:
                    pool.wait_ge(c_o, 8)
                    pool.wait_ge(c_s, 6)
                pool.wait_ge(t_kvc, 8)
                for q in range(4):
                    n = 4 * b + q
                    t, d = n // 2, n % 2
                    cols = slice(4 * d, 4 * d + 4)
                    if q < 2:
                        decay_rows(n + 2)
                    pool.wait_ge(m_a, n + 1)
                    g_.tensor_tensor(AL[q], AA[q], bc(mask(6 * d), S4, 1), ALU.mult).then_inc(m_m, 1)
                    pool.wait_ge(m_q, n + 1)
                    g_.tensor_tensor(QK[q], QK[q], bc(incl[d], S4, 1), ALU.mult).then_inc(m_qm, 1)
                for lv in range(1, 6):
                    for q in range(4):
                        n = 4 * b + q
                        t, d = n // 2, n % 2
                        cols = slice(4 * d, 4 * d + 4)
                        g = 20 * b + 4 * (lv - 1) + q
                        if lv == 1:
                            pool.wait_ge(m_x0, 2 * (n + 1))
                            pool.wait_ge(m_mt, n + 1)
                        else:
                            pool.wait_ge(m_y, g - 3)
                        g_.tensor_tensor(AL[q], AA[q], bc(mask(6 * d + lv), S4, 1), ALU.mult).then_inc(m_al, 1)
                        if lv == 1:
                            g_.tensor_tensor(KBG[q], ktok[:, t, :, :], bc(gt[:, KBS, t, cols], S4, 2), ALU.mult).then_inc(m_s, 1)
                        if lv == 2:
                            g_.tensor_tensor(VB[q], vtok[:, t, :, :], bc(gt[:, BETA, t, cols], S4, 2), ALU.mult).then_inc(m_s, 1)
                        if lv == 3:
                            g_.tensor_tensor(KD[q], ktok[:, t, :, :], bc(gt[:, KDS, t, cols], S4, 2), ALU.mult).then_inc(m_s, 1)
                        if lv == 4:
                            pool.wait_ge(m_gl, n + 1)
                            g_.tensor_tensor(QD[q], QD[q], qT[:, :, t * P:(t + 1) * P], ALU.mult).then_inc(m_qd, 1)

            def moe(L):
                B = NPAIR * L
                table = tab_dram[L][:, :].rearrange("a (b o) -> (a b) o", o=1)
                pool.wait_ge(tab_init, 32)
                pool.wait_ge(r_row, L + 1)
                for k in range(2):
                    for t in range(NT):
                        g_.indirect_dma_start(table, bass.IndirectOffsetOnAxis(rowi[:, k, t:t + 1], 0),
                                              tokid[:, k * NT + t:k * NT + t + 1], None).then_inc(r_sc, 16)
                pool.wait_ge(r_hd, 16 * NT * (L + 1))
                pool.wait_ge(r_fl, L + 1)

                def gather(e, j, idx):
                    g_.indirect_dma_start(xg[j], None, h_dram[L][:, :], bass.IndirectOffsetOnAxis(idx, 0),
                                          bounds_check=last_token, oob_is_err=False).then_inc(e_xg[j], 16)

                def scatter(e, j, idx):
                    g_.indirect_dma_start(yk_dram[L][:, :], bass.IndirectOffsetOnAxis(idx, 0), yt[j % 2], None,
                                          bounds_check=last_row, oob_is_err=False).then_inc(e_sc[j % 2], 16)

                def four(i, last=False):
                    for j in range(4):
                        e = i * 4 + j
                        col = e if isinstance(e, int) else pool.snap(e)
                        if not last:
                            col4 = e + 4 if isinstance(e, int) else pool.snap(e + 4)
                            pool.wait_ge(e_T, e + (B + 1))
                            g_.tensor_copy(gcur[:, j:j + 1], gat_i[:, bass.ds(col4, 1)]).then_inc(e_cg, 1)
                            copied = count(e + (B + 5))
                            pool.wait_ge(r_fl, L + 1)
                            pool.wait_ge(e_cg, copied)
                            gather(e + 4, j, gcur[:, j:j + 1])
                        pool.wait_ge(e_ya, e + (B + 1))
                        pool.wait_ge(e_yd, e + (B + 1))
                        g_.tensor_copy(scur[:, j:j + 1], sca_i[:, bass.ds(col, 1)]).then_inc(e_cs, 1)
                        copied = count(e + (B + 1))
                        pool.wait_ge(r_fl, L + 1)
                        pool.wait_ge(e_cs, copied)
                        scatter(e, j, scur[:, j:j + 1])

                for j in range(4):
                    g_.tensor_copy(gcur[:, j:j + 1], gat_i[:, j:j + 1]).then_inc(e_cg, 1)
                    pool.wait_ge(e_cg, B + j + 1)
                    gather(j, j, gcur[:, j:j + 1])
                with pool.Fori(0, NPAIR // 4 - 1) as i:
                    four(i)
                four(NPAIR // 4 - 1, last=True)

                o = ov[L]
                more = g_.value_load(flag[0:1, 0:1], min_val=0, max_val=TOK)
                with pool.If(more > CAP):
                    for s in range(2):
                        pool.wait_ge(e_sc[s], 16 * (NPAIR // 2) * (L + 1))
                    for r in range(1, ROUNDS):
                        R = (r - 1) * NPAIR
                        with pool.Fori(0, NPAIR) as e:
                            col = pool.snap(e + r * NPAIR)
                            g_.tensor_copy(gcur[:, 0:1], gat_i[:, bass.ds(col, 1)]).then_inc(o["ids"], 1)
                            g_.tensor_copy(scur[:, 0:1], sca_i[:, bass.ds(col, 1)]).then_inc(o["ids"], 1)
                            copied = count(e * 2 + (2 * R + 2))
                            pool.wait_ge(r_fl, L + 1)
                            pool.wait_ge(o["ids"], copied)
                            g_.indirect_dma_start(xg[0], None, h_dram[L][:, :],
                                                  bass.IndirectOffsetOnAxis(gcur[:, 0:1], 0), bounds_check=last_token,
                                                  oob_is_err=False).then_inc(o["g"], 16)
                            y_act, y_dve = count(e * 4 + (4 * R + 4)), count(e * 3 + (3 * R + 3))
                            pool.wait_ge(r_fl, L + 1)
                            pool.wait_ge(o["act"], y_act)
                            pool.wait_ge(o["dve"], y_dve)
                            g_.indirect_dma_start(yk_dram[L][:, :], bass.IndirectOffsetOnAxis(scur[:, 0:1], 0), yt[0],
                                                  None, bounds_check=last_row, oob_is_err=False).then_inc(o["sc"], 16)
                            pool.wait_ge(o["sc"], e * 16 + 16 * (R + 1))

            moe(0)
            for n in range(32):
                pool.wait_ge(a_rd, n + 1)
                g_.tensor_tensor(SC[n % 4], SC[n % 4], bc(den[:, n % 8, :], [P, 2, SEQ], 2), ALU.mult).then_inc(a_p, 1)
            moe(1)


def kernel(**inputs):
    import numpy as _np
    import concourse.bacc as _bacc
    from concourse import mybir as _mybir
    from concourse.bass_utils import run_bass_kernel_spmd as _run

    a = {k: _np.asarray(v) for k, v in inputs.items()}
    cat, tile = _np.concatenate, _np.ascontiguousarray

    def k_major(w):
        return w.reshape(w.shape[0] // P, P, w.shape[1]).transpose(1, 0, 2)

    def chunks(w):
        return tile(w.reshape(KT, P, w.shape[1] // U, U).transpose(2, 1, 0, 3))

    win = a["ev_w_in"][0]
    w_in = chunks(cat([win[:, 2064:3600], win[:, 0:2048]], 1))
    w_ab = tile(k_major(win[:, 2048:2064]))
    order = [h for t in range(8) for h in ((t, 4 + t) if t < 4 else (4 + t, 8 + t))]
    wq = a["od_w_qkv"][0]
    q_cols = cat([wq[:, h * HD:(h + 1) * HD] for h in order], 1)
    w_qkv = chunks(cat([q_cols, wq[:, HQ * HD:]], 1))
    w_out1 = tile(k_major(cat([a["od_w_out"][0][h * HD:(h + 1) * HD] for h in order], 0)))
    w_out0 = tile(k_major(a["ev_w_out"][0]))
    w_router = tile(_np.stack([k_major(cat([a["moe_w_group"][L], a["moe_w_expert"][L]], 1)) for L in range(2)]))

    def rows(w, n):
        return w.reshape(2, NEXP, n, P, w.shape[-1]).transpose(0, 1, 3, 2, 4)
    gate_up = cat([rows(a["moe_w_gate"], KT), rows(a["moe_w_up"], KT)], 4)

    def pairs(w):
        return tile(w.reshape(2, NPAIR, 2, P, -1).transpose(0, 1, 3, 2, 4)).reshape(2, NPAIR, P, -1)
    w_gu, w_dn = pairs(gate_up), pairs(rows(a["moe_w_down"], FE // P))

    def on_partitions(w):
        return w.reshape(-1, P, w.shape[-1]).transpose(1, 0, 2).reshape(P, -1)

    def row(w):
        return _np.broadcast_to(w.reshape(1, -1), (P, w.size))

    def padded(w):
        return cat([w, _np.zeros((P - w.shape[0], w.shape[1]), w.dtype)], 0)
    db = a["hy_dbias"][0].reshape(2, 4, P).transpose(2, 0, 1).reshape(P, 8)
    params = cat([
        on_partitions(a["ev_conv_a"][0]), on_partitions(a["ev_conv_b"][0]), db, a["ev_onorm"][0].reshape(P, 1),
        padded(a["hy_freq"][0].T), padded(_np.stack([a["hy_b1"][0], a["hy_b2"][0], a["hy_b3"][0]], 1)),
        row(cat([a["ev_alog_f"][0], a["ev_alog_b"][0]])), row(cat([a["ev_dtb_f"][0], a["ev_dtb_b"][0]])),
        row(a["od_sinks"][0]), padded(a["hy_w1"][0]), padded(a["hy_w2"][0]), padded(a["hy_w3"][0]),
        padded(a["hy_w4"][0])], 1)
    assert params.shape == (P, NPAR)
    g5 = cat([_np.stack([a["norm_mix"][0], a["norm_ffn"][0], a["norm_mix"][1], a["norm_ffn"][1]]), a["norm_final"].reshape(1, D)], 0)
    gains = _np.broadcast_to(g5.reshape(5, 1, D), (5, P, D))
    x = cat([a["x_prompt"].reshape(SEQ, D), a["x_sample"].reshape(SEQ, D)], 0)

    nc = _bacc.Bacc("TRN2", target_bir_lowering=False, num_devices=1)
    arrays, args = {}, []
    for name, arr in (("x_in", x), ("gains", gains), ("pconst", persistent_constants()), ("mconst", mixer_constants()),
                      ("dconst", distance_constants()), ("params", params), ("w_in", w_in), ("w_ab", w_ab),
                      ("w_out0", w_out0), ("w_qkv", w_qkv), ("w_out1", w_out1), ("w_router", w_router),
                      ("w_gu", w_gu), ("w_dn", w_dn)):
        arr = tile(arr)
        arrays[f"{name}_dram"] = arr
        args.append(nc.dram_tensor(f"{name}_dram", arr.shape, _mybir.dt.from_np(arr.dtype), kind="ExternalInput").ap())
    y = nc.dram_tensor("y_dram", (TOK, D), _mybir.dt.float32, kind="ExternalOutput").ap()
    trunk_program(nc, *args, y)
    r = _run(nc, [arrays], core_ids=[0])
    got = r.results[0]["y_dram"].reshape(NSEQ, 1, SEQ, D)
    return got[0], got[1]
```

```python
import math
from contextlib import ExitStack

import numpy as np

import concourse.bass as bass
from concourse import mybir

D, SEQ, NSEQ = 1024, 256, 2
TOK = NSEQ * SEQ
P = 128
NT = TOK // P
KT = D // P
EPS = 1e-6
HEADS, CHUNK = 4, 64
B_WIDTH = 512
HQ, HD, WINDOW = 16, 64, 128
NEXP, NGRP, EPG, FE = 32, 4, 8, 256
CAP = P // 2
NPAIR = NEXP // 2
ROUNDS = TOK // CAP
NOROW = 4096.0
U = 512
NEG = -1e30
LEVELS = (1, 2, 4, 8, 16, 32)
GUW = KT * 2 * FE
DNW = (FE // P) * D


def persistent_constants():
    c = np.zeros((P, 1024), np.float32)
    r = np.arange(P)
    c[:, 0:128] = np.eye(P)
    c[:, 128:256] = r[:, None] < r[None, :]
    c[:, 256:384] = 1.0
    c[:, 384:416] = np.arange(NEXP)[None, :]
    for k in range(2):
        for t in range(NT):
            c[:, 416 + k * NT + t] = k * TOK + t * P + r
    c[:, 424] = EPS
    c[:, 492:492 + ROUNDS - 1] = CAP * np.arange(1, ROUNDS)[None, :]
    c[:, 512:640] = r[:, None] // CHUNK == r[None, :] // CHUNK
    c[0:CHUNK, 640:768] = 1.0
    c[CHUNK:P, 768:896] = 1.0
    c[:, 428:460] = np.arange(NEXP)[None, :] * CAP
    c[:, 460:492] = np.arange(NEXP)[None, :] // EPG
    return c


def mixer_constants():
    c = np.zeros((P, 12 * U), np.float32)
    r = np.arange(P)
    row, col = r[:, None], r[None, :]
    same = row // CHUNK == col // CHUNK

    def put_compact(n, m):
        c[0:CHUNK, n * CHUNK:(n + 1) * CHUNK] = m[0:CHUNK, 0:CHUNK]
        c[CHUNK:P, n * CHUNK:(n + 1) * CHUNK] = m[CHUNK:P, CHUNK:P]
    for n, s in enumerate(LEVELS):
        low = (row // (2 * s) == col // (2 * s)) & ((row // s) % 2 == 1) & ((col // s) % 2 == 0)
        c[:, n * P:(n + 1) * P] = low
        c[:, (6 + n) * P:(7 + n) * P] = low.T
    c[:, 12 * P:13 * P] = same & (row <= col)
    c[:, 13 * P:14 * P] = same & (row >= col)
    put_compact(28, same & (row <= col))
    put_compact(29, same & (row >= col))
    put_compact(30, row == col)
    t = np.arange(SEQ)
    f = np.arange(SEQ)
    w = 2.0 * np.pi * np.outer(t, f) / (2 * SEQ)
    alt = (-1.0) ** t
    cos, msin = np.cos(w), -np.sin(w)
    fu = np.concatenate([cos, msin], 1)
    fu[:, SEQ] = alt
    fs = msin.copy()
    fs[:, 0] = 0.0
    fc = cos[:, :P].copy()
    fc[:, 0] = alt
    g = np.concatenate([2 * cos.T, 2 * msin.T], 0) / (2 * SEQ)
    g[0] *= 0.5
    g[SEQ] = alt / (2 * SEQ)
    for k in range(4):
        c[:, 4 * U + k * SEQ:4 * U + (k + 1) * SEQ] = g[k * P:(k + 1) * P]
    for k in range(2):
        c[:, 6 * U + k * U:6 * U + (k + 1) * U] = fu[k * P:(k + 1) * P]
        c[:, 8 * U + k * SEQ:8 * U + (k + 1) * SEQ] = fs[k * P:(k + 1) * P]
        c[:, 9 * U + k * P:9 * U + (k + 1) * P] = fc[k * P:(k + 1) * P]
    tt = np.linspace(0.0, 1.0, SEQ)[:, None]
    wpos = (2.0 * np.pi / SEQ) * t[:, None]
    bands = np.linspace(1e-4, 15, 16)[None, :]
    feats = np.concatenate([tt, np.cos(bands * wpos), -np.sin(bands * wpos)], 1)
    c[0:33, 9 * U + 256:10 * U] = feats.T
    deltas = np.abs(np.linspace(math.log(1e-2) / 1.5, math.log(1e-2) / 0.3, B_WIDTH))
    win = np.exp(-tt * deltas[None, :])
    for k in range(2):
        c[:, (10 + k) * U:(11 + k) * U] = win[k * P:(k + 1) * P]
    return c


def distance_constants():
    i = np.arange(SEQ)[:, None]
    j = np.arange(SEQ)[None, :]
    d = np.where(np.abs(i - j) <= WINDOW, -np.abs(i - j).astype(np.float64), NEG)
    return d.reshape(2, P, SEQ).transpose(1, 0, 2).reshape(P, 2 * SEQ).astype(np.float32).copy()


PA_CONVA, PA_CONVB, PA_DB, PA_ON = 0, 36, 72, 80
PA_FREQ, PA_B = 81, 84
PA_ALOG, PA_DTB, PA_SINK = 87, 95, 103
PA_W1, PA_W2, PA_W3 = 119, 183, 247
PA_W4 = 311
NPAR = PA_W4 + 2048


def trunk_program(nc, x_in, gains, pconst, mconst, dconst, params, w_in, w_ab, w_out0, w_qkv, w_out1,
                  w_router, w_gu, w_dn, y_out):
    f32, u32 = mybir.dt.float32, mybir.dt.uint32
    ALU, ACT = mybir.AluOpType, mybir.ActivationFunctionType
    AXX = mybir.AxisListType.X
    ctx = ExitStack()
    with ctx:
        def sb(name, shape, dt=f32):
            return ctx.enter_context(nc.sbuf_tensor(name, shape, dt))

        def sem(name):
            return ctx.enter_context(nc.semaphore(name))

        def sems(name, n):
            return [sem(f"{name}{i}") for i in range(n)]

        h_dram = [nc.dram_tensor(f"h_dram{L}", (TOK, D), f32, kind="Internal").ap() for L in range(2)]
        yk_dram = [nc.dram_tensor(f"yk_dram{L}", (2 * TOK, D), f32, kind="Internal").ap() for L in range(2)]
        tab_dram = [nc.dram_tensor(f"tab_dram{L}", (P, P), f32, kind="Internal").ap() for L in range(2)]

        arena = sb("arena", [P, 100 * U])
        parm = sb("parm", [P, PA_W4])

        def units(a, n=1):
            return arena[:, a * U:(a + n) * U]

        X = units(0, 8).rearrange("p (t d) -> p t d", t=NT)
        HT = units(8, 8).rearrange("p (k t) -> p k t", k=KT)
        pc = units(16, 2)
        ident, strictU, ones = pc[:, 0:128], pc[:, 128:256], pc[:, 256:384]
        iota_e, tokid, eps_c = pc[:, 384:416], pc[:, 416:424], pc[:, 424:425]
        e_row, e_grp, round_row = pc[:, 428:460], pc[:, 460:492], pc[:, 492:492 + ROUNDS - 1]
        gu = [units(18 + 16 * s, 16).rearrange("p (h k n) -> p h k n", h=2, k=KT) for s in range(2)]
        dn = [units(50 + 8 * s, 8).rearrange("p (h f n) -> p h f n", h=2, f=FE // P) for s in range(2)]
        mc = units(18, 12)

        def mask(n):
            return mc[:, n * P:(n + 1) * P]
        incl = [mask(12), mask(13)]
        incl_c = [mc[:, (28 + d) * CHUNK:(29 + d) * CHUNK] for d in range(2)]
        eye_c = mc[:, 30 * CHUNK:31 * CHUNK]
        chunk_ones = pc[:, 512:640]
        half_ones = [pc[:, 640 + u * P:768 + u * P] for u in range(2)]
        G = mc[:, 4 * U:6 * U].rearrange("p (k t) -> p k t", k=4)
        F = mc[:, 6 * U:8 * U].rearrange("p (k f) -> p k f", k=2)
        Fs0 = mc[:, 8 * U:9 * U].rearrange("p (k f) -> p k f", k=2)
        Fc0 = mc[:, 9 * U:9 * U + 256].rearrange("p (k f) -> p k f", k=2)
        featsT = mc[0:33, 9 * U + 256:10 * U]
        window = mc[:, 10 * U:12 * U].rearrange("p (k f) -> p k f", k=2)
        wchunk = [units(30 + 8 * s, 8).rearrange("p (k n) -> p k n", k=KT) for s in range(3)]
        NCH = 7
        hx = units(54, 12).rearrange("p (m t) -> p m t", m=12)
        qT, kT, vT, zT = (units(66 + 4 * s, 4).rearrange("p (h t) -> p h t", h=HEADS) for s in range(4))
        qkvz = units(66, 16).rearrange("p (m t) -> p m t", m=16)
        Kf = units(82, 10).rearrange("p (o j c) -> p o j c", o=2, j=5)
        HP = units(92, 8).rearrange("p (o i s c) -> p o i s c", o=2, i=2, s=2)
        w4 = units(74, 4)[0:64, :]
        UT = units(30, 4).rearrange("p (b i c) -> p b i c", b=2, i=2)
        RF = units(66, 4).rearrange("p (j s c) -> p j s c", j=2, s=2)
        fz = units(70, 2)[0:64, 0:3 * SEQ].rearrange("p (j t) -> p j t", j=3)
        norow = units(72)[:, 0:P]
        YF = units(34, 8).rearrange("p (b f c) -> p b f c", b=2, f=4)
        TP = units(42, 8).rearrange("p (s j c) -> p s j c", s=2, j=4)
        Z1 = units(50, 4).rearrange("p (m t) -> p m t", m=4)
        OB = units(92, 4).rearrange("p (m t) -> p m t", m=4)
        ZT = units(96, 2).rearrange("p (s t) -> p s t", s=2)
        ktok = units(8, 4).rearrange("p (t h d) -> p t h d", t=NT, h=HEADS)
        vtok = units(12, 4).rearrange("p (t h d) -> p t h d", t=NT, h=HEADS)
        sqn = units(8, 8).rearrange("p (n t) -> p n t", n=8)
        rsn = units(42, 8).rearrange("p (n t) -> p n t", n=8)

        def h4(ap):
            return ap.rearrange("p (h c) -> p h c", h=HEADS)

        def c4(a):
            return h4(units(a)[:, 0:HEADS * CHUNK])
        QD, KD, UU, WT = ([h4(units(26 + 4 * n + q)) for q in range(4)] for n in range(4))
        QK = [c4(22 + q) for q in range(4)]
        XT, AA = ([c4(46 + 4 * n + q) for q in range(4)] for n in range(2))
        XX, AL, YY = ([h4(units(a + q)) for q in range(4)] for a in (42, 54, 58))
        YC = [h4(units(50 + q)[:, 256:512]) for q in range(4)]
        halves = [slice(0, CHUNK), slice(CHUNK, P)]
        KBG = [h4(units(82 + q)) for q in range(4)]
        VB = [h4(units(86 + q)) for q in range(4)]
        DA, DT = c4(90), c4(91)
        RG = [c4(96 + s) for s in range(2)]
        VN = [h4(units(98 + s)) for s in range(2)]
        ST = [[h4(units(62 + 2 * d + s)) for s in range(2)] for d in range(2)]
        OA = units(74, 4).rearrange("p (h t) -> p h t", h=HEADS)
        osq = units(22, 4).rearrange("p (h t) -> p h t", h=HEADS)
        ors = units(26, 4).rearrange("p (h t) -> p h t", h=HEADS)
        wo = [units(a, 16).rearrange("p (k n) -> p k n", k=KT) for a in (42, 34)]
        aw = [units(a, 8).rearrange("p (k n) -> p k n", k=KT) for a in (18, 26, 50)]
        QT = units(66, 8).rearrange("p (m t) -> p m t", m=8)
        KTT = units(74, 2).rearrange("p (m t) -> p m t", m=2)
        V = units(76, 2).rearrange("p (t n) -> p t n", t=NT)
        SC = [units(78 + s).rearrange("p (h k) -> p h k", h=2) for s in range(4)]
        PT = [units(82 + 2 * s, 2).rearrange("p (j h q) -> p j h q", j=2, h=4) for s in range(2)]
        negd = units(90).rearrange("p (b k) -> p b k", b=2)
        OT = units(91, 8).rearrange("p (m t) -> p m t", m=8)
        HTOK = [units(54, 8).rearrange("p (t d) -> p t d", t=NT)] + \
               [units(66, 8).rearrange("p (t d) -> p t d", t=NT) for _ in range(4)]
        GAIN = [units(62, 2)] + [units(86, 2)] * 4
        JUNK = [units(64, 2)] + [units(88, 2)] * 4
        xg = [units(66 + 2 * s, 2) for s in range(4)]
        xgT = [units(78 + 2 * s, 2).rearrange("p (k t) -> p k t", k=KT) for s in range(2)]
        yt = [units(74 + 2 * s, 2) for s in range(2)]
        sil = [units(88)[:, 256 * s:256 * s + 256] for s in range(2)]
        act_h = [units(89)[:, 256 * s:256 * s + 256] for s in range(2)]
        actT = [units(90)[:, 256 * s:256 * s + 256].rearrange("p (j t) -> p j t", j=2) for s in range(2)]
        YK = units(66, 16).rearrange("p (n d) -> p n d", n=8)
        tab_sb = units(91)[:, 0:128]
        tab_val = units(91)[:, 128:256]
        tab_gat = units(91)[:, 256:384]
        router = sb("router", [P, KT * 36]).rearrange("p (k n) -> p k n", k=KT)

        ss = sb("ss", [P, 5, NT])
        rstd = sb("rstd", [P, 5, NT])
        lnv = sb("lnv", [P, 5, NT])
        ab = sb("ab", [P, NT, 16])
        gt = sb("gt", [P, 6, NT, 8])
        wab = units(98)[:, 0:128].rearrange("p (k n) -> p k n", k=KT)
        GTEMP, BETA, GG, GC, KDS, KBS = range(6)
        rt = units(94, 4)
        lg = rt[:, 0:144].rearrange("p (t n) -> p t n", t=NT)
        gpad = rt[:, 144:176].rearrange("p (t n) -> p t n", t=NT)
        top_g = rt[:, 176:208].rearrange("p (t n) -> p t n", t=NT)
        idx_g = rt[:, 208:240].bitcast(u32).rearrange("p (t n) -> p t n", t=NT)
        top_e = rt[:, 240:272].rearrange("p (t n) -> p t n", t=NT)
        idx_e = rt[:, 272:304].bitcast(u32).rearrange("p (t n) -> p t n", t=NT)
        fi = rt[:, 304:320].rearrange("p (t n) -> p t n", t=NT)
        gexp = rt[:, 320:336].rearrange("p (t n) -> p t n", t=NT)
        emsk = rt[:, 336:464].rearrange("p (t n) -> p t n", t=NT)
        oh = rt[:, 512:1024].rearrange("p (k t n) -> p k t n", k=4, t=NT)
        gat_i = rt[:, 1024:1152].bitcast(u32)
        sca_i = rt[:, 1152:1280].bitcast(u32)
        rtmp = rt[:, 1280:1312].rearrange("p (k t) -> p k t", k=8)
        rt_ge = rt[:, 1312:1312 + 8 * (ROUNDS - 1)].rearrange("p (n r) -> p n r", n=8)
        coef = sb("coef", [P, 8, NT])
        rowf = sb("rowf", [P, 2, NT])
        rowi = sb("rowi", [P, 2, NT], u32)
        gcur = sb("gcur", [P, 4], u32)
        scur = sb("scur", [P, 4], u32)
        cmax = sb("cmax", [P, 1])
        flag = sb("flag", [P, 1], u32)
        mx = sb("mx", [P, 8, 2])
        den = sb("den", [P, 8, 2])
        es = sb("es", [P, 8, 2])
        nb = sb("nb", [P, 8, 2])
        sink8 = sb("sink8", [P, HQ])
        gls = sb("gls", [P, 8, HEADS, 2])

        pb = [ctx.enter_context(nc.psum_tensor(f"bank{i}", [P, U], f32)) for i in range(8)]

        ld_c, ld_p, ld_ab, ld_w4, ld_dist = (sem(n) for n in
            ("constants_loaded", "params_loaded", "wab_loaded", "w4_loaded", "dist_loaded"))
        ld_gain = sem("gain_loaded")
        ld_wc = sems("mixer_weights_loaded", 3)
        ld_wo = sem("w_out_loaded")
        ld_rt = sem("router_loaded")
        tab_init = sem("table_initialised")
        s_ss, s_rstd = sem("sumsq_done"), sem("rstd_done")
        s_h = sem("h_done")
        s_tr = sem("h_transposed")
        s_hT = sem("hT_copied")
        s_x = sem("x_updated")
        dch, ach, pch = sem("vector_chain"), sem("scalar_chain"), sem("pool_chain")
        f_ps, f_sin, f_ht, f_h4 = (sem(n) for n in ("filter_psum", "filter_sin", "filter_taps", "filter_rows"))
        f_red = sem("filter_reduced")
        m_qm, m_gl = sem("qkmat_masked"), sem("chunk_gates_kept")
        r_gs = sem("group_shifted")
        e_cg, e_cs = sem("gather_ids_copied"), sem("scatter_ids_copied")
        f_k, f_kc = sem("filter_dft"), sem("filter_dft_copied")
        s_pm, s_cva, s_cvd, s_sil = (sem(n) for n in ("proj_done", "conv_centre", "conv_sides", "silu_done"))
        s_ab, s_abc = sem("ab_done"), sem("ab_copied")
        y_tr, y_ut, y_u, y_p, y_y, y_i, y_z, y_o = (sem(n) for n in (
            "hy_transposed", "hy_time_copied", "hy_spectrum", "hy_products", "hy_product_sums",
            "hy_inverse", "hy_biased", "hy_gated"))
        g_gate, g_cum, g_gc, g_gx = (sem(n) for n in ("gates_done", "cumsum_done", "cumsum_copied", "cumsum_exp"))
        n_sq, n_ss, n_rs, n_n = (sem(n) for n in ("squared", "sumsq_bcast", "rstd_bcast", "qk_normed"))
        t_kv, t_kvc = sem("kv_transposed"), sem("kv_copied")
        m_r, m_gb, m_kk, m_qk = (sem(n) for n in ("decay_rows", "decay_bcast", "kk_done", "qk_done"))
        m_d, m_c, m_e, m_a, m_q, m_s = (sem(n) for n in (
            "decay_diff", "decay_clamped", "decay_exp", "amat_done", "qkmat_done", "scaled_done"))
        m_m, m_mt, m_x0, m_al = (sem(n) for n in ("mask1_done", "mask1_transposed", "inverse_started", "level_masked"))
        m_y, m_yc, m_xp, m_xc = (sem(n) for n in ("zT_done", "zT_copied", "offdiag_done", "inverse_updated"))
        m_uw, m_uwc, m_qd, m_kd = sem("uw_done"), sem("uw_copied"), sem("qdec_done"), sem("kdec_done")
        c_w, c_v, c_o, c_oc, c_s, c_sc = (sem(n) for n in (
            "scan_ws", "scan_vnew", "scan_o", "scan_o_copied", "scan_kv", "scan_state"))
        o_n = sem("o_gated")
        p_o = sem("out_proj_done")
        r_lg, r_lc, r_oh, r_rk, r_row, r_val, r_tt, r_fl = (sem(n) for n in (
            "logits_done", "group_exp_done", "onehot_done", "rank_done", "rows_done", "table_loaded",
            "table_transposed", "slots_ready"))
        r_sc, r_hd = sem("ids_scattered"), sem("h_stored")
        w_gs, w_ds = sems("gate_up_loaded", 2), sems("down_loaded", 2)
        e_xg = sems("expert_gathered", 4)
        e_T, e_xa, e_xd = sem("exp_transposed"), sem("exp_xT_a_copied"), sem("exp_xT_d_copied")
        e_GU, e_si, e_ac = sem("exp_gate_up"), sem("exp_silu"), sem("exp_act")
        e_HT, e_aT, e_D, e_ya, e_yd = (sem(n) for n in (
            "exp_act_transposed", "exp_actT_copied", "exp_down", "exp_y_a_copied", "exp_y_d_copied"))
        e_sc = sems("expert_scattered", 2)
        ld_yk = sems("x_and_yk_loaded", NT)
        ov = [{n: sem(f"more_{n}{L}") for n in ("pe", "act", "dve", "ids", "w", "g", "sc")} for L in range(2)]
        a_pm, a_pca, a_pcd = sem("qkv_done"), sem("qkv_even_copied"), sem("qkv_odd_copied")
        a_s, a_sc, a_mx, a_nb = (sem(n) for n in ("scores_done", "scores_biased", "score_max", "score_negmax"))
        a_e, a_rd, a_p, a_pt, a_pc, a_o, a_oc = (sem(n) for n in (
            "exp_done", "den_recip", "probs_done", "probs_transposed", "probsT_copied", "attn_out", "attn_copied"))
        st_y = sem("y_stored")

        X_DONE = [0, 8, 16, 24, 32]
        RSTD_DONE = [1, 1 + NT, 3 + NT, 3 + 2 * NT, 5 + 2 * NT]
        LOGD = 1.0 / D

        def slopes(head):
            return float(2.0 ** (-8.0 * (head + 1) / HQ))

        def head_of(t, s):
            return (4 * s + t) if t < 4 else (8 + 4 * s + t - 4)

        block = ctx.enter_context(nc.Block())

        @block.sync
        def _(sp):
            for t in range(NT):
                sp.dma_start(X[:, t, :], x_in[t * P:(t + 1) * P, :]).then_inc(ld_yk[t], 16)
            sp.dma_start(pc, pconst[:, :]).then_inc(ld_c, 16)
            sp.dma_start(GAIN[0], gains[0, :, :]).then_inc(ld_gain, 16)
            sp.dma_start(wchunk[0], w_in[0, :, :, :]).then_inc(ld_wc[0], 16)
            sp.dma_start(parm[:, :], params[:, 0:PA_W4]).then_inc(ld_p, 16)
            sp.dma_start(mc, mconst[:, :]).then_inc(ld_p, 16)
            sp.dma_start(wchunk[1], w_in[1, :, :, :]).then_inc(ld_wc[1], 16)
            sp.dma_start(w4, params[0:64, PA_W4:NPAR]).then_inc(ld_w4, 16)
            sp.wait_ge(pch, 1)
            for L in range(2):
                sp.dma_start(tab_dram[L][:, :], norow).then_inc(tab_init, 16)
            for c in range(2, NCH):
                if c >= 3:
                    sp.wait_ge(s_pm, 4 * (c - 2))
                sp.dma_start(wchunk[c % 3], w_in[c, :, :, :]).then_inc(ld_wc[c % 3], 16)
            sp.wait_ge(f_k, 10)
            sp.dma_start(wab, w_ab[:, :, :]).then_inc(ld_ab, 16)
            sp.wait_ge(m_uw, 2 * 8)
            sp.dma_start(wo[0], w_out0[:, :, :]).then_inc(ld_wo, 16)

            def routing_loads(L):
                sp.dma_start(GAIN[2 * L + 1], gains[2 * L + 1, :, :]).then_inc(ld_gain, 16)
                sp.dma_start(router, w_router[L, :, :, :]).then_inc(ld_rt, 16)

            def moe_loads(L):
                for t in range(NT):
                    sp.wait_ge(s_h, NT * (2 * L + 1) + t + 1)
                    sp.dma_start(h_dram[L][t * P:(t + 1) * P, :], HTOK[1][:, t, :]).then_inc(r_hd, 16)
                sp.dma_start(GAIN[2 * L + 2], gains[2 * L + 2, :, :]).then_inc(ld_gain, 16)
                if L == 0:
                    sp.dma_start(dn[0], w_dn[L, 0, :, :]).then_inc(w_ds[0], 16)
                sp.dma_start(gu[1], w_gu[L, 1, :, :]).then_inc(w_gs[1], 16)
                if L == 0:
                    sp.dma_start(dn[1], w_dn[L, 1, :, :]).then_inc(w_ds[1], 16)
                sp.wait_ge(r_sc, 128 * (L + 1))
                sp.dma_start(tab_sb, tab_dram[L][:, :]).then_inc(r_val, 16)

                B = NPAIR * L
                with sp.Fori(0, NPAIR // 2 - 1) as i:
                    for j in range(2):
                        g_src = w_gu[L, bass.ds(sp.snap(i * 2 + (j + 2)), 1), :, :].rearrange("o p n -> (o p) n")
                        d_src = w_dn[L, bass.ds(sp.snap(i * 2 + (j + 2)), 1), :, :].rearrange("o p n -> (o p) n")
                        sp.wait_ge(e_GU, i * 2 + (j + 1 + B))
                        sp.dma_start(gu[j], g_src).then_inc(w_gs[j], 16)
                        sp.wait_ge(e_D, i * 2 + (j + 1 + B))
                        sp.dma_start(dn[j], d_src).then_inc(w_ds[j], 16)
                if L == 0:
                    sp.wait_ge(e_GU, NPAIR - 1)
                    sp.dma_start(aw[0], w_qkv[0, :, :, :]).then_inc(ld_wc[0], 16)
                o = ov[L]
                sp.wait_ge(r_fl, L + 1)
                more = sp.value_load(flag[0:1, 0:1], min_val=0, max_val=TOK)
                with sp.If(more > CAP):
                    sp.wait_ge(e_D, NPAIR * (L + 1))
                    sp.dma_start(gu[1], w_gu[L, 0, :, :]).then_inc(o["w"], 16)
                    sp.dma_start(dn[1], w_dn[L, 0, :, :]).then_inc(o["w"], 16)
                    for r in range(1, ROUNDS):
                        lo = 1 if r == 1 else 0
                        with sp.Fori(lo, NPAIR) as e:
                            g_src = w_gu[L, bass.ds(e, 1), :, :].rearrange("o p n -> (o p) n")
                            d_src = w_dn[L, bass.ds(e, 1), :, :].rearrange("o p n -> (o p) n")
                            sp.wait_ge(o["pe"], e * 4 + 4 * (r - 1) * NPAIR)
                            sp.dma_start(gu[1], g_src).then_inc(o["w"], 16)
                            sp.dma_start(dn[1], d_src).then_inc(o["w"], 16)
                    sp.wait_ge(o["sc"], 16 * NPAIR * (ROUNDS - 1))
                for s in range(2):
                    sp.wait_ge(e_sc[s], 16 * (NPAIR // 2) * (L + 1))
                for t in range(NT):
                    for n in (t, NT + t):
                        sp.dma_start(YK[:, n, :], yk_dram[L][n * P:(n + 1) * P, :]).then_inc(ld_yk[t], 16)

            sp.wait_ge(m_uw, 4 * 4)
            routing_loads(0)
            sp.wait_ge(o_n, HEADS)
            sp.dma_start(gu[0], w_gu[0, 0, :, :]).then_inc(w_gs[0], 16)
            moe_loads(0)
            for s in (1, 2):
                sp.dma_start(aw[s], w_qkv[s, :, :, :]).then_inc(ld_wc[s], 16)
            sp.wait_ge(e_D, NPAIR)
            sp.dma_start(wo[1], w_out1[:, :, :]).then_inc(ld_wo, 16)
            sp.dma_start(negd, dconst[:, :].rearrange("p (b k) -> p b k", b=2)).then_inc(ld_dist, 16)
            sp.wait_ge(a_pm, 14)
            sp.dma_start(gu[0], w_gu[1, 0, :, :]).then_inc(w_gs[0], 16)
            for s in range(2):
                sp.dma_start(dn[s], w_dn[1, s, :, :]).then_inc(w_ds[s], 16)
            sp.wait_ge(s_h, 3 * NT)
            routing_loads(1)
            moe_loads(1)
            for t in range(NT):
                sp.wait_ge(s_h, 4 * NT + t + 1)
                sp.dma_start(y_out[t * P:(t + 1) * P, :], HTOK[4][:, t, :]).then_inc(st_y, 16)
            sp.wait_ge(st_y, 16 * NT)

        @block.tensor
        def _(pe):
            mm, tr = nc.tensor.matmul, nc.tensor.transpose

            def transpose_tile(n, t):
                pe.wait_ge(s_h, NT * n + t + 1)
                for half in range(2):
                    if t >= 2:
                        pe.wait_ge(s_hT, 8 * n + 2 * (t - 2) + half + 1)
                    for k in range(4):
                        i = tr(pb[4 * (t % 2) + half][:, k * P:(k + 1) * P],
                               HTOK[n][:, t, (4 * half + k) * P:(4 * half + k + 1) * P], ident)
                    i.then_inc(s_tr, 1)

            def transpose_h(n):
                for t in range(NT):
                    transpose_tile(n, t)

            def hT_ready(n, tiles=NT):
                pe.wait_ge(s_hT, 8 * n + 2 * tiles)

            def filter_layer(j):
                if j == 0:
                    pe.wait_ge(ld_p, 32)
                    mm(pb[7][0:64, 0:SEQ], parm[0:33, PA_W1:PA_W1 + 64], featsT, start=True, stop=True).then_inc(f_ps, 1)
                else:
                    pe.wait_ge(f_sin, j)
                    w = (PA_W2, PA_W3)[j - 1]
                    mm(pb[7][0:64, 0:SEQ], parm[0:64, w:w + 64], fz[:, 0, :], start=True, stop=True).then_inc(f_ps, 1)

            def filter_rows(first):
                pe.wait_ge(f_sin, 3)
                pe.wait_ge(ld_w4, 16)
                for n in range(first, first + 4):
                    o, i, s = n // 4, (n // 2) % 2, n % 2
                    if n >= 4:
                        pe.wait_ge(f_ht, n // 2 - 1)
                    mm(pb[4 + n % 4][:, :], fz[:, 0, i * P:(i + 1) * P], w4[:, (2 * o + s) * U:(2 * o + s + 1) * U],
                       start=True, stop=True).then_inc(f_h4, 1)

            def filter_spectra(first):
                pe.wait_ge(f_ht, 4)
                for n in range(first, first + 2):
                    o, j = n // 5, n % 5
                    if n >= 2:
                        pe.wait_ge(f_kc, n - 1)
                    for i in range(2):
                        lhs = F[:, i, j * P:(j + 1) * P] if j < 2 else (
                            Fs0[:, i, (j - 2) * P:(j - 1) * P] if j < 4 else Fc0[:, i, :])
                        q = mm(pb[6 + n % 2][:, :], lhs, HP[:, o, i, 1 if j in (2, 3) else 0, :],
                               start=(i == 0), stop=(i == 1))
                    q.then_inc(f_k, 1)

            pe.wait_ge(ld_c, 16)
            transpose_h(0)
            hT_ready(0)
            for m in range(28):
                c = m // 4
                if m % 4 == 0:
                    pe.wait_ge(ld_wc[c % 3], 16 * (c // 3 + 1))
                if m >= 4:
                    if m - 4 < 24:
                        pe.wait_ge(s_cvd, 2 * (m - 3))
                for k in range(KT):
                    i = mm(pb[m % 4][:, :], wchunk[c % 3][:, k, (m % 4) * P:(m % 4 + 1) * P], HT[:, k, :],
                           start=(k == 0), stop=(k == KT - 1))
                i.then_inc(s_pm, 1)
                if m < 3:
                    filter_layer(m)
                elif m < 5:
                    filter_rows(4 * (m - 3))
                elif m < 10:
                    filter_spectra(2 * (m - 5))
            pe.wait_ge(ld_ab, 16)
            for t in range(NT):
                for k in range(KT):
                    i = mm(pb[4][:, t * 16:(t + 1) * 16], HT[:, k, t * P:(t + 1) * P], wab[:, k, :],
                           start=(k == 0), stop=(k == KT - 1))
            i.then_inc(s_ab, 1)

            pe.wait_ge(s_abc, 1)
            pe.wait_ge(f_kc, 10)
            for o in range(2):
                src = hx[:, 8:12, :] if o == 0 else Z1
                if o == 0:
                    pe.wait_ge(s_cvd, 24)
                    pe.wait_ge(s_sil, 16)
                else:
                    pe.wait_ge(y_o, 4)
                for n in range(4):
                    if o == 1:
                        pe.wait_ge(y_z, 4)
                    for c in range(4):
                        i = tr(pb[n][:, c * P:(c + 1) * P], src[:, c, n * P:(n + 1) * P], ident)
                    i.then_inc(y_tr, 1)
                for b in range(2):
                    pe.wait_ge(y_ut, 4 * o + 2 * b + 2)
                    for pair in range(2):
                        u = 2 * b + pair
                        if u >= 2:
                            pe.wait_ge(y_p, 16 * o + 4 * (u - 1))
                        for ri in range(2):
                            f = pair + 2 * ri
                            for i in range(2):
                                q = mm(pb[4 + 2 * (u % 2) + ri][:, :], F[:, i, f * P:(f + 1) * P], UT[:, b, i, :],
                                       start=(i == 0), stop=(i == 1))
                        q.then_inc(y_u, 1)
                for b in range(2):
                    pe.wait_ge(y_y, 8 * o + 4 * (b + 1))
                    for c in range(4):
                        for f in range(4):
                            i = mm(pb[c][:, b * SEQ:(b + 1) * SEQ], YF[:, b, f, c * P:(c + 1) * P], G[:, f, :],
                                   start=(f == 0), stop=(f == 3))
                        if b == 1:
                            i.then_inc(y_i, 1)

            pe.wait_ge(g_gate, 1)
            pe.wait_ge(y_p, 32)
            for d in range(2):
                mm(pb[4][:, 16 * d:16 * d + 16], incl[d], gt[:, GG, :, 4 * d:4 * d + 4], start=True, stop=True)
            mm(pb[4][:, 32:64], chunk_ones, gt[:, GG, :, :], start=True, stop=True).then_inc(g_cum, 1)
            pe.wait_ge(n_sq, 8)
            for n in range(8):
                if n == 3:
                    pe.wait_ge(y_z, 8)
                if n == 7:
                    pe.wait_ge(g_gc, 1)
                mm(pb[(5 + n) % 8 if n < 3 else n - 3][:, :], ones, sqn[:, n, :], start=True, stop=True).then_inc(n_ss, 1)
            pe.wait_ge(n_rs, 1)
            for n in range(8):
                src = vT if n < 4 else kT
                t = n % 4
                if n == 4:
                    pe.wait_ge(n_n, 8)
                if n >= 4:
                    pe.wait_ge(t_kvc, n - 3)
                for h in range(HEADS):
                    i = tr(pb[n % 4][:, h * P:(h + 1) * P], src[:, h, t * P:(t + 1) * P], ident)
                i.then_inc(t_kv, 1)
            pe.wait_ge(t_kvc, 8)

            def chunk_products(bank, lhsT, rhs):
                for h in range(HEADS):
                    i = mm(bank[:, h * CHUNK:(h + 1) * CHUNK], lhsT[:, h, :], rhs[:, h, :], start=True, stop=True)
                return i

            def level_transpose(b, q):
                n = 4 * b + q
                pe.wait_ge(m_m, n + 1)
                if q >= 2:
                    pe.wait_ge(m_x0, 2 * (n - 1))
                chunk_products(pb[4 + q % 2], AL[q], eye_c.unsqueeze(1).broadcast_to([P, HEADS, CHUNK]))\
                    .then_inc(m_mt, 1)

            for b in range(NSEQ):
                if b == 1:
                    pe.wait_ge(c_oc, 8)
                for q in range(4):
                    n = 4 * b + q
                    t, d = 2 * b + q // 2, q % 2
                    pe.wait_ge(m_r, n + 1)
                    if n >= 2:
                        pe.wait_ge(m_d, n - 1)
                        pe.wait_ge(m_e, 3 * n - 5)
                    mm(pb[6 + n % 2][:, 0:HEADS * CHUNK], chunk_ones, RG[n % 2], start=True, stop=True)
                    for u in range(2):
                        i = mm(h4(pb[n % 2][:, :])[:, :, halves[u]], half_ones[u], RG[n % 2], start=True, stop=True)
                    i.then_inc(m_gb, 1)
                    if d == 0:
                        if n >= 2:
                            pe.wait_ge(m_a, n)
                            pe.wait_ge(m_q, n)
                        for bank, src, done in ((pb[2], kT, m_kk), (pb[3], qT, m_qk)):
                            for h in range(HEADS):
                                for u in range(2):
                                    toks = slice(t * P + u * CHUNK, t * P + (u + 1) * CHUNK)
                                    i = mm(bank[halves[u], h * CHUNK:(h + 1) * CHUNK], kT[:, h, toks],
                                           src[:, h, toks], start=True, stop=True)
                            i.then_inc(done, 1)
                    if q:
                        level_transpose(b, q - 1)
                level_transpose(b, 3)
                for lv in range(1, 6):
                    for q in range(4):
                        n = 4 * b + q
                        g = 20 * b + 4 * (lv - 1) + q
                        pe.wait_ge(m_al, g + 1)
                        if lv == 1:
                            pe.wait_ge(m_x0, 2 * (n + 1))
                            pe.wait_ge(m_q, n + 1)
                        else:
                            pe.wait_ge(m_xc, 36 * b + 8 * (lv - 2) + 2 * (q + 1))
                        if g >= 2:
                            pe.wait_ge(m_yc, g - 1)
                        chunk_products(pb[g % 2], AL[q], XT[q]).then_inc(m_y, 1)
                    for q in range(4):
                        g = 20 * b + 4 * (lv - 1) + q
                        pe.wait_ge(m_yc, g + 1)
                        n2 = 36 * b + 8 * (lv - 1) + (2 * q if lv < 5 else q)
                        if lv < 5:
                            if n2 >= 4:
                                pe.wait_ge(m_xc, n2 - 3)
                            for h in range(HEADS):
                                i = mm(pb[2 + n2 % 4][:, h * P:(h + 1) * P], YY[q][:, h, :], XX[q][:, h, :],
                                       start=True, stop=True)
                            i.then_inc(m_xp, 1)
                            n2 += 1
                        if n2 >= 4:
                            pe.wait_ge(m_xc, n2 - 3)
                        chunk_products(pb[2 + n2 % 4], XX[q], YC[q]).then_inc(m_xp, 1)
                for q in range(4):
                    n = 4 * b + q
                    pe.wait_ge(m_s, 2 * (n + 1))
                    pe.wait_ge(m_xc, 36 * (b + 1))
                    if q >= 2:
                        pe.wait_ge(m_uwc, 2 * (n - 1))
                    for h in range(HEADS):
                        i = mm(pb[2 * (q % 2)][:, h * P:(h + 1) * P], XX[q][:, h, :], VB[q][:, h, :],
                               start=True, stop=True)
                    i.then_inc(m_uw, 1)
                    for h in range(HEADS):
                        i = mm(pb[2 * (q % 2) + 1][:, h * P:(h + 1) * P], KBG[q][:, h, :], XX[q][:, h, :],
                               start=True, stop=True)
                    i.then_inc(m_uw, 1)
                pe.wait_ge(m_uwc, 8 * (b + 1))
                pe.wait_ge(m_qd, 4 * (b + 1))
                pe.wait_ge(m_kd, 4 * (b + 1))
                pe.wait_ge(m_qm, 4 * (b + 1))
                pe.wait_ge(n_n, 8)
                for s in range(4):
                    place = []
                    for d in range(2):
                        c = s if d == 0 else 3 - s
                        q, half = 2 * (c // 2) + d, c % 2
                        place.append((q, slice(CHUNK * half, CHUNK * half + CHUNK), ST[d][s % 2],
                                      pb[6 + d][:, 0:HEADS * CHUNK].rearrange("p (h c) -> p h c", h=HEADS)))
                    if s > 0:
                        pe.wait_ge(c_sc, 6 * b + 2 * s)
                        pe.wait_ge(c_v, 8 * b + 2 * s)
                        for h in range(HEADS):
                            for d, (q, rows, S, out) in enumerate(place):
                                i = mm(pb[4 + d][rows, h * P:(h + 1) * P], WT[q][:, h, rows], S[:, h, :],
                                       start=True, stop=True)
                                if h == HEADS - 1:
                                    i.then_inc(c_w, 1)
                    if 8 * b + 2 * s:
                        pe.wait_ge(c_oc, 8 * b + 2 * s)
                    if s > 0:
                        for q, rows, S, out in place:
                            for h in range(HEADS):
                                mm(out[:, h, :], S[:, h, :], QD[q][:, h, rows], start=(h == 0), stop=False)
                    pe.wait_ge(c_v, 8 * b + 2 * s + 2)
                    if s < 3:
                        for h in range(HEADS):
                            for d, (q, rows, S, out) in enumerate(place):
                                i = mm(pb[2 + d][:, h * P:(h + 1) * P], KD[q][rows, h, :], VN[d][rows, h, :],
                                       start=True, stop=True)
                                if h == HEADS - 1:
                                    i.then_inc(c_s, 1)
                    for d, (q, rows, S, out) in enumerate(place):
                        for h in range(HEADS):
                            i = mm(out[:, h, :], VN[d][rows, h, :], QK[q][rows, h, :], start=(s == 0),
                                   stop=(s == 0 or h == HEADS - 1))
                        i.then_inc(c_o, 1)

            pe.wait_ge(c_oc, 16)
            pe.wait_ge(c_sc, 12)
            for h in range(HEADS):
                pe.wait_ge(n_sq, 8 + h + 1)
                mm(pb[h][:, :], ones, osq[:, h, :], start=True, stop=True).then_inc(n_ss, 1)

            def logits(L, t):
                pe.wait_ge(ld_rt, 16 * (L + 1))
                hT_ready(2 * L + 1, t + 1)
                for k in range(KT):
                    i = mm(pb[6][:, t * 36:(t + 1) * 36], HT[:, k, t * P:(t + 1) * P], router[:, k, :],
                           start=(k == 0), stop=(k == KT - 1))
                if t == NT - 1:
                    i.then_inc(r_lg, 1)

            def out_proj(L, oT):
                pe.wait_ge(ld_wo, 16 * (L + 1))
                for n in range(8):
                    t, c = n // 2, n % 2
                    if n >= 2:
                        pe.wait_ge(s_x, X_DONE[2 * L] + n - 1)
                    for k in range(KT):
                        i = mm(pb[2 + n % 2][:, :], oT(k)[:, t * P:(t + 1) * P], wo[L][:, k, c * U:(c + 1) * U],
                               start=(k == 0), stop=(k == KT - 1))
                    i.then_inc(p_o, 1)
                    if t and c == 0:
                        transpose_tile(2 * L + 1, t - 1)
                    elif t:
                        logits(L, t - 1)
                transpose_tile(2 * L + 1, NT - 1)
                logits(L, NT - 1)

            pe.wait_ge(o_n, HEADS)
            pe.wait_ge(c_sc, 12)
            pe.wait_ge(y_o, 8)
            out_proj(0, lambda k: OA[:, k, :] if k < 4 else OB[:, k - 4, :])

            def gate_up_products(out, xT, w):
                for k in range(KT):
                    for h in range(2):
                        cols = slice(CAP * h, CAP * h + CAP)
                        i = mm(out[cols, :], xT[:, k, cols], w[:, h, k, :], start=(k == 0), stop=(k == KT - 1))
                return i

            def down_products(aT, w):
                for c in range(2):
                    for f in range(2):
                        for h in range(2):
                            cols = slice(CAP * h, CAP * h + CAP)
                            i = mm(pb[5 + c][cols, :], aT[:, f, cols], w[:, h, f, c * U:(c + 1) * U],
                                   start=(f == 0), stop=(f == 1))
                return i

            def moe(L):
                pe.wait_ge(r_oh, L + 1)
                for s in range(NT):
                    mm(pb[3][:, s * NEXP:NT * NEXP], ones if s else strictU, oh[:, 2, 0:NT - s, :],
                       start=(s == 0), stop=(s == NT - 1))
                for u in range(NT):
                    i = mm(pb[3][:, NT * NEXP:(NT + 1) * NEXP], ones, oh[:, 2, u, :], start=(u == 0), stop=(u == NT - 1))
                i.then_inc(r_rk, 1)
                pe.wait_ge(r_val, 16 * (L + 1))
                tr(pb[4][:, 0:P], tab_sb, ident).then_inc(r_tt, 1)
                pe.wait_ge(r_fl, L + 1)
                B = NPAIR * L

                def transposes(e, j):
                    pe.wait_ge(e_xg[j], (e - j) * 4 + (16 + 4 * B))
                    if not (isinstance(e, int) and e + B == 0):
                        pe.wait_ge(e_xa, e + B)
                        pe.wait_ge(e_xd, e + B)
                    for half in range(2):
                        for k in range(4):
                            i = tr(pb[half][:, k * P:(k + 1) * P],
                                   xg[j][:, (4 * half + k) * P:(4 * half + k + 1) * P], ident)
                    i.then_inc(e_T, 1)

                def gate_up(e, j):
                    pe.wait_ge(w_gs[j % 2], (e - j % 2) * 8 + (16 + 8 * B))
                    pe.wait_ge(e_xa, e + (B + 1))
                    pe.wait_ge(e_xd, e + (B + 1))
                    if not (isinstance(e, int) and e + B < 2):
                        pe.wait_ge(e_ac, e + (B - 1))
                    gate_up_products(pb[2 + j % 2], xgT[j % 2], gu[j % 2]).then_inc(e_GU, 1)

                def act_transposes(e, j):
                    pe.wait_ge(e_ac, e + (B + 1))
                    if not (isinstance(e, int) and e + B == 0):
                        pe.wait_ge(e_aT, e + B)
                    for f in range(2):
                        i = tr(pb[4][:, f * P:(f + 1) * P], act_h[j % 2][:, f * P:(f + 1) * P], ident)
                    i.then_inc(e_HT, 1)

                def down(e, j):
                    pe.wait_ge(e_aT, e + (B + 1))
                    if not (isinstance(e, int) and e + B == 0):
                        pe.wait_ge(e_ya, e + B)
                        pe.wait_ge(e_yd, e + B)
                    pe.wait_ge(w_ds[j % 2], (e - j % 2) * 8 + (16 + 8 * B))
                    down_products(actT[j % 2], dn[j % 2]).then_inc(e_D, 1)

                def four(i, first=False, last=False):
                    for j in range(4):
                        e = i * 4 + j
                        gate_up(e, j)
                        if not (first and j == 0):
                            act_transposes(e - 1, (j - 1) % 4)
                        if not (last and j == 3):
                            transposes(e + 1, (j + 1) % 4)
                        if not (first and j == 0):
                            down(e - 1, (j - 1) % 4)

                transposes(0, 0)
                four(0, first=True)
                with pe.Fori(1, NPAIR // 4 - 1) as i:
                    four(i)
                four(NPAIR // 4 - 1, last=True)
                act_transposes(NPAIR - 1, 3)
                down(NPAIR - 1, 3)

                o = ov[L]
                more = nc.tensor.value_load(flag[0:1, 0:1], min_val=0, max_val=TOK)
                with pe.If(more > CAP):
                    pe.wait_ge(e_ya, B + NPAIR)
                    pe.wait_ge(e_yd, B + NPAIR)
                    pe.wait_ge(e_aT, B + NPAIR)
                    for r in range(1, ROUNDS):
                        R = (r - 1) * NPAIR
                        with pe.Fori(0, NPAIR) as e:
                            pe.wait_ge(o["g"], e * 16 + 16 * (R + 1))
                            for half in range(2):
                                for k in range(4):
                                    i = tr(pb[half][:, k * P:(k + 1) * P],
                                           xg[0][:, (4 * half + k) * P:(4 * half + k + 1) * P], ident)
                            i.then_inc(o["pe"], 1)
                            pe.wait_ge(o["act"], e * 4 + (4 * R + 1))
                            pe.wait_ge(o["dve"], e * 3 + (3 * R + 1))
                            pe.wait_ge(o["w"], e * 32 + 32 * (R + 1))
                            i = gate_up_products(pb[2], xgT[0], gu[1])
                            i.then_inc(o["pe"], 1)
                            pe.wait_ge(o["dve"], e * 3 + (3 * R + 2))
                            for f in range(2):
                                i = tr(pb[4][:, f * P:(f + 1) * P], act_h[0][:, f * P:(f + 1) * P], ident)
                            i.then_inc(o["pe"], 1)
                            pe.wait_ge(o["act"], e * 4 + (4 * R + 3))
                            i = down_products(actT[0], dn[1])
                            i.then_inc(o["pe"], 1)
                            pe.wait_ge(o["act"], e * 4 + (4 * R + 4))
                            pe.wait_ge(o["dve"], e * 3 + (3 * R + 3))

            moe(0)

            transpose_h(2)
            hT_ready(2)
            for m in range(14):
                if m % 4 == 0 and m < 12:
                    pe.wait_ge(ld_wc[m // 4], (64, 48, 48)[m // 4])
                if m >= 4:
                    pe.wait_ge((a_pca, a_pcd)[m % 2], m // 2 - 1)
                for k in range(KT):
                    if m < 10:
                        i = mm(pb[m % 4][:, :], aw[m // 4][:, k, (m % 4) * P:(m % 4 + 1) * P], HT[:, k, :],
                               start=(k == 0), stop=(k == KT - 1))
                    else:
                        t = m - 10
                        i = mm(pb[m % 4][:, 0:256], HT[:, k, t * P:(t + 1) * P], aw[2][:, k, 256:512],
                               start=(k == 0), stop=(k == KT - 1))
                i.then_inc(a_pm, 1)
            pe.wait_ge(a_pca, 7)
            pe.wait_ge(a_pcd, 7)

            def unit(n):
                b, qb, g, pr = n // 16, (n // 8) % 2, (n // 2) % 4, n % 2
                return b, qb, g, pr

            def scores(n):
                b, qb, g, pr = unit(n)
                rows = slice(64 * (g % 2), 64 * (g % 2) + 64)
                if n >= 2:
                    pe.wait_ge(a_sc, 2 * (n - 1))
                for hh in range(2):
                    t = 4 * (g // 2) + 2 * pr + hh
                    tok0 = b * SEQ + qb * P
                    i = mm(pb[n % 2][:, hh * SEQ:(hh + 1) * SEQ], QT[rows, t, tok0:tok0 + P],
                           KTT[rows, g // 2, b * SEQ:(b + 1) * SEQ], start=True, stop=True)
                i.then_inc(a_s, 1)

            def probs_t(n):
                pe.wait_ge(a_p, n + 1)
                if n >= 2:
                    pe.wait_ge(a_pc, n - 1)
                for hh in range(2):
                    for kt in range(2):
                        i = tr(pb[2 + n % 2][:, (2 * kt + hh) * P:(2 * kt + hh + 1) * P],
                               SC[n % 4][:, hh, kt * P:(kt + 1) * P], ident)
                i.then_inc(a_pt, 1)

            def pv(u):
                b, qb, g, _ = unit(2 * u)
                rows = slice(64 * (g % 2), 64 * (g % 2) + 64)
                pe.wait_ge(a_pc, 2 * u + 2)
                if u >= 2:
                    pe.wait_ge(a_oc, u - 1)
                for kt in range(2):
                    i = mm(pb[4 + u % 2][rows, :], V[:, 2 * b + kt, g * HD:(g + 1) * HD], PT[u % 2][:, kt, :, :],
                           start=(kt == 0), stop=(kt == 1))
                i.then_inc(a_o, 1)

            NU = 32
            for n in range(NU + 5):
                if n < NU:
                    scores(n)
                if 3 <= n < NU + 3:
                    probs_t(n - 3)
                if n >= 6 and n % 2 == 0:
                    pv((n - 6) // 2)
            pe.wait_ge(a_oc, 16)
            out_proj(1, lambda k: OT[:, k, :])
            moe(1)


        @block.scalar
        def _(act):
            af = nc.scalar.activation
            ac = [0]

            def link(i):
                ac[0] += 1
                i.then_inc(ach, 1)
                act.wait_ge(ach, ac[0])

            def norm_stats(n):
                for t in range(NT):
                    if n:
                        act.wait_ge(s_x, X_DONE[n] - 8 + 2 * (t + 1))
                    else:
                        act.wait_ge(ld_yk[t], 16)
                    link(af(JUNK[n], X[:, t, :], ACT.Square, accum_out=ss[:, n, t:t + 1]))
                    if t == 1 and n or t == NT - 1:
                        done = slice(0 if t == 1 or n == 0 else 2, t + 1)
                        if n == 0:
                            act.wait_ge(ld_c, 16)
                        link(af(lnv[:, n, done], ss[:, n, done], ACT.Ln, bias=eps_c, scale=LOGD))
                        af(rstd[:, n, done], lnv[:, n, done], ACT.Exp, scale=-0.5).then_inc(s_rstd, 1)

            def hT_copy(n, t):
                for half in range(2):
                    act.wait_ge(s_tr, 8 * n + 2 * t + half + 1)
                    af(HT[:, 4 * half:4 * half + 4, t * P:(t + 1) * P],
                       pb[4 * (t % 2) + half][:, :].rearrange("p (k c) -> p k c", k=4), ACT.Copy).then_inc(s_hT, 1)

            def hT_copies(n):
                for t in range(NT):
                    hT_copy(n, t)

            def norm_by_tiles(n):
                for t in range(NT):
                    act.wait_ge(s_x, X_DONE[n] - 8 + 2 * (t + 1))
                    link(af(JUNK[n], X[:, t, :], ACT.Square, accum_out=ss[:, n, t:t + 1]))
                    link(af(lnv[:, n, t:t + 1], ss[:, n, t:t + 1], ACT.Ln, bias=eps_c, scale=LOGD))
                    af(rstd[:, n, t:t + 1], lnv[:, n, t:t + 1], ACT.Exp, scale=-0.5).then_inc(s_rstd, 1)
                    hT_copy(n, t)

            norm_stats(0)
            hT_copies(0)
            act.wait_ge(ld_p, 32)

            def silu_tile(m):
                act.wait_ge(s_cvd, 2 * (m + 1))
                af(qkvz[:, m - 12, :], qkvz[:, m - 12, :], ACT.Silu).then_inc(s_sil, 1)
            for m in range(28):
                if m == 12:
                    act.wait_ge(tab_init, 32)
                act.wait_ge(s_pm, m + 1)
                if m < 24:
                    dst = hx[:, m, :] if m < 12 else qkvz[:, m - 12, :]
                    w = PA_CONVB + 3 * m + 1 if m < 12 else PA_CONVA + 3 * (m - 12) + 1
                    af(dst, pb[m % 4][:, :], ACT.Copy, scale=parm[:, w:w + 1]).then_inc(s_cva, 1)
                else:
                    if m == 24:
                        silu_tile(23)
                    af(qkvz[:, m - 12, :], pb[m % 4][:, :], ACT.Silu).then_inc(s_sil, 1)
                if 13 <= m < 24:
                    silu_tile(m - 1)
                if m < 3:
                    act.wait_ge(f_red, m + 1)
                    af(fz[:, 0, :], fz[:, 1, :], ACT.Sin).then_inc(f_sin, 1)
                elif 5 <= m < 10:
                    for n in range(2 * (m - 5), 2 * (m - 4)):
                        act.wait_ge(f_k, n + 1)
                        af(Kf[:, n // 5, n % 5, :], pb[6 + n % 2][:, :], ACT.Copy).then_inc(f_kc, 1)

            act.wait_ge(s_abc, 1)
            af(gt[:, GTEMP, :, :], ab[:, :, 0:8], ACT.Exp, scale=-1.0)
            act.wait_ge(s_abc, 2)
            link(af(gt[:, KDS, :, :], gt[:, KDS, :, :], ACT.Exp))
            link(af(gt[:, KDS, :, :], gt[:, KDS, :, :], ACT.Ln, bias=ones[:, 0:1]))
            af(gt[:, KBS, 0, :], parm[:, PA_ALOG:PA_ALOG + 8], ACT.Exp).then_inc(g_gx, 1)

            for o in range(2):
                for n in range(4):
                    act.wait_ge(y_tr, 4 * o + n + 1)
                    af(UT[:, n // 2, n % 2, :], pb[n][:, :], ACT.Copy).then_inc(y_ut, 1)
                if o == 0:
                    for n in range(8):
                        af(sqn[:, n, :], qkvz[:, n, :], ACT.Square).then_inc(n_sq, 1)

            act.wait_ge(g_gc, 1)
            af(gt[:, KDS, :, :], gt[:, KDS, :, :], ACT.Exp)
            af(gt[:, KBS, :, :], gt[:, GC, :, :], ACT.Exp).then_inc(g_gx, 1)

            act.wait_ge(y_y, 16)
            for n in range(8):
                act.wait_ge(n_ss, n + 1)
                i = af(rsn[:, n, :], pb[(5 + n) % 8 if n < 3 else n - 3][:, :], ACT.Ln, bias=eps_c)
            link(i)
            for n in range(8):
                af(rsn[:, n, :], rsn[:, n, :], ACT.Exp, scale=-0.5).then_inc(n_rs, 1)
            for n in range(8):
                act.wait_ge(t_kv, n + 1)
                dst = vtok[:, n, :, :] if n < 4 else ktok[:, n - 4, :, :]
                af(dst, h4(pb[n % 4][:, :]), ACT.Copy).then_inc(t_kvc, 1)

            for b in range(NSEQ):
                if b == 1:
                    act.wait_ge(c_o, 8)
                    act.wait_ge(c_s, 6)
                for q in range(4):
                    n = 4 * b + q
                    act.wait_ge(m_gb, n + 1)
                    af(QD[q], h4(pb[n % 2][:, :]), ACT.Exp).then_inc(m_e, 1)
                    act.wait_ge(m_e, 3 * n + 1)
                    last = QD[q][:, :, 63:128:64] if q % 2 == 0 else QD[q][:, :, 0:128:64]
                    af(gls[:, n, :, :], last, ACT.Copy).then_inc(m_gl, 1)
                    act.wait_ge(m_d, n + 1)
                    af(DA, DA, ACT.Exp, scale=-1.0).then_inc(m_e, 1)
                    af(DT, DT, ACT.Exp).then_inc(m_e, 1)
                for g in range(20 * b, 20 * b + 20):
                    act.wait_ge(m_y, g + 1)
                    af(YC[g % 4], h4(pb[g % 2][:, 0:HEADS * CHUNK]), ACT.Copy)
                    for rows in halves:
                        i = af(YY[g % 4][rows, :, rows], h4(pb[g % 2][rows, 0:HEADS * CHUNK]), ACT.Copy)
                    i.then_inc(m_yc, 1)
                for q in range(4):
                    for j in range(2):
                        act.wait_ge(m_uw, 8 * b + 2 * q + j + 1)
                        af((UU, WT)[j][q], h4(pb[2 * (q % 2) + j][:, :]), ACT.Copy).then_inc(m_uwc, 1)

            act.wait_ge(c_oc, 16)
            for h in range(HEADS):
                af(osq[:, h, :], OA[:, h, :], ACT.Square).then_inc(n_sq, 1)
            for h in range(HEADS):
                act.wait_ge(n_ss, 8 + h + 1)
                i = af(ors[:, h, :], pb[h][:, :], ACT.Ln, bias=eps_c, scale=1.0 / P)
            link(i)
            for h in range(HEADS):
                af(ors[:, h, :], ors[:, h, :], ACT.Exp, scale=-0.5).then_inc(n_rs, 1)

            def moe(L):
                n = 2 * L + 1
                norm_by_tiles(n)
                act.wait_ge(r_gs, L + 1)
                af(gexp, gexp, ACT.Exp)
                af(coef[:, 0, :], coef[:, 0, :], ACT.Exp).then_inc(r_lc, 1)
                B = NPAIR * L
                act.wait_ge(r_fl, L + 1)

                def xT_copy(e, j):
                    act.wait_ge(e_T, e + (B + 1))
                    af(xgT[j % 2][:, 0:4, :], pb[0][:, :].rearrange("p (k t) -> p k t", k=4), ACT.Copy).then_inc(e_xa, 1)

                def silu(e, j):
                    act.wait_ge(e_GU, e + (B + 1))
                    if not (isinstance(e, int) and e + B < 2):
                        act.wait_ge(e_ac, e + (B - 1))
                    af(sil[j % 2], pb[2 + j % 2][:, 0:FE], ACT.Silu).then_inc(e_si, 1)

                def actT_copy(e, j):
                    act.wait_ge(e_HT, e + (B + 1))
                    af(actT[j % 2], pb[4][:, 0:FE].rearrange("p (j t) -> p j t", j=2), ACT.Copy).then_inc(e_aT, 1)

                def y_copy(e, j):
                    act.wait_ge(e_D, e + (B + 1))
                    if not (isinstance(e, int) and e + B < 2):
                        act.wait_ge(e_sc[j % 2], e * 8 + (8 * B - 8 * (j % 2)))
                    af(yt[j % 2][:, 0:U], pb[5][:, :], ACT.Copy).then_inc(e_ya, 1)

                def four(i, first=False, last=False):
                    for j in range(4):
                        e = i * 4 + j
                        silu(e, j)
                        if not (first and j == 0):
                            actT_copy(e - 1, (j - 1) % 4)
                        if not (last and j == 3):
                            xT_copy(e + 1, (j + 1) % 4)
                        if not (first and j == 0):
                            y_copy(e - 1, (j - 1) % 4)

                xT_copy(0, 0)
                four(0, first=True)
                with act.Fori(1, NPAIR // 4 - 1) as i:
                    four(i)
                four(NPAIR // 4 - 1, last=True)
                actT_copy(NPAIR - 1, 3)
                y_copy(NPAIR - 1, 3)

                o = ov[L]
                more = nc.scalar.value_load(flag[0:1, 0:1], min_val=0, max_val=TOK)
                with act.If(more > CAP):
                    for s in range(2):
                        act.wait_ge(e_sc[s], 16 * (NPAIR // 2) * (L + 1))
                    for r in range(1, ROUNDS):
                        R = (r - 1) * NPAIR
                        with act.Fori(0, NPAIR) as e:
                            act.wait_ge(o["pe"], e * 4 + (4 * R + 1))
                            af(xgT[0][:, 0:4, :], pb[0][:, :].rearrange("p (k t) -> p k t", k=4), ACT.Copy)\
                                .then_inc(o["act"], 1)
                            act.wait_ge(o["pe"], e * 4 + (4 * R + 2))
                            af(sil[0], pb[2][:, 0:FE], ACT.Silu).then_inc(o["act"], 1)
                            act.wait_ge(o["pe"], e * 4 + (4 * R + 3))
                            af(actT[0], pb[4][:, 0:FE].rearrange("p (j t) -> p j t", j=2), ACT.Copy)\
                                .then_inc(o["act"], 1)
                            act.wait_ge(o["pe"], e * 4 + (4 * R + 4))
                            af(yt[0][:, 0:U], pb[5][:, :], ACT.Copy).then_inc(o["act"], 1)

            moe(0)
            norm_stats(2)
            hT_copies(2)
            for m in range(0, 14, 2):
                act.wait_ge(a_pm, m + 1)
                if m < 10:
                    af(QT[:, m, :] if m < 8 else KTT[:, m - 8, :], pb[m % 4][:, :], ACT.Copy).then_inc(a_pca, 1)
                else:
                    af(V[:, m - 10, :], pb[m % 4][:, 0:256], ACT.Copy).then_inc(a_pca, 1)

            def exps(n):
                act.wait_ge(a_nb, n + 1)
                for hh in range(2):
                    af(SC[n % 4][:, hh, :], SC[n % 4][:, hh, :], ACT.Exp, bias=nb[:, n % 8, hh:hh + 1],
                       scale=HD ** -0.5, accum_out=den[:, n % 8, hh:hh + 1])
                af(es[:, n % 8, :], es[:, n % 8, :], ACT.Exp).then_inc(a_e, 1)

            def probsT_copy(n):
                u = n // 2
                act.wait_ge(a_pt, n + 1)
                if u >= 2:
                    act.wait_ge(a_o, u - 1)
                af(PT[u % 2][:, :, 2 * (n % 2):2 * (n % 2) + 2, :],
                   pb[2 + n % 2][:, :].rearrange("p (j h q) -> p j h q", j=2, h=2), ACT.Copy).then_inc(a_pc, 1)

            def o_copy(u):
                b, qb, g = u // 8, (u // 4) % 2, u % 4
                rows = slice(64 * (g % 2), 64 * (g % 2) + 64)
                tok0 = b * SEQ + qb * P
                act.wait_ge(a_o, u + 1)
                af(OT[rows, 4 * (g // 2):4 * (g // 2) + 4, tok0:tok0 + P],
                   pb[4 + u % 2][rows, :].rearrange("p (h q) -> p h q", h=4), ACT.Copy).then_inc(a_oc, 1)

            NU = 32
            for n in range(NU + 5):
                if n < NU:
                    exps(n)
                if 3 <= n < NU + 3:
                    probsT_copy(n - 3)
                if n >= 6 and n % 2 == 0:
                    o_copy((n - 6) // 2)
            moe(1)
            norm_stats(4)

        @block.vector
        def _(dve):
            v = nc.vector
            dc = [0]

            def link(i):
                dc[0] += 1
                i.then_inc(dch, 1)
                dve.wait_ge(dch, dc[0])

            def mark(i):
                dc[0] += 1
                i.then_inc(dch, 1)
                return dc[0]

            def bc(ap, shape, axis):
                return ap.unsqueeze(axis).broadcast_to(shape)

            def norm_apply(n, tiles=range(NT)):
                dve.wait_ge(ld_gain, 16 * (n + 1))
                for t in tiles:
                    dve.wait_ge(s_rstd, RSTD_DONE[n] - (1 if n and t < 2 else 0))
                    v.scalar_tensor_tensor(HTOK[n][:, t, :], X[:, t, :], rstd[:, n, t:t + 1], GAIN[n],
                                           ALU.mult, ALU.mult).then_inc(s_h, 1)

            def reduce_angle(j):
                C = 2 * math.pi
                hi = float(np.float32(6.28125))
                lo = C - hi
                magic = 12582912.0
                z, m, x = fz[:, 1, :], fz[:, 2, :], pb[7][0:64, 0:SEQ]
                if j == 0:
                    dve.wait_ge(ld_p, 32)
                dve.wait_ge(f_ps, j + 1)
                link(v.tensor_scalar(z, x, parm[0:64, PA_B + j:PA_B + j + 1], parm[0:64, PA_FREQ + j:PA_FREQ + j + 1],
                                     ALU.add, ALU.mult))
                link(v.tensor_scalar(m, z, 1.0 / C, magic, ALU.mult, ALU.add))
                link(v.tensor_scalar(m, m, magic, None, ALU.subtract))
                link(v.scalar_tensor_tensor(z, m, -hi, z, ALU.mult, ALU.add))
                link(v.scalar_tensor_tensor(z, m, -lo, z, ALU.mult, ALU.add))
                lim = 3.1415925
                v.tensor_scalar(z, z, lim, -lim, ALU.min, ALU.max).then_inc(f_red, 1)

            def filter_taps(first):
                for n in range(first, first + 4):
                    o, i, s = n // 4, (n // 2) % 2, n % 2
                    dve.wait_ge(f_h4, n + 1)
                    k = v.tensor_tensor(RF[:, i, s, :], pb[4 + n % 4][:, :], window[:, i, :], ALU.mult)
                    if s == 1:
                        link(k)
                        v.tensor_tensor(HP[:, o, i, 0, :], RF[:, i, 0, :], RF[:, i, 1, :], ALU.add)
                        v.tensor_tensor(HP[:, o, i, 1, :], RF[:, i, 0, :], RF[:, i, 1, :], ALU.subtract).then_inc(f_ht, 1)

            norm_apply(0)
            dve.wait_ge(ld_p, 32)
            for m in range(24):
                base = hx[:, m, :] if m < 12 else qkvz[:, m - 12, :]
                w = PA_CONVB + 3 * m if m < 12 else PA_CONVA + 3 * (m - 12)
                dst = base.rearrange("p (b t) -> p b t", b=NSEQ)
                src = pb[m % 4][:, :].rearrange("p (b t) -> p b t", b=NSEQ)
                dve.wait_ge(s_cva, m + 1)
                v.scalar_tensor_tensor(dst[:, :, 1:SEQ], src[:, :, 0:SEQ - 1], parm[:, w:w + 1], dst[:, :, 1:SEQ],
                                       ALU.mult, ALU.add).then_inc(s_cvd, 1)
                dve.wait_ge(s_cvd, 2 * m + 1)
                v.scalar_tensor_tensor(dst[:, :, 0:SEQ - 1], src[:, :, 1:SEQ], parm[:, w + 2:w + 3],
                                       dst[:, :, 0:SEQ - 1], ALU.mult, ALU.add).then_inc(s_cvd, 1)
                if m < 3:
                    reduce_angle(m)
                elif m < 5:
                    filter_taps(4 * (m - 3))
            dve.wait_ge(s_ab, 1)
            v.tensor_copy(ab[:, :, :], pb[4][:, 0:64].rearrange("p (t n) -> p t n", t=NT)).then_inc(s_abc, 1)
            dve.wait_ge(s_abc, 1)
            dtb = bc(parm[:, PA_DTB:PA_DTB + 8], [P, NT, 8], 1)
            link(v.tensor_tensor(gt[:, GG, :, :], ab[:, :, 8:16], dtb, ALU.add))
            v.scalar_tensor_tensor(gt[:, KDS, :, :], gt[:, GG, :, :], -1.0, gt[:, GG, :, :],
                                   ALU.mult, ALU.min).then_inc(s_abc, 1)
            dve.wait_ge(g_gx, 1)
            link(v.tensor_scalar(gt[:, GTEMP, :, :], gt[:, GTEMP, :, :], 1.0, None, ALU.add))
            link(v.reciprocal(gt[:, BETA, :, :], gt[:, GTEMP, :, :]))
            v.tensor_scalar(gt[:, GTEMP, :, :], gt[:, BETA, :, :], -1.0, None, ALU.mult)
            link(v.scalar_tensor_tensor(gt[:, GG, :, :], gt[:, GG, :, :], 0.0, gt[:, KDS, :, :], ALU.max, ALU.add))
            link(v.tensor_tensor(gt[:, GG, :, :], gt[:, GG, :, :], bc(gt[:, KBS, 0, :], [P, NT, 8], 1), ALU.mult))
            v.tensor_scalar(gt[:, GG, :, :], gt[:, GG, :, :], -1.0, None, ALU.mult).then_inc(g_gate, 1)

            for o in range(2):
                for u in range(4):
                    b, pair = u // 2, u % 2
                    re, im = pb[4 + 2 * (u % 2)][:, :], pb[5 + 2 * (u % 2)][:, :]
                    A, Bk, C = Kf[:, o, pair, :], Kf[:, o, 2 + pair, :], Kf[:, o, 4 if pair == 0 else 1, :]
                    dve.wait_ge(y_u, 4 * o + u + 1)
                    if 4 * o + u >= 2:
                        dve.wait_ge(y_y, 2 * (4 * o + u - 1))
                    T = TP[:, u % 2, :, :]
                    v.tensor_tensor(T[:, 0, :], re, A, ALU.mult).then_inc(y_p, 1)
                    v.tensor_tensor(T[:, 1, :], im, Bk, ALU.mult).then_inc(y_p, 1)
                    v.tensor_tensor(T[:, 2, :], re, Bk, ALU.mult).then_inc(y_p, 1)
                    v.tensor_tensor(T[:, 3, :], im, C, ALU.mult).then_inc(y_p, 1)
                for c in range(4):
                    src = hx[:, 8 + c, :] if o == 0 else Z1[:, c, :]
                    n = 4 * o + c
                    dve.wait_ge(y_i, n + 1)
                    if n >= 2:
                        dve.wait_ge(y_o, n - 1)
                    w = PA_DB + 4 * o + c
                    v.scalar_tensor_tensor(ZT[:, c % 2, :], src, parm[:, w:w + 1], pb[c][:, :],
                                           ALU.mult, ALU.add).then_inc(y_z, 1)

            dve.wait_ge(g_cum, 1)
            for d in range(2):
                i = v.tensor_copy(gt[:, GC, :, 4 * d:4 * d + 4], pb[4][:, 16 * d:16 * d + 16].rearrange("p (t h) -> p t h", t=NT))
            link(i)
            v.tensor_tensor(gt[:, KDS, :, :], pb[4][:, 32:64].rearrange("p (t n) -> p t n", t=NT), gt[:, GC, :, :],
                            ALU.subtract).then_inc(g_gc, 1)
            dve.wait_ge(g_gx, 2)
            v.tensor_tensor(gt[:, KBS, :, :], gt[:, KBS, :, :], gt[:, BETA, :, :], ALU.mult).then_inc(g_gate, 1)
            for n in range(8):
                dve.wait_ge(n_rs, n + 1)
                v.scalar_tensor_tensor(qkvz[:, n, :], qkvz[:, n, :], float(P) ** -0.5 if n < 4 else 1.0, rsn[:, n, :],
                                       ALU.mult, ALU.mult).then_inc(n_n, 1)

            S4 = [P, HEADS, CHUNK]
            CC = HEADS * CHUNK
            for b in range(NSEQ):
                if b == 1:
                    dve.wait_ge(c_o, 8)
                    dve.wait_ge(c_s, 6)
                def start_inverse(q):
                    n = 4 * b + q
                    dve.wait_ge(m_m, n + 1)
                    v.tensor_tensor(XX[q], AL[q], bc(ident, [P, HEADS, P], 1), ALU.add).then_inc(m_x0, 1)
                    dve.wait_ge(m_mt, n + 1)
                    v.tensor_tensor(XT[q], h4(pb[4 + q % 2][:, 0:CC]), bc(eye_c, S4, 1), ALU.add).then_inc(m_x0, 1)

                for q in range(4):
                    n = 4 * b + q
                    t, d = 2 * b + q // 2, q % 2
                    gcol = gt[:, GC, t, 4 * d:4 * d + 4]
                    dve.wait_ge(m_gb, n + 1)
                    if n:
                        dve.wait_ge(m_q, n)
                    link(v.tensor_tensor(DT, h4(pb[6 + n % 2][:, 0:CC]), bc(gcol, S4, 2), ALU.subtract))
                    v.tensor_scalar(DA, DT, 0.0, None, ALU.max)
                    v.tensor_scalar(DT, DT, 0.0, None, ALU.min).then_inc(m_d, 1)
                    dve.wait_ge(m_e, 3 * n + 3)
                    dve.wait_ge(m_kk, 2 * b + q // 2 + 1)
                    link(v.tensor_tensor(AA[q], h4(pb[2][:, 0:CC]), DA, ALU.mult))
                    v.tensor_tensor(AA[q], AA[q], bc(gt[:, GTEMP, t, 4 * d:4 * d + 4], S4, 2), ALU.mult).then_inc(m_a, 1)
                    dve.wait_ge(m_qk, 2 * b + q // 2 + 1)
                    v.tensor_tensor(QK[q], h4(pb[3][:, 0:CC]), DT, ALU.mult).then_inc(m_q, 1)
                    if q:
                        start_inverse(q - 1)
                start_inverse(3)
                for lv in range(1, 6):
                    for q in range(4):
                        n2 = 36 * b + 8 * (lv - 1) + (2 * q if lv < 5 else q)
                        if lv < 5:
                            dve.wait_ge(m_xp, n2 + 2)
                            v.tensor_tensor(XX[q], XX[q], h4(pb[2 + n2 % 4][:, :]), ALU.add).then_inc(m_xc, 1)
                            n2 += 1
                        dve.wait_ge(m_xp, n2 + 1)
                        bank = h4(pb[2 + n2 % 4][:, 0:CC])
                        if lv < 5:
                            v.tensor_tensor(XT[q], XT[q], bank, ALU.add).then_inc(m_xc, 1)
                            if lv == 2:
                                t, cols = 2 * b + q // 2, slice(4 * (q % 2), 4 * (q % 2) + 4)
                                wide = [P, HEADS, P]
                                v.tensor_tensor(KBG[q], ktok[:, t, :, :], bc(gt[:, KBS, t, cols], wide, 2),
                                                ALU.mult).then_inc(m_s, 1)
                                v.tensor_tensor(VB[q], vtok[:, t, :, :], bc(gt[:, BETA, t, cols], wide, 2),
                                                ALU.mult).then_inc(m_s, 1)
                        else:
                            for rows in halves:
                                i = v.tensor_tensor(XX[q][rows, :, rows], XT[q][rows, :, :], bank[rows, :, :], ALU.add)
                            i.then_inc(m_xc, 1)
                for s in range(4):
                    for d in range(2):
                        g = 8 * b + 2 * s + d
                        c = s if d == 0 else 3 - s
                        q, half = 2 * (c // 2) + d, c % 2
                        rows = slice(CHUNK * half, CHUNK * half + CHUNK)
                        if g >= 2:
                            dve.wait_ge(c_o, g - 1)
                            if s > 0:
                                dve.wait_ge(c_s, 6 * b + 2 * (s - 1) + d + 1)
                        if s == 0:
                            dve.wait_ge(m_uwc, 8 * b + 2 * q + 1)
                            v.tensor_copy(VN[d][rows, :, :], UU[q][rows, :, :]).then_inc(c_v, 1)
                        else:
                            dve.wait_ge(c_w, 6 * b + 2 * (s - 1) + d + 1)
                            v.tensor_tensor(VN[d][rows, :, :], UU[q][rows, :, :], h4(pb[4 + d][rows, :]),
                                            ALU.subtract).then_inc(c_v, 1)
                    for d in range(2):
                        g = 8 * b + 2 * s + d
                        c = s if d == 0 else 3 - s
                        q, half = 2 * (c // 2) + d, c % 2
                        if s < 3:
                            dve.wait_ge(c_s, 6 * b + 2 * s + d + 1)
                            new = ST[d][(s + 1) % 2]
                            if s == 0:
                                v.tensor_copy(new, h4(pb[2 + d][:, :])).then_inc(c_sc, 1)
                            else:
                                for h in range(HEADS):
                                    i = v.scalar_tensor_tensor(new[:, h, :], ST[d][s % 2][:, h, :],
                                                               gls[:, 4 * b + q, h, half:half + 1],
                                                               pb[2 + d][:, h * P:(h + 1) * P], ALU.mult, ALU.add)
                                i.then_inc(c_sc, 1)
                    for d in range(2):
                        g = 8 * b + 2 * s + d
                        c = s if d == 0 else 3 - s
                        dve.wait_ge(c_o, g + 1)
                        dst = OA[:, :, b * SEQ + c * CHUNK:b * SEQ + (c + 1) * CHUNK]
                        src = pb[6 + d][:, 0:HEADS * CHUNK].rearrange("p (h c) -> p h c", h=HEADS)
                        if s < 2:
                            v.tensor_copy(dst, src).then_inc(c_oc, 1)
                        else:
                            v.tensor_tensor(dst, dst, src, ALU.add).then_inc(c_oc, 1)
            for h in range(HEADS):
                dve.wait_ge(n_rs, 8 + h + 1)
                link(v.scalar_tensor_tensor(OA[:, h, :], OA[:, h, :], parm[:, PA_ON:PA_ON + 1], ors[:, h, :],
                                            ALU.mult, ALU.mult))
                v.tensor_tensor(OA[:, h, :], OA[:, h, :], zT[:, h, :], ALU.mult).then_inc(o_n, 1)

            def out_proj(L):
                for n in range(8):
                    t, c = n // 2, n % 2
                    dst = X[:, t, c * U:(c + 1) * U]
                    dve.wait_ge(p_o, 8 * L + n + 1)
                    v.tensor_tensor(dst, dst, pb[2 + n % 2][:, :], ALU.add).then_inc(s_x, 1)
                    if c == 1:
                        m = 2 * L + 1
                        if t == 0:
                            dve.wait_ge(ld_gain, 16 * (m + 1))
                        dve.wait_ge(s_rstd, RSTD_DONE[m] - NT + t + 1)
                        v.scalar_tensor_tensor(HTOK[m][:, t, :], X[:, t, :], rstd[:, m, t:t + 1], GAIN[m],
                                               ALU.mult, ALU.mult).then_inc(s_h, 1)

            def moe(L):
                n = 2 * L + 1
                S32 = [P, NT, NEXP]
                link(v.memset(gpad, -3.0e38))
                dve.wait_ge(r_lg, L + 1)
                lps = pb[6][:, 0:NT * 36].rearrange("p (t n) -> p t n", t=NT)
                v.tensor_copy(lg, lps)
                link(v.tensor_copy(gpad[:, :, 0:NGRP], lps[:, :, 0:NGRP]))
                for t in range(NT):
                    i = v.max(top_g[:, t, :], gpad[:, t, :])
                link(i)
                for t in range(NT):
                    i = v.max_index(idx_g[:, t, :], top_g[:, t, :], gpad[:, t, :])
                link(i)
                v.tensor_tensor(gexp, lg[:, :, 0:NGRP], top_g[:, :, 0:1].broadcast_to([P, NT, NGRP]), ALU.subtract)
                link(v.tensor_copy(fi[:, :, 0:1], idx_g[:, :, 0:1]))
                link(v.tensor_tensor(oh[:, 3, :, :], bc(e_grp, S32, 1), fi[:, :, 0:1].broadcast_to(S32), ALU.is_equal))
                v.tensor_scalar(emsk, oh[:, 3, :, :], -1.0, -NEG, ALU.add, ALU.mult)
                link(v.tensor_tensor(oh[:, 0, :, :], oh[:, 3, :, :], lg[:, :, NGRP:NGRP + NEXP], ALU.mult))
                link(v.tensor_tensor(emsk, emsk, oh[:, 0, :, :], ALU.add))
                for t in range(NT):
                    i = v.max(top_e[:, t, :], emsk[:, t, :])
                link(i)
                for t in range(NT):
                    i = v.max_index(idx_e[:, t, :], top_e[:, t, :], emsk[:, t, :])
                link(i)
                v.tensor_tensor(coef[:, 0, :].unsqueeze(2), top_e[:, :, 1:2], top_e[:, :, 0:1], ALU.subtract).then_inc(r_gs, 1)
                link(v.tensor_copy(fi[:, :, 1:3], idx_e[:, :, 0:2]))
                for k in range(2):
                    i = v.tensor_tensor(oh[:, k, :, :], bc(iota_e, S32, 1), fi[:, :, 1 + k:2 + k].broadcast_to(S32), ALU.is_equal)
                link(i)
                v.tensor_tensor(oh[:, 2, :, :], oh[:, 0, :, :], oh[:, 1, :, :], ALU.add).then_inc(r_oh, 1)
                dve.wait_ge(r_lc, L + 1)
                link(v.tensor_reduce(coef[:, 1, :], gexp, AXX, ALU.add))
                link(v.scalar_tensor_tensor(coef[:, 2, :], coef[:, 0, :], 1.0, coef[:, 1, :], ALU.add, ALU.mult))
                link(v.reciprocal(coef[:, 3, :], coef[:, 2, :]))
                v.tensor_tensor(coef[:, 4, :], coef[:, 3, :], coef[:, 0, :], ALU.mult)
                dve.wait_ge(r_rk, L + 1)
                rps = pb[3][:, 0:NT * NEXP].rearrange("p (t n) -> p t n", t=NT)
                link(v.tensor_reduce(cmax[:, :], pb[3][:, NT * NEXP:(NT + 1) * NEXP], AXX, ALU.max))
                v.tensor_copy(flag[:, :], cmax[:, :])
                for k in range(2):
                    link(v.tensor_tensor(emsk, oh[:, k, :, :], rps, ALU.mult))
                    link(v.tensor_reduce(rowf[:, k, :], emsk, AXX, ALU.add))
                link(v.tensor_scalar(rtmp[:, 0:2, :], fi[:, :, 1:3].rearrange("p t k -> p k t"), float(CAP), None, ALU.mult))
                link(v.tensor_tensor(rtmp[:, 0:2, :], rtmp[:, 0:2, :], rowf[:, :, :], ALU.add))
                rounds = [P, 2 * NT, ROUNDS - 1]
                link(v.tensor_tensor(rt_ge, bc(rowf.rearrange("p k t -> p (k t)"), rounds, 2), bc(round_row, rounds, 1),
                                     ALU.is_ge))
                link(v.tensor_reduce(rtmp[:, 2:4, :].rearrange("p k t -> p (k t)"), rt_ge, AXX, ALU.add))
                link(v.scalar_tensor_tensor(rtmp[:, 0:2, :], rtmp[:, 2:4, :], float((NEXP - 1) * CAP), rtmp[:, 0:2, :],
                                            ALU.mult, ALU.add))
                v.tensor_copy(rowi[:, :, :], rtmp[:, 0:2, :]).then_inc(r_row, 1)
                dve.wait_ge(r_tt, L + 1)
                link(v.tensor_copy(tab_val, pb[4][:, 0:P]))
                v.tensor_copy(sca_i, tab_val)
                link(v.tensor_scalar(tab_gat, tab_val, float(TOK), -float(TOK), ALU.is_ge, ALU.mult))
                link(v.tensor_tensor(tab_gat, tab_gat, tab_val, ALU.add))
                v.tensor_copy(gat_i, tab_gat).then_inc(r_fl, 1)
                B = NPAIR * L

                def xT_copy(e, j):
                    dve.wait_ge(e_T, e + (B + 1))
                    v.tensor_copy(xgT[j % 2][:, 4:8, :], pb[1][:, :].rearrange("p (k t) -> p k t", k=4)).then_inc(e_xd, 1)

                def product(e, j):
                    dve.wait_ge(e_si, e + (B + 1))
                    v.tensor_tensor(act_h[j % 2], sil[j % 2], pb[2 + j % 2][:, FE:2 * FE], ALU.mult).then_inc(e_ac, 1)

                def y_copy(e, j):
                    dve.wait_ge(e_D, e + (B + 1))
                    if not (isinstance(e, int) and e + B < 2):
                        dve.wait_ge(e_sc[j % 2], e * 8 + (8 * B - 8 * (j % 2)))
                    v.tensor_copy(yt[j % 2][:, U:2 * U], pb[6][:, :]).then_inc(e_yd, 1)

                def four(i, first=False, last=False):
                    for j in range(4):
                        e = i * 4 + j
                        product(e, j)
                        if not (last and j == 3):
                            xT_copy(e + 1, (j + 1) % 4)
                        if not (first and j == 0):
                            y_copy(e - 1, (j - 1) % 4)

                xT_copy(0, 0)
                four(0, first=True)
                with dve.Fori(1, NPAIR // 4 - 1) as i:
                    four(i)
                four(NPAIR // 4 - 1, last=True)
                y_copy(NPAIR - 1, 3)

                o = ov[L]
                more = nc.vector.value_load(flag[0:1, 0:1], min_val=0, max_val=TOK)
                with dve.If(more > CAP):
                    for s in range(2):
                        dve.wait_ge(e_sc[s], 16 * (NPAIR // 2) * (L + 1))
                    for r in range(1, ROUNDS):
                        R = (r - 1) * NPAIR
                        with dve.Fori(0, NPAIR) as e:
                            dve.wait_ge(o["pe"], e * 4 + (4 * R + 1))
                            v.tensor_copy(xgT[0][:, 4:8, :], pb[1][:, :].rearrange("p (k t) -> p k t", k=4))\
                                .then_inc(o["dve"], 1)
                            dve.wait_ge(o["act"], e * 4 + (4 * R + 2))
                            v.tensor_tensor(act_h[0], sil[0], pb[2][:, FE:2 * FE], ALU.mult).then_inc(o["dve"], 1)
                            dve.wait_ge(o["pe"], e * 4 + (4 * R + 4))
                            v.tensor_copy(yt[0][:, U:2 * U], pb[6][:, :]).then_inc(o["dve"], 1)

                for t in range(NT):
                    for k in range(2):
                        dve.wait_ge(ld_yk[t], 32 * (L + 1) + 16)
                        if k:
                            dve.wait_ge(s_x, X_DONE[n] + 2 * t + 1)
                        v.scalar_tensor_tensor(X[:, t, :], YK[:, k * NT + t, :], coef[:, 3 + k, t:t + 1], X[:, t, :],
                                               ALU.mult, ALU.add).then_inc(s_x, 1)

            out_proj(0)
            moe(0)
            norm_apply(2)
            link(v.tensor_scalar(sink8[:, :], parm[:, PA_SINK:PA_SINK + HQ], float(HD) ** 0.5, None, ALU.mult))
            for m in range(1, 14, 2):
                dve.wait_ge(a_pm, m + 1)
                if m < 10:
                    v.tensor_copy(QT[:, m, :] if m < 8 else KTT[:, m - 8, :], pb[m % 4][:, :]).then_inc(a_pcd, 1)
                else:
                    v.tensor_copy(V[:, m - 10, :], pb[m % 4][:, 0:256]).then_inc(a_pcd, 1)
            dve.wait_ge(ld_dist, 16)
            NU = 32

            def bias_and_max(n):
                qb, g, pr = (n // 8) % 2, (n // 2) % 4, n % 2
                head = 4 * g + 2 * pr
                sc, r = SC[n % 4], n % 8
                dve.wait_ge(a_s, n + 1)
                if n >= 4:
                    dve.wait_ge(a_pt, n - 3)
                for hh in range(2):
                    v.scalar_tensor_tensor(sc[:, hh, :], negd[:, qb, :], slopes(head + hh) * HD ** 0.5,
                                           pb[n % 2][:, hh * SEQ:(hh + 1) * SEQ], ALU.mult, ALU.add).then_inc(a_sc, 1)
                dve.wait_ge(a_sc, 2 * (n + 1))
                maxima = mark(v.tensor_reduce(mx[:, r, :], sc, AXX, ALU.max))
                if n:
                    o = (n - 1) % 8
                    dve.wait_ge(a_e, n)
                    total = mark(v.tensor_tensor(den[:, o, :], den[:, o, :], es[:, o, :], ALU.add))
                dve.wait_ge(dch, maxima)
                maxima = mark(v.tensor_tensor(mx[:, r, :], mx[:, r, :], sink8[:, head:head + 2], ALU.max))
                if n:
                    dve.wait_ge(dch, total)
                    v.reciprocal(den[:, o, :], den[:, o, :]).then_inc(a_rd, 1)
                dve.wait_ge(dch, maxima)
                link(v.tensor_scalar(nb[:, r, :], mx[:, r, :], -(HD ** -0.5), None, ALU.mult))
                v.scalar_tensor_tensor(es[:, r, :], sink8[:, head:head + 2], HD ** -0.5, nb[:, r, :],
                                       ALU.mult, ALU.add).then_inc(a_nb, 1)

            def denominators(n):
                r = n % 8
                dve.wait_ge(a_e, n + 1)
                link(v.tensor_tensor(den[:, r, :], den[:, r, :], es[:, r, :], ALU.add))
                v.reciprocal(den[:, r, :], den[:, r, :]).then_inc(a_rd, 1)
            for n in range(NU):
                bias_and_max(n)
            denominators(NU - 1)
            out_proj(1)
            moe(1)
            norm_apply(4)

        @block.gpsimd
        def _(pool):
            g_ = nc.gpsimd
            S4 = [P, HEADS, P]
            C4 = [P, HEADS, CHUNK]

            def bc(ap, shape, axis):
                return ap.unsqueeze(axis).broadcast_to(shape)

            def count(value):
                return value if isinstance(value, int) else pool.to_reg(value)
            g_.memset(norow, NOROW).then_inc(pch, 1)
            last_token, last_row = pool.to_reg(TOK - 1), pool.to_reg(2 * TOK - 1)
            for o in range(2):
                for u in range(4):
                    b, pair = u // 2, u % 2
                    T = TP[:, u % 2, :, :]
                    pool.wait_ge(y_p, 16 * o + 4 * u + 2)
                    if o == 1 and u == 0:
                        pool.wait_ge(y_i, 4)
                    g_.tensor_tensor(YF[:, b, pair, :], T[:, 0, :], T[:, 1, :], ALU.subtract).then_inc(y_y, 1)
                    pool.wait_ge(y_p, 16 * o + 4 * u + 4)
                    g_.tensor_tensor(YF[:, b, pair + 2, :], T[:, 2, :], T[:, 3, :], ALU.add).then_inc(y_y, 1)
                for c in range(4):
                    pool.wait_ge(y_z, 4 * o + c + 1)
                    dst = Z1[:, c, :] if o == 0 else OB[:, c, :]
                    g_.tensor_tensor(dst, ZT[:, c % 2, :], hx[:, 4 * o + c, :], ALU.mult).then_inc(y_o, 1)
            pool.wait_ge(y_o, 8)
            g_.memset(units(58, 4), 0.0).then_inc(pch, 1)
            pool.wait_ge(pch, 2)
            pool.wait_ge(g_gate, 2)

            def masked(q, m):
                twice = [P, HEADS, 2, CHUNK]
                return g_.tensor_tensor(AL[q].rearrange("p h (u c) -> p h u c", u=2), bc(AA[q], twice, 2),
                                        bc(mask(m).rearrange("p (u c) -> p u c", u=2), twice, 1), ALU.mult)

            def decay_rows(n):
                t, d = n // 2, n % 2
                if n >= 2:
                    pool.wait_ge(m_gb, n - 1)
                g_.tensor_tensor(RG[n % 2], bc(incl_c[d], C4, 1), bc(gt[:, GG, t, 4 * d:4 * d + 4], C4, 2),
                                 ALU.mult).then_inc(m_r, 1)
            for b in range(NSEQ):
                for q in range(2):
                    decay_rows(4 * b + q)
                if b == 1:
                    pool.wait_ge(c_o, 8)
                    pool.wait_ge(c_s, 6)
                pool.wait_ge(t_kvc, 8)
                for q in range(4):
                    n = 4 * b + q
                    t, d = n // 2, n % 2
                    cols = slice(4 * d, 4 * d + 4)
                    if q < 2:
                        decay_rows(n + 2)
                    pool.wait_ge(m_a, n + 1)
                    masked(q, 6 * d).then_inc(m_m, 1)
                    pool.wait_ge(m_q, n + 1)
                    g_.tensor_tensor(QK[q], QK[q], bc(incl_c[d], C4, 1), ALU.mult).then_inc(m_qm, 1)
                for lv in range(1, 6):
                    for q in range(4):
                        n = 4 * b + q
                        t, d = n // 2, n % 2
                        cols = slice(4 * d, 4 * d + 4)
                        g = 20 * b + 4 * (lv - 1) + q
                        if lv == 1:
                            pool.wait_ge(m_x0, 2 * (n + 1))
                            pool.wait_ge(m_mt, n + 1)
                        else:
                            pool.wait_ge(m_y, g - 3)
                        masked(q, 6 * d + lv).then_inc(m_al, 1)
                        if lv == 4:
                            g_.tensor_tensor(KD[q], ktok[:, t, :, :], bc(gt[:, KDS, t, cols], S4, 2), ALU.mult).then_inc(m_kd, 1)
                        if lv == 5:
                            pool.wait_ge(m_gl, n + 1)
                            g_.tensor_tensor(QD[q], QD[q], qT[:, :, t * P:(t + 1) * P], ALU.mult).then_inc(m_qd, 1)

            def moe(L):
                B = NPAIR * L
                table = tab_dram[L][:, :].rearrange("a (b o) -> (a b) o", o=1)
                pool.wait_ge(tab_init, 32)
                pool.wait_ge(r_row, L + 1)
                for k in range(2):
                    for t in range(NT):
                        g_.indirect_dma_start(table, bass.IndirectOffsetOnAxis(rowi[:, k, t:t + 1], 0),
                                              tokid[:, k * NT + t:k * NT + t + 1], None).then_inc(r_sc, 16)
                pool.wait_ge(r_hd, 16 * NT * (L + 1))
                pool.wait_ge(r_fl, L + 1)

                def gather(e, j, idx):
                    g_.indirect_dma_start(xg[j], None, h_dram[L][:, :], bass.IndirectOffsetOnAxis(idx, 0),
                                          bounds_check=last_token, oob_is_err=False).then_inc(e_xg[j], 16)

                def scatter(e, j, idx):
                    g_.indirect_dma_start(yk_dram[L][:, :], bass.IndirectOffsetOnAxis(idx, 0), yt[j % 2], None,
                                          bounds_check=last_row, oob_is_err=False).then_inc(e_sc[j % 2], 16)

                def four(i, last=False):
                    for j in range(4):
                        e = i * 4 + j
                        col = e if isinstance(e, int) else pool.snap(e)
                        if not last:
                            col4 = e + 4 if isinstance(e, int) else pool.snap(e + 4)
                            pool.wait_ge(e_T, e + (B + 1))
                            g_.tensor_copy(gcur[:, j:j + 1], gat_i[:, bass.ds(col4, 1)]).then_inc(e_cg, 1)
                            copied = count(e + (B + 5))
                            pool.wait_ge(r_fl, L + 1)
                            pool.wait_ge(e_cg, copied)
                            gather(e + 4, j, gcur[:, j:j + 1])
                        pool.wait_ge(e_ya, e + (B + 1))
                        pool.wait_ge(e_yd, e + (B + 1))
                        g_.tensor_copy(scur[:, j:j + 1], sca_i[:, bass.ds(col, 1)]).then_inc(e_cs, 1)
                        copied = count(e + (B + 1))
                        pool.wait_ge(r_fl, L + 1)
                        pool.wait_ge(e_cs, copied)
                        scatter(e, j, scur[:, j:j + 1])

                for j in range(4):
                    g_.tensor_copy(gcur[:, j:j + 1], gat_i[:, j:j + 1]).then_inc(e_cg, 1)
                    pool.wait_ge(e_cg, B + j + 1)
                    gather(j, j, gcur[:, j:j + 1])
                with pool.Fori(0, NPAIR // 4 - 1) as i:
                    four(i)
                four(NPAIR // 4 - 1, last=True)

                o = ov[L]
                more = g_.value_load(flag[0:1, 0:1], min_val=0, max_val=TOK)
                with pool.If(more > CAP):
                    for s in range(2):
                        pool.wait_ge(e_sc[s], 16 * (NPAIR // 2) * (L + 1))
                    for r in range(1, ROUNDS):
                        R = (r - 1) * NPAIR
                        with pool.Fori(0, NPAIR) as e:
                            col = pool.snap(e + r * NPAIR)
                            g_.tensor_copy(gcur[:, 0:1], gat_i[:, bass.ds(col, 1)]).then_inc(o["ids"], 1)
                            g_.tensor_copy(scur[:, 0:1], sca_i[:, bass.ds(col, 1)]).then_inc(o["ids"], 1)
                            copied = count(e * 2 + (2 * R + 2))
                            pool.wait_ge(r_fl, L + 1)
                            pool.wait_ge(o["ids"], copied)
                            g_.indirect_dma_start(xg[0], None, h_dram[L][:, :],
                                                  bass.IndirectOffsetOnAxis(gcur[:, 0:1], 0), bounds_check=last_token,
                                                  oob_is_err=False).then_inc(o["g"], 16)
                            y_act, y_dve = count(e * 4 + (4 * R + 4)), count(e * 3 + (3 * R + 3))
                            pool.wait_ge(r_fl, L + 1)
                            pool.wait_ge(o["act"], y_act)
                            pool.wait_ge(o["dve"], y_dve)
                            g_.indirect_dma_start(yk_dram[L][:, :], bass.IndirectOffsetOnAxis(scur[:, 0:1], 0), yt[0],
                                                  None, bounds_check=last_row, oob_is_err=False).then_inc(o["sc"], 16)
                            pool.wait_ge(o["sc"], e * 16 + 16 * (R + 1))

            moe(0)
            for n in range(32):
                pool.wait_ge(a_rd, n + 1)
                g_.tensor_tensor(SC[n % 4], SC[n % 4], bc(den[:, n % 8, :], [P, 2, SEQ], 2), ALU.mult).then_inc(a_p, 1)
            moe(1)


def kernel(**inputs):
    import numpy as _np
    import concourse.bacc as _bacc
    from concourse import mybir as _mybir
    from concourse.bass_utils import run_bass_kernel_spmd as _run

    a = {k: _np.asarray(v) for k, v in inputs.items()}
    cat, tile = _np.concatenate, _np.ascontiguousarray

    def k_major(w):
        return w.reshape(w.shape[0] // P, P, w.shape[1]).transpose(1, 0, 2)

    def chunks(w):
        return tile(w.reshape(KT, P, w.shape[1] // U, U).transpose(2, 1, 0, 3))

    win = a["ev_w_in"][0]
    w_in = chunks(cat([win[:, 2064:3600], win[:, 0:2048]], 1))
    w_ab = tile(k_major(win[:, 2048:2064]))
    order = [h for t in range(8) for h in ((t, 4 + t) if t < 4 else (4 + t, 8 + t))]
    wq = a["od_w_qkv"][0]
    q_cols = cat([wq[:, h * HD:(h + 1) * HD] for h in order], 1)
    w_qkv = chunks(cat([q_cols, wq[:, HQ * HD:]], 1))
    w_out1 = tile(k_major(cat([a["od_w_out"][0][h * HD:(h + 1) * HD] for h in order], 0)))
    w_out0 = tile(k_major(a["ev_w_out"][0]))
    w_router = tile(_np.stack([k_major(cat([a["moe_w_group"][L], a["moe_w_expert"][L]], 1)) for L in range(2)]))

    def rows(w, n):
        return w.reshape(2, NEXP, n, P, w.shape[-1]).transpose(0, 1, 3, 2, 4)
    gate_up = cat([rows(a["moe_w_gate"], KT), rows(a["moe_w_up"], KT)], 4)

    def pairs(w):
        return tile(w.reshape(2, NPAIR, 2, P, -1).transpose(0, 1, 3, 2, 4)).reshape(2, NPAIR, P, -1)
    w_gu, w_dn = pairs(gate_up), pairs(rows(a["moe_w_down"], FE // P))

    def on_partitions(w):
        return w.reshape(-1, P, w.shape[-1]).transpose(1, 0, 2).reshape(P, -1)

    def row(w):
        return _np.broadcast_to(w.reshape(1, -1), (P, w.size))

    def padded(w):
        return cat([w, _np.zeros((P - w.shape[0], w.shape[1]), w.dtype)], 0)
    db = a["hy_dbias"][0].reshape(2, 4, P).transpose(2, 0, 1).reshape(P, 8)
    params = cat([
        on_partitions(a["ev_conv_a"][0]), on_partitions(a["ev_conv_b"][0]), db, a["ev_onorm"][0].reshape(P, 1),
        padded(a["hy_freq"][0].T), padded(_np.stack([a["hy_b1"][0], a["hy_b2"][0], a["hy_b3"][0]], 1)),
        row(cat([a["ev_alog_f"][0], a["ev_alog_b"][0]])), row(cat([a["ev_dtb_f"][0], a["ev_dtb_b"][0]])),
        row(a["od_sinks"][0]), padded(a["hy_w1"][0]), padded(a["hy_w2"][0]), padded(a["hy_w3"][0]),
        padded(a["hy_w4"][0])], 1)
    assert params.shape == (P, NPAR)
    g5 = cat([_np.stack([a["norm_mix"][0], a["norm_ffn"][0], a["norm_mix"][1], a["norm_ffn"][1]]), a["norm_final"].reshape(1, D)], 0)
    gains = _np.broadcast_to(g5.reshape(5, 1, D), (5, P, D))
    x = cat([a["x_prompt"].reshape(SEQ, D), a["x_sample"].reshape(SEQ, D)], 0)

    nc = _bacc.Bacc("TRN2", target_bir_lowering=False, num_devices=1)
    arrays, args = {}, []
    for name, arr in (("x_in", x), ("gains", gains), ("pconst", persistent_constants()), ("mconst", mixer_constants()),
                      ("dconst", distance_constants()), ("params", params), ("w_in", w_in), ("w_ab", w_ab),
                      ("w_out0", w_out0), ("w_qkv", w_qkv), ("w_out1", w_out1), ("w_router", w_router),
                      ("w_gu", w_gu), ("w_dn", w_dn)):
        arr = tile(arr)
        arrays[f"{name}_dram"] = arr
        args.append(nc.dram_tensor(f"{name}_dram", arr.shape, _mybir.dt.from_np(arr.dtype), kind="ExternalInput").ap())
    y = nc.dram_tensor("y_dram", (TOK, D), _mybir.dt.float32, kind="ExternalOutput").ap()
    trunk_program(nc, *args, y)
    r = _run(nc, [arrays], core_ids=[0])
    got = r.results[0]["y_dram"].reshape(NSEQ, 1, SEQ, D)
    return got[0], got[1]
```
